# Optimizing a Trainium2 kernel written in Bass

```python
import math
import jax, jax.numpy as jnp
from jax import lax
import numpy as np

D_MODEL = 1024
BATCH = 1
SEQ = 1024
DEPTH = 2

CHUNK = 64
SSD_HEADS = 16
SSD_HEAD_DIM = 64
SSD_INNER = SSD_HEADS * SSD_HEAD_DIM
SSD_GROUPS = 2
SSD_STATE = 128
SSD_CONV = 4
SSD_CHUNK = CHUNK
SSD_CONV_DIM = SSD_INNER + 2 * SSD_GROUPS * SSD_STATE
SGU_BLOCK = 128
SGU_GROUPS = 8
SGU_WIDTH = 1024
SGU_GROUP_DIM = SGU_WIDTH // SGU_GROUPS
EVEN_IN = SSD_INNER + SSD_CONV_DIM + SSD_HEADS + 2 * SGU_WIDTH
EVEN_MIX = SSD_INNER + SGU_WIDTH
DIFF_HEADS = 8
DIFF_HEAD_DIM = 64
DIFF_V_DIM = 2 * DIFF_HEAD_DIM
DIFF_QK = DIFF_HEADS * 2 * DIFF_HEAD_DIM
Q_BLOCK = 128
D_FF = 4 * D_MODEL
DEEPNORM_ALPHA = (2 * DEPTH) ** 0.25
DEEPNORM_BETA = (8 * DEPTH) ** -0.25
N_EVEN = (DEPTH + 1) // 2
N_ODD = DEPTH // 2
LN_EPS = 1e-5

kernel_name = 'hybrid_ssd_sgu_diffattn_deepnorm'

def layer_norm(x, g, b):
    xf = x.astype(jnp.float32)
    mu = jnp.mean(xf, axis=-1, keepdims=True)
    var = jnp.mean(jnp.square(xf - mu), axis=-1, keepdims=True)
    y = (xf - mu) * lax.rsqrt(var + LN_EPS) * g.astype(jnp.float32) + b.astype(jnp.float32)
    return y.astype(x.dtype)

def rms_norm(x, w):
    xf = x.astype(jnp.float32)
    y = xf * lax.rsqrt(jnp.mean(jnp.square(xf), axis=-1, keepdims=True) + LN_EPS)
    return (y * w.astype(jnp.float32)).astype(x.dtype)

def causal_dwconv(x, w, b):
    c = x.shape[-1]
    y = lax.conv_general_dilated(x, w[:, None, :].astype(x.dtype), window_strides=(1,),
                                 padding=[(SSD_CONV - 1, 0)],
                                 dimension_numbers=('NWC', 'WIO', 'NWC'),
                                 feature_group_count=c)
    return y + b.astype(x.dtype)

def ssd_chunked_scan(x, dt, a, bm, cm):
    bsz, s, h, p = x.shape
    L = SSD_CHUNK
    nc = s // L
    g = SSD_GROUPS
    hg = h // g
    n = bm.shape[-1]
    xdt = (x * dt[..., None]).reshape(bsz, nc, L, g, hg, p)
    da = (dt * a).reshape(bsz, nc, L, g, hg)
    bm = bm.reshape(bsz, nc, L, g, n)
    cm = cm.reshape(bsz, nc, L, g, n)
    a_cs = jnp.cumsum(da, axis=2)
    causal = jnp.tril(jnp.ones((L, L), dtype=bool))
    seg = a_cs[:, :, :, None] - a_cs[:, :, None, :]
    decay = jnp.exp(jnp.where(causal[None, None, :, :, None, None], seg, -jnp.inf))
    cb = jnp.einsum('bctgn,bcsgn->bctsg', cm, bm)
    y_diag = jnp.einsum('bctsgh,bcsghp->bctghp', cb[..., None] * decay, xdt)
    state_decay = jnp.exp(a_cs[:, :, -1:] - a_cs)
    chunk_states = jnp.einsum('bclgn,bclgh,bclghp->bcghpn', bm, state_decay, xdt)
    chunk_decay = jnp.exp(a_cs[:, :, -1])

    def step(state, inp):
        s_c, d_c = inp
        return d_c[..., None, None] * state + s_c, state

    h0 = jnp.zeros((bsz, g, hg, p, n), jnp.float32)
    _, prev = lax.scan(step, h0, (jnp.moveaxis(chunk_states, 1, 0), jnp.moveaxis(chunk_decay, 1, 0)))
    prev = jnp.moveaxis(prev, 0, 1)
    y_off = jnp.einsum('bctgn,bcghpn,bctgh->bctghp', cm, prev, jnp.exp(a_cs))
    return (y_diag + y_off).reshape(bsz, s, h, p)

def ssd_mixer(z, xbc, dt_raw, conv_w, conv_b, dt_bias, a_log, d_skip, norm_w):
    bsz, s, _ = z.shape
    f32 = jnp.float32
    xbc = jax.nn.silu(causal_dwconv(xbc, conv_w, conv_b))
    xs, bm, cm = jnp.split(xbc, [SSD_INNER, SSD_INNER + SSD_GROUPS * SSD_STATE], axis=-1)
    xs = xs.astype(f32).reshape(bsz, s, SSD_HEADS, SSD_HEAD_DIM)
    bm = bm.astype(f32).reshape(bsz, s, SSD_GROUPS, SSD_STATE)
    cm = cm.astype(f32).reshape(bsz, s, SSD_GROUPS, SSD_STATE)
    dt = jax.nn.softplus(dt_raw.astype(f32) + dt_bias.astype(f32))
    a = -jnp.exp(a_log.astype(f32))
    y = ssd_chunked_scan(xs, dt, a, bm, cm) + xs * d_skip.astype(f32)[:, None]
    y = y.reshape(bsz, s, SSD_INNER) * jax.nn.silu(z.astype(f32))
    yg = y.reshape(bsz, s, SSD_GROUPS, SSD_INNER // SSD_GROUPS)
    yg = yg * lax.rsqrt(jnp.mean(jnp.square(yg), axis=-1, keepdims=True) + LN_EPS)
    y = yg.reshape(bsz, s, SSD_INNER) * norm_w.astype(f32)
    return y.astype(z.dtype)

def sgu_mixer(proj, ln_g, ln_b, w_s, b_s):
    bsz, s, _ = proj.shape
    u, v = jnp.split(jax.nn.gelu(proj, approximate=False), 2, axis=-1)
    v = layer_norm(v, ln_g, ln_b)
    nb = s // SGU_BLOCK
    v = v.reshape(bsz, nb, SGU_BLOCK, SGU_GROUPS, SGU_GROUP_DIM)
    cpos = jnp.arange(SGU_BLOCK) // CHUNK
    mask = cpos[:, None] >= cpos[None, :]
    w = jnp.where(mask[None], w_s, jnp.zeros_like(w_s))
    mixed = jnp.einsum('gts,bnsgc->bntgc', w, v) + b_s.T[None, None, :, :, None]
    return u * mixed.reshape(bsz, s, SGU_WIDTH)

def alibi_slopes(n_heads):
    return jnp.exp2(-8.0 * jnp.arange(1, n_heads + 1, dtype=jnp.float32) / n_heads)

def diff_attention(x, w_qkv, lq1, lk1, lq2, lk2, subln_w, w_out, lambda_init):
    bsz, s, _ = x.shape
    f32 = jnp.float32
    qkv = x @ w_qkv
    q, k, v = jnp.split(qkv, [DIFF_QK, 2 * DIFF_QK], axis=-1)
    q = q.reshape(bsz, s, DIFF_HEADS, 2, DIFF_HEAD_DIM)
    k = k.reshape(bsz, s, DIFF_HEADS, 2, DIFF_HEAD_DIM)
    v = v.reshape(bsz, s, DIFF_HEADS, DIFF_V_DIM)
    lam = (jnp.exp(jnp.sum(lq1.astype(f32) * lk1.astype(f32)))
           - jnp.exp(jnp.sum(lq2.astype(f32) * lk2.astype(f32))) + lambda_init)
    slopes = alibi_slopes(DIFF_HEADS)
    nb = s // Q_BLOCK
    qb = jnp.moveaxis(q.reshape(bsz, nb, Q_BLOCK, DIFF_HEADS, 2, DIFF_HEAD_DIM), 1, 0)
    k_pos = jnp.arange(s)
    scale = DIFF_HEAD_DIM ** -0.5

    def block(args):
        q_i, i = args
        q_pos = i * Q_BLOCK + jnp.arange(Q_BLOCK)
        sc = jnp.einsum('bqhmd,bkhmd->bhmqk', q_i, k, preferred_element_type=f32) * scale
        dist = jnp.abs(q_pos[:, None] - k_pos[None, :]).astype(f32)
        allowed = (k_pos[None, :] // CHUNK) <= (q_pos[:, None] // CHUNK)
        bias = jnp.where(allowed[None], -slopes[:, None, None] * dist[None], -jnp.inf)
        pr = jax.nn.softmax(sc + bias[None, :, None], axis=-1)
        attn = pr[:, :, 0] - lam * pr[:, :, 1]
        return jnp.einsum('bhqk,bkhe->bqhe', attn.astype(v.dtype), v)

    o = lax.map(block, (qb, jnp.arange(nb)))
    o = jnp.moveaxis(o, 0, 1).reshape(bsz, s, DIFF_HEADS, DIFF_V_DIM)
    o = rms_norm(o, subln_w) * (1.0 - lambda_init)
    return o.reshape(bsz, s, DIFF_HEADS * DIFF_V_DIM) @ w_out

def setup_inputs(seed: int = 0) -> dict:
    key = jax.random.key(seed)
    ks = jax.random.split(key, 28)
    f32 = jnp.float32

    def nrm(k, shape, sd):
        return sd * jax.random.normal(k, shape, f32)

    x = jax.random.normal(ks[0], (BATCH, SEQ, D_MODEL), f32)
    even_w_in = nrm(ks[1], (N_EVEN, D_MODEL, EVEN_IN), D_MODEL ** -0.5)
    even_conv_w = nrm(ks[2], (N_EVEN, SSD_CONV, SSD_CONV_DIM), SSD_CONV ** -0.5)
    even_conv_b = nrm(ks[3], (N_EVEN, SSD_CONV_DIM), 0.01)
    dt0 = jnp.exp(jax.random.uniform(ks[4], (N_EVEN, SSD_HEADS), f32, math.log(1e-3), math.log(1e-1)))
    even_dt_bias = dt0 + jnp.log(-jnp.expm1(-dt0))
    even_a_log = jnp.log(jax.random.uniform(ks[5], (N_EVEN, SSD_HEADS), f32, 1.0, 16.0))
    even_d = 1.0 + nrm(ks[6], (N_EVEN, SSD_HEADS), 0.1)
    even_ssd_norm_w = 1.0 + nrm(ks[7], (N_EVEN, SSD_INNER), 0.02)
    even_sgu_ln_g = 1.0 + nrm(ks[8], (N_EVEN, SGU_WIDTH), 0.02)
    even_sgu_ln_b = nrm(ks[9], (N_EVEN, SGU_WIDTH), 0.02)
    even_sgu_w = nrm(ks[10], (N_EVEN, SGU_GROUPS, SGU_BLOCK, SGU_BLOCK), 0.5 * SGU_BLOCK ** -0.5)
    even_sgu_b = 1.0 + nrm(ks[11], (N_EVEN, SGU_GROUPS, SGU_BLOCK), 0.02)
    even_w_out = nrm(ks[12], (N_EVEN, EVEN_MIX, D_MODEL), EVEN_MIX ** -0.5 * DEEPNORM_BETA)
    w_qk = nrm(ks[13], (N_ODD, D_MODEL, 2 * DIFF_QK), D_MODEL ** -0.5)
    w_v = nrm(ks[14], (N_ODD, D_MODEL, DIFF_HEADS * DIFF_V_DIM), D_MODEL ** -0.5 * DEEPNORM_BETA)
    odd_w_qkv = jnp.concatenate([w_qk, w_v], axis=-1)
    odd_lambda_q1 = nrm(ks[15], (N_ODD, DIFF_HEAD_DIM), 0.1)
    odd_lambda_k1 = nrm(ks[16], (N_ODD, DIFF_HEAD_DIM), 0.1)
    odd_lambda_q2 = nrm(ks[17], (N_ODD, DIFF_HEAD_DIM), 0.1)
    odd_lambda_k2 = nrm(ks[18], (N_ODD, DIFF_HEAD_DIM), 0.1)
    odd_subln_w = 1.0 + nrm(ks[19], (N_ODD, DIFF_V_DIM), 0.02)
    odd_w_out = nrm(ks[20], (N_ODD, DIFF_HEADS * DIFF_V_DIM, D_MODEL),
                    (DIFF_HEADS * DIFF_V_DIM) ** -0.5 * DEEPNORM_BETA)
    ln_mix_g = 1.0 + nrm(ks[21], (DEPTH, D_MODEL), 0.02)
    ln_mix_b = nrm(ks[22], (DEPTH, D_MODEL), 0.02)
    ln_ffn_g = 1.0 + nrm(ks[23], (DEPTH, D_MODEL), 0.02)
    ln_ffn_b = nrm(ks[24], (DEPTH, D_MODEL), 0.02)
    mlp_w_up = nrm(ks[25], (DEPTH, D_MODEL, D_FF), D_MODEL ** -0.5 * DEEPNORM_BETA)
    mlp_w_down = nrm(ks[26], (DEPTH, D_FF, D_MODEL), D_FF ** -0.5 * DEEPNORM_BETA)
    return {'x': x, 'even_w_in': even_w_in, 'even_conv_w': even_conv_w, 'even_conv_b': even_conv_b,
            'even_dt_bias': even_dt_bias, 'even_a_log': even_a_log, 'even_d': even_d,
            'even_ssd_norm_w': even_ssd_norm_w, 'even_sgu_ln_g': even_sgu_ln_g,
            'even_sgu_ln_b': even_sgu_ln_b, 'even_sgu_w': even_sgu_w, 'even_sgu_b': even_sgu_b,
            'even_w_out': even_w_out, 'odd_w_qkv': odd_w_qkv, 'odd_lambda_q1': odd_lambda_q1,
            'odd_lambda_k1': odd_lambda_k1, 'odd_lambda_q2': odd_lambda_q2, 'odd_lambda_k2': odd_lambda_k2,
            'odd_subln_w': odd_subln_w, 'odd_w_out': odd_w_out, 'ln_mix_g': ln_mix_g, 'ln_mix_b': ln_mix_b,
            'ln_ffn_g': ln_ffn_g, 'ln_ffn_b': ln_ffn_b, 'mlp_w_up': mlp_w_up, 'mlp_w_down': mlp_w_down}

def reference(x, even_w_in, even_conv_w, even_conv_b, even_dt_bias, even_a_log, even_d,
              even_ssd_norm_w, even_sgu_ln_g, even_sgu_ln_b, even_sgu_w, even_sgu_b, even_w_out,
              odd_w_qkv, odd_lambda_q1, odd_lambda_k1, odd_lambda_q2, odd_lambda_k2, odd_subln_w,
              odd_w_out, ln_mix_g, ln_mix_b, ln_ffn_g, ln_ffn_b, mlp_w_up, mlp_w_down):
    h = x
    split_pts = [SSD_INNER, SSD_INNER + SSD_CONV_DIM, SSD_INNER + SSD_CONV_DIM + SSD_HEADS]
    for l in range(DEPTH):
        i = l // 2
        if l % 2 == 0:
            proj = h @ even_w_in[i]
            z, xbc, dt_raw, sgu_in = jnp.split(proj, split_pts, axis=-1)
            y_a = ssd_mixer(z, xbc, dt_raw, even_conv_w[i], even_conv_b[i], even_dt_bias[i],
                            even_a_log[i], even_d[i], even_ssd_norm_w[i])
            y_b = sgu_mixer(sgu_in, even_sgu_ln_g[i], even_sgu_ln_b[i], even_sgu_w[i], even_sgu_b[i])
            mix = jnp.concatenate([y_a, y_b], axis=-1) @ even_w_out[i]
        else:
            lambda_init = 0.8 - 0.6 * math.exp(-0.3 * l)
            mix = diff_attention(h, odd_w_qkv[i], odd_lambda_q1[i], odd_lambda_k1[i],
                                 odd_lambda_q2[i], odd_lambda_k2[i], odd_subln_w[i], odd_w_out[i],
                                 lambda_init)
        h = layer_norm(DEEPNORM_ALPHA * h + mix, ln_mix_g[l], ln_mix_b[l])
        f = jnp.square(jax.nn.relu(h @ mlp_w_up[l])) @ mlp_w_down[l]
        h = layer_norm(DEEPNORM_ALPHA * h + f, ln_ffn_g[l], ln_ffn_b[l])
    return h


_drawn_inputs = setup_inputs


def setup_inputs(seed=0):
    import zlib

    import numpy as np

    out = dict(_drawn_inputs(seed))
    spreads = {}
    factors = {'even_conv_b': 8.0,
     'even_d': 3.546,
     'even_ssd_norm_w': 50.484,
     'even_sgu_ln_g': 189.415,
     'even_sgu_ln_b': 184.017,
     'even_sgu_b': 30.243,
     'odd_lambda_q1': 3.991,
     'odd_lambda_k1': 5.457,
     'odd_lambda_q2': 4.257,
     'odd_lambda_k2': 8.0,
     'odd_subln_w': 73.863}
    for name, (base, spread) in spreads.items():
        noise = np.random.default_rng([zlib.crc32(name.encode()), seed]).standard_normal(out[name].shape)
        drawn = base * np.exp(spread * noise) if base else spread * noise
        out[name] = __import__('jax').numpy.asarray(drawn.astype(out[name].dtype))
    for name, factor in factors.items():
        out[name] = (out[name] * factor).astype(out[name].dtype)
    return out
```

```python
import math
from contextlib import ExitStack, contextmanager

import concourse.bass as bass
from concourse import mybir

F32 = mybir.dt.float32
F32R = mybir.dt.float32r
ALU = mybir.AluOpType
ACT = mybir.ActivationFunctionType

P = 128
D = 1024
SEQ = 1024
KT = D // P
TT = SEQ // P
HALF = 512
F_FF = 4 * D
HEADS = 16
HPT = 2
GROUPS = 2
TPG = KT // GROUPS
CONV = 4
CHUNK = 64
QK = D
SGU_G = 8
DIFF_H = 8
ALPHA = 4.0 ** 0.25
EPS = 1e-5
LAMBDA_INIT = 0.8 - 0.6 * math.exp(-0.3)
SCALE = 64 ** -0.5
NEG = -1e30

COL_Z, COL_X = 0, D
COL_B = 2 * D
COL_C = COL_B + GROUPS * P
COL_DT = COL_C + GROUPS * P
COL_U = COL_DT + HEADS
COL_V = COL_U + D

N_DT, N_SSD = 0, 1
SSD_TILES = 2 + 2 * TPG
N_SGU = N_SSD + GROUPS * SSD_TILES
N_MLP0 = N_SGU + SGU_G
N_ATT = N_MLP0 + F_FF // P
N_MLP1 = N_ATT + 3 * DIFF_H
N_END = N_MLP1 + F_FF // P
Q_SSD = 0
Q_V = Q_SSD + KT
Q_SGU = Q_V + KT
Q_MLP0 = Q_SGU + SGU_G
Q_ATT = Q_MLP0 + F_FF // P
Q_MLP1 = Q_ATT + DIFF_H
Q_END = Q_MLP1 + F_FF // P
D_SSD = 0
D_SGU = D_SSD + KT // 2
D_MLP0 = D_SGU + SGU_G // 2
D_ATT = D_MLP0 + F_FF // P // 2
D_MLP1 = D_ATT + DIFF_H
D_END = D_MLP1 + F_FF // P // 2

ROW_CW, ROW_CB, ROW_NW, ROW_SUB = 0, CONV * 12, CONV * 12 + 12, CONV * 12 + 20
ROWS = ROW_SUB + 1
SMALL = 11
DA, ACS, DT, DECAY, CHUNKDECAY = range(5)


class Chain:

    def __init__(self, eng, sem):
        self.eng, self.sem, self.k, self.off = eng, sem, 0, 0

    def __call__(self, ins):
        ins.then_inc(self.sem, 1)
        self.k += 1
        self.eng.wait_ge(self.sem, self.off + self.k)

    @contextmanager
    def loop(self, times, steps):
        with self.eng.Fori(0, times) as i:
            off, k = self.off, self.k
            if steps:
                self.off = self.off + i * steps
            yield i
            assert self.k - k == steps, (self.k - k, steps)
            self.off, self.k = off, k + steps * times


class Index:

    def __init__(self, at, off=0, half=0):
        self.at, self.off, self.half = at, off, half

    def __add__(self, k):
        return Index(self.at + k, self.off, self.half)

    def count(self, k, per=1):
        return self.off * per + (self.at * per + k)

    @property
    def slot(self):
        return self.at % 2

    def filled(self):
        return self.half * 16 + 16 * (self.at // 2 + 1)


def build(nc, t, out, upto=99):
    with ExitStack() as ctx:
        program(nc, ctx, t, out, upto)


def program(nc, ctx, t, out, upto):
    def sb(name, shape, dt=F32, at=None):
        return (at or ctx).enter_context(nc.sbuf_tensor(name, shape, dt))

    def sem(name):
        return ctx.enter_context(nc.semaphore(name))

    act_hi = sb("act_hi", [P, KT, SEQ], F32R)
    act_lo = sb("act_lo", [P, KT, SEQ], F32R)
    hid_hi = sb("hid_hi", [P, 2, SEQ], F32R)
    hid_lo = sb("hid_lo", [P, 2, SEQ], F32R)
    wu_raw = sb("wu_raw", [P, 2, KT, P])
    wu_hi = sb("wu_hi", [P, 2, KT, P], F32R)
    wu_lo = sb("wu_lo", [P, 2, KT, P], F32R)
    wd_raw = sb("wd_raw", [P, 2, D])
    wd_hi = sb("wd_hi", [P, 2, D], F32R)
    wd_lo = sb("wd_lo", [P, 2, D], F32R)
    ident = sb("ident", [P, P])
    upper = sb("upper", [P, P])
    negmask = sb("negmask", [P, P])
    ones = sb("ones", [P, P])
    feat = sb("feat", [P, ROWS])
    skip = sb("skip", [P, KT])
    stats = sb("stats", [P, 2, 2, 6])
    moments = sb("moments", [P, 2, 4])
    rms = sb("rms", [P, GROUPS, TT])
    lam = sb("lam", [P, 8])
    cols = sb("cols", [P, 8])
    spare = sb("spare", [P, 1])
    inv0 = sb("inv0", [P, TT])
    ostat = sb("ostat", [P, 3, TT])

    big_at = ExitStack()
    big = sb("big", [P, TT, D], F32, big_at)
    big_at.close()
    r1 = ExitStack()
    q_hi, q_lo = (sb(f"q_{x}", [P, SEQ], F32R, r1) for x in ("hi", "lo"))
    k_hi, k_lo = (sb(f"k_{x}", [P, SEQ], F32R, r1) for x in ("hi", "lo"))
    v_hi, v_lo = (sb(f"v_{x}", [P, TT, P], F32R, r1) for x in ("hi", "lo"))
    pt_hi, pt_lo = (sb(f"pt_{x}", [P, TT, P], F32R, r1) for x in ("hi", "lo"))
    r1.close()
    r1 = ExitStack()
    relu_h = sb("relu_h", [P, 2, HALF], F32, r1)
    sq_h = sb("sq_h", [P, 2, HALF], F32, r1)
    gam = sb("gam", [P, D], F32, r1)
    bet = sb("bet", [P, D], F32, r1)
    r1.close()
    keep_r1 = sb("keep_r1", [P, TT, D])

    r2 = ExitStack()
    par = sb("par", [P, TT, 5, HEADS], F32, r2)
    parj = sb("parj", [P, TT, 5, HPT], F32, r2)
    parf = sb("parf", [P, 8], F32, r2)
    r2b = ExitStack()
    cT = sb("cT", [P, SEQ], F32, r2b)
    b_tok = sb("b_tok", [P, TT, P], F32, r2b)
    cb = sb("cb", [P, SEQ], F32, r2b)
    cin = sb("cin", [P, CONV - 1 + SEQ], F32, r2b)
    xsT = sb("xsT", [P, SEQ], F32, r2b)
    x_dt = sb("x_dt", [P, TT, P], F32, r2b)
    x_dec = sb("x_dec", [P, TT, P], F32, r2b)
    c_dec = sb("c_dec", [P, SEQ], F32, r2b)
    mt = sb("mt", [P, SEQ], F32, r2b)
    state = sb("state", [P, TT, P], F32, r2b)
    r2b.close()
    rows = sb("rows", [ROWS, P], F32, r2b)
    d_rows = sb("d_rows", [KT, 2], F32, r2b)
    d_rep = sb("d_rep", [KT, P], F32, r2b)
    dtT = sb("dtT", [HEADS, SEQ], F32, r2b)
    dtb = sb("dtb", [HEADS, 1], F32, r2b)
    sp = sb("sp", [P, 8, P], F32, r2b)
    a_row = sb("a_row", [P, HEADS], F32, r2b)
    lrow = sb("lrow", [P, 4, 64], F32, r2b)
    r2b.close()
    r2.close()
    acc = sb("acc", [P, TT, D])
    r3 = ExitStack()
    vgam = sb("vgam", [P, D], F32, r3)
    vbet = sb("vbet", [P, D], F32, r3)
    r3.close()
    r3 = ExitStack()
    u_t = sb("u_t", [P, SEQ], F32, r3)
    v_g = sb("v_g", [P, TT, P], F32, r3)
    ws = sb("ws", [P, P], F32, r3)
    wsT = sb("wsT", [P, P], F32, r3)
    bs = sb("bs", [P, P], F32, r3)
    r3.close()
    r3 = ExitStack()
    tab = sb("tab", [P, SEQ], F32, r3)
    e01 = sb("e01", [P, 2, SEQ], F32, r3)
    r3.close()

    up_ps = [ctx.enter_context(nc.psum_tensor(f"up_ps{i}", [P, SEQ], F32)) for i in range(2)]
    dn_ps = [ctx.enter_context(nc.psum_tensor(f"dn_ps{i}", [P, SEQ], F32)) for i in range(2)]

    x_in = [sem(f"x_in{i}") for i in range(4)]
    small_in = sem("small_in")
    consts = sem("consts")
    acc_in = sem("acc_in")
    wu_in = [sem("wu_in0"), sem("wu_in1")]
    wu_rounded = sem("wu_rounded")
    wu_split = sem("wu_split")
    wd_in = [sem("wd_in0"), sem("wd_in1")]
    wd_rounded = sem("wd_rounded")
    wd_split = sem("wd_split")
    up_done = sem("up_done")
    up_free = sem("up_free")
    dn_done = sem("dn_done")
    dn_free = sem("dn_free")
    hid_rounded = sem("hid_rounded")
    hid_ready = sem("hid_ready")
    tr_done = sem("tr_done")
    tr_rounded = sem("tr_rounded")
    tr_split = sem("tr_split")
    acc_ready = sem("acc_ready")
    ln_in = sem("ln_in")
    ln_var = sem("ln_var")
    ln_std = sem("ln_std")
    ln_done = sem("ln_done")
    dve_step = sem("dve_step")
    act_step = sem("act_step")
    par_t = sem("par_t")
    feat_ready = sem("feat_ready")
    feat_done = sem("feat_done")
    lam_act = sem("lam_act")
    sq_rounded = sem("sq_rounded")
    hid_rounded_att = sem("hid_rounded_att")
    dt_tok = sem("dt_tok")
    sp_dve = sem("sp_dve")
    sp_act = sem("sp_act")
    dec_mm = sem("dec_mm")
    par_ready = sem("par_ready")
    cin_ready = sem("cin_ready")
    conv_done = sem("conv_done")
    silu_done = sem("silu_done")
    bt_done = sem("bt_done")
    bt_evac = sem("bt_evac")
    y_read = sem("y_read")
    sq_done = sem("sq_done")
    parj_ready = sem("parj_ready")
    conv_step = sem("conv_step")
    xt_done = sem("xt_done")
    xd_ready = sem("xd_ready")
    st_done = sem("st_done")
    scan_done = sem("scan_done")
    cum_done = sem("cum_done")
    seg_done = sem("seg_done")
    cexp_done = sem("cexp_done")
    mexp_done = sem("mexp_done")
    mc_ready = sem("mc_ready")
    y_done = sem("y_done")
    yg_ready = sem("yg_ready")
    ysq = sem("ysq")
    ysq_used = sem("ysq_used")
    rms_var = sem("rms_var")
    rms_std = sem("rms_std")
    rms_ready = sem("rms_ready")
    v_done = sem("v_done")
    v_evac = sem("v_evac")
    v_piece = sem("v_piece")
    g_in = sem("g_in")
    vg_ready = sem("vg_ready")
    ws_t = sem("ws_t")
    ws_ready = sem("ws_ready")
    mix_done = sem("mix_done")
    uy_ready = sem("uy_ready")
    tab_iota = sem("tab_iota")
    lam_dve = sem("lam_dve")
    qkv_rounded = sem("qkv_rounded")
    vt_done = sem("vt_done")
    vt_rounded = sem("vt_rounded")
    v_ready = sem("v_ready")
    s_done = sem("s_done")
    s_biased = sem("s_biased")
    negmax = sem("negmax")
    e_done = sem("e_done")
    attn_ready = sem("attn_ready")
    pt_done = sem("pt_done")
    pt_rounded = sem("pt_rounded")
    pt_ready = sem("pt_ready")
    o_done = sem("o_done")
    osq_done = sem("osq_done")
    osum_done = sem("osum_done")
    os_dve = sem("os_dve")
    os_std = sem("os_std")
    out_sent = sem("out_sent")

    w_in, w_out0 = t["even_w_in"][0], t["even_w_out"][0]
    w_qkv, w_out1 = t["odd_w_qkv"][0], t["odd_w_out"][0]
    x_tok = t["x"][0].rearrange("(t p) d -> p t d", p=P)
    out_tok = out[0].rearrange("(t p) d -> p t d", p=P)

    def halves(x):
        return x.rearrange("p (b n) -> p b n", b=2)

    def eight(ps):
        return ps[:, :].rearrange("p (k n) -> p k n", k=KT)

    def mlp_load(eng, load, l, n0):
        with eng.Fori(0, F_FF // P // 2) as i:
            for u in range(2):
                load(Index(n0 + u, i * 2, i), t["mlp_w_up"][l], (i * 2 + u) * P)

    def mlp_strips(eng, strip, l, q0):
        with eng.Fori(0, F_FF // P // 2) as i:
            for u in range(2):
                strip(Index(q0 + u, i * 2, i), t["mlp_w_down"][l], i * 2 * P + u * P)

    def ln_load(eng, number, gname, bname, l):
        eng.wait_ge(ln_done, TT * number)
        eng.dma_start(gam[:, :], t[gname][l].partition_broadcast(P)).then_inc(ln_in, 16)
        eng.dma_start(bet[:, :], t[bname][l].partition_broadcast(P)).then_inc(ln_in, 16)

    def wait_piece(eng, p):
        if p % 4 == 3:
            eng.wait_ge(v_done, TT * (p // 4 + 1))
        else:
            eng.wait_ge(v_piece, p // 4 * 3 + p % 4 + 1)

    block = ctx.enter_context(nc.Block())

    @block.sync
    def _(sp_):
        def load(n, w, col):
            if n.at >= 2:
                sp_.wait_ge(wu_split, n.count(-1))
            sp_.dma_start(wu_raw[:, n.slot], w.rearrange("(k p) n -> p k n", p=P)[:, :, bass.ds(col, P)]
                          ).then_inc(wu_in[n.slot], 16)

        for i in range(4):
            sp_.dma_start(big[:, 2 * i:2 * i + 2, :], x_tok[:, 2 * i:2 * i + 2, :]).then_inc(x_in[i], 16)
        load(Index(N_DT), w_in, COL_DT)
        for g in range(GROUPS):
            n = N_SSD + g * SSD_TILES
            load(Index(n), w_in, COL_B + g * P)
            load(Index(n + 1), w_in, COL_C + g * P)
            with sp_.Fori(0, TPG) as j:
                load(Index(n + 2, j * 2, j), w_in, (j + g * TPG) * P + COL_X)
                load(Index(n + 3, j * 2, j), w_in, j * HPT * (P // HPT) + (COL_Z + g * TPG * P))
        with sp_.Fori(0, SGU_G // 2) as i:
            for u in range(2):
                load(Index(N_SGU + u, i * 2, i), w_in, (i * 2 + u) * P + COL_U)
        mlp_load(sp_, load, 0, N_MLP0)
        with sp_.Fori(0, DIFF_H // 2) as i:
            for u in range(2):
                for c in range(3):
                    load(Index(N_ATT + 3 * u + c, i * 6, i * 3), w_qkv, (i * 2 + (u + c * QK // P)) * P)
        mlp_load(sp_, load, 1, N_MLP1)
        for s in range(TT):
            sp_.wait_ge(ln_done, TT * 4 + s + 1)
            sp_.dma_start(out_tok[:, s, :], acc[:, s, :]).then_inc(out_sent, 16)
        sp_.wait_ge(out_sent, 16 * TT)

    @block.gpsimd
    def _(pool):
        def strip(q, w, row):
            if q.at >= 2:
                pool.wait_ge(wd_split, q.count(-1))
            pool.dma_start(wd_raw[:, q.slot], w[bass.ds(row, P), :]).then_inc(wd_in[q.slot], 16)

        small = [
            (rows[ROW_CW:ROW_CB], t["even_conv_w"][0].rearrange("k (t p) -> (k t) p", p=P)),
            (rows[ROW_CB:ROW_NW], t["even_conv_b"][0].rearrange("(t p) -> t p", p=P)),
            (rows[ROW_NW:ROW_SUB], t["even_ssd_norm_w"][0].rearrange("(t p) -> t p", p=P)),
            (rows[ROW_SUB:ROWS], t["odd_subln_w"]),
            (d_rows[:, :], t["even_d"][0].rearrange("(j h) -> j h", h=HPT)),
            (dtb[:, :], t["even_dt_bias"][0].rearrange("(h o) -> h o", o=1)),
            (a_row[:, :], t["even_a_log"][0].partition_broadcast(P)),
        ] + [(lrow[:, i, :], t[name][0].partition_broadcast(P)) for i, name in
             enumerate(("odd_lambda_q1", "odd_lambda_k1", "odd_lambda_q2", "odd_lambda_k2"))]
        assert len(small) == SMALL
        for dst, src in small:
            pool.dma_start(dst, src).then_inc(small_in, 16)
        nc.gpsimd.memset(ident[:, :], 0.0).then_inc(consts, 1)
        nc.gpsimd.memset(upper[:, :], 1.0).then_inc(consts, 1)
        nc.gpsimd.memset(negmask[:, :], 0.0).then_inc(consts, 1)
        nc.gpsimd.memset(ones[:, :], 1.0).then_inc(consts, 1)
        pool.wait_ge(consts, 4)
        nc.gpsimd.affine_select(out=ident[:, :], in_=ident[:, :], compare_op=ALU.not_equal, fill=1.0, base=0,
                                pattern=[[-1, P]], channel_multiplier=1).then_inc(consts, 1)
        for m, fill in ((upper, 0.0), (negmask, NEG)):
            nc.gpsimd.affine_select(out=m[:, :], in_=m[:, :], compare_op=ALU.is_ge, fill=fill, base=0,
                                    pattern=[[1, P]], channel_multiplier=-1).then_inc(consts, 1)

        for j in range(2):
            strip(Index(Q_SSD + j), w_out0, j * P)
        pool.wait_ge(rms_ready, 1)
        pool.dma_start(acc[:, :, :], x_tok).then_inc(acc_in, 16)
        pool.dma_start(vgam[:, :], t["even_sgu_ln_g"][0].partition_broadcast(P)).then_inc(ln_in, 16)
        pool.dma_start(vbet[:, :], t["even_sgu_ln_b"][0].partition_broadcast(P)).then_inc(ln_in, 16)
        for j in range(2, KT):
            strip(Index(Q_SSD + j), w_out0, j * P)
        for b in range(2):
            for kp in range(KT // 2):
                q = Q_V + b * (KT // 2) + kp
                pool.wait_ge(wd_split, q - 1)
                pool.dma_start(halves(wd_raw[:, q % 2]),
                               w_in[2 * kp * P:2 * (kp + 1) * P, COL_V + b * HALF:COL_V + (b + 1) * HALF]
                               .rearrange("(k p) n -> p k n", p=P)).then_inc(wd_in[q % 2], 16)
        pool.wait_ge(ln_done, TT)
        with pool.Fori(0, SGU_G // 2) as i:
            for u in range(2):
                g = i * 2 + u
                pool.dma_start(ws[:, :], t["even_sgu_w"][0].rearrange("g t s -> (g t) s")[bass.ds(g * P, P), :]
                               ).then_inc(g_in, 16)
                pool.dma_start(bs[0:1, :], t["even_sgu_b"][0][bass.ds(g, 1), :]).then_inc(g_in, 16)
                nc.gpsimd.tensor_copy(v_g[:, :, :], big[:, :, bass.ds(g * P, P)]).then_inc(vg_ready, 1)
                strip(Index(Q_SGU + u, i * 2, i), w_out0, i * 2 * P + (D + u * P))
                pool.wait_ge(mix_done, g + 1)
        ln_load(pool, 1, "ln_mix_g", "ln_mix_b", 0)
        mlp_strips(pool, strip, 0, Q_MLP0)
        nc.gpsimd.iota(tab[:, :], pattern=[[-1, SEQ]], base=SEQ - P, channel_multiplier=1,
                       allow_small_or_imprecise_dtypes=True).then_inc(tab_iota, 1)
        ln_load(pool, 2, "ln_ffn_g", "ln_ffn_b", 0)
        with pool.Fori(0, DIFF_H // 2) as i:
            for u in range(2):
                strip(Index(Q_ATT + u, i * 2, i), w_out1, i * 2 * P + u * P)
        pool.wait_ge(dn_done, TT * D_MLP1)
        ln_load(pool, 3, "ln_mix_g", "ln_mix_b", 1)
        mlp_strips(pool, strip, 1, Q_MLP1)
        ln_load(pool, 4, "ln_ffn_g", "ln_ffn_b", 1)

    @block.tensor
    def _(pe):
        mm = nc.tensor.matmul

        def three(ps, hi, lo, mhi, mlo, start, stop):
            mm(ps, hi, mhi, start=start, stop=False)
            mm(ps, hi, mlo, start=False, stop=False)
            return mm(ps, lo, mhi, start=False, stop=stop)

        def up(n):
            pe.wait_ge(wu_split, n.count(1))
            for b in range(2):
                if n.at >= 2:
                    pe.wait_ge(up_free, n.count(b - 3, 2))
                for k in range(KT):
                    cut = slice(b * HALF, (b + 1) * HALF)
                    last = three(up_ps[n.slot][:, cut], wu_hi[:, n.slot, k, :], wu_lo[:, n.slot, k, :],
                                 act_hi[:, k, cut], act_lo[:, k, cut], k == 0, k == KT - 1)
                last.then_inc(up_done, 1)

        def down(d, width, q, h):
            pe.wait_ge(wd_split, q.count(width))
            for s in range(TT):
                if 8 * d.at + s >= 2:
                    pe.wait_ge(dn_free, d.count(s - 1, TT))
                for c in range(width):
                    if s == 0:
                        pe.wait_ge(hid_ready, h.count(c + 1))
                    w, row, tok = (q + c).slot, (c if width == 2 else q.slot), slice(s * P, (s + 1) * P)
                    for st, mv in ((hid_hi, wd_hi), (hid_hi, wd_lo), (hid_lo, wd_hi)):
                        for b in range(2):
                            cut = slice(b * HALF, (b + 1) * HALF)
                            last = mm(dn_ps[s % 2][:, cut], st[:, row, tok], mv[:, w, cut],
                                      start=(c == 0 and (st, mv) == (hid_hi, wd_hi)),
                                      stop=(c == width - 1 and st is hid_lo))
                last.then_inc(dn_done, 1)

        def transposes(src, number):
            for s in range(TT):
                if s >= 2:
                    pe.wait_ge(tr_split, TT * number + s - 1)
                if number == 0:
                    pe.wait_ge(x_in[s // 2], 16)
                else:
                    pe.wait_ge(ln_done, TT * number + s + 1)
                for k in range(KT):
                    last = nc.tensor.transpose(up_ps[s % 2][:, k * P:(k + 1) * P], src[:, s, k * P:(k + 1) * P],
                                               ident[:, :])
                last.then_inc(tr_done, 1)
            pe.wait_ge(tr_split, TT * (number + 1))

        pe.wait_ge(consts, 7)
        transposes(big, 0)

        pe.wait_ge(small_in, 16 * SMALL)
        nc.tensor.transpose(dn_ps[0][:, 0:ROWS], rows[:, :], ident[0:ROWS, 0:ROWS])
        pe.wait_ge(feat_ready, 1)
        nc.tensor.transpose(dn_ps[0][:, HALF:HALF + KT], d_rep[:, :], ident[0:KT, 0:KT]).then_inc(par_t, 1)
        up(Index(N_DT))
        pe.wait_ge(up_free, 2)
        for c in range(TT):
            last = nc.tensor.transpose(dn_ps[1][:, c * HEADS:(c + 1) * HEADS], dtT[:, c * P:(c + 1) * P],
                                       ident[0:HEADS, 0:HEADS])
        last.then_inc(dt_tok, 1)
        pe.wait_ge(par_ready, 1)
        pe.wait_ge(feat_done, 1)
        for i, m in enumerate((upper, ones)):
            last = mm(dn_ps[0][:, i * P:(i + 1) * P].rearrange("p (c h) -> p c h", c=TT), m[:, :], par[:, :, DA, :],
                      start=True, stop=True, skip_group_check=True)
        last.then_inc(dec_mm, 1)

        for g in range(GROUPS):
            n = N_SSD + g * SSD_TILES
            up(Index(n))
            if g:
                pe.wait_ge(y_read, 5 * g)
            up(Index(n + 1))
            pe.wait_ge(silu_done, 6 * g + 1)
            if g == 0:
                pe.wait_ge(par_ready, 2)
            for c in range(TT):
                nc.tensor.transpose(dn_ps[0][:, c * P:(c + 1) * P], xsT[:, c * P:(c + 1) * P], ident[:, :])
            pe.wait_ge(silu_done, 6 * g + 2)
            for c in range(TT):
                cut = slice(c * P, (c + 1) * P)
                last = mm(dn_ps[1][:, cut], xsT[:, cut], cT[:, cut], start=True, stop=True, skip_group_check=True)
            last.then_inc(bt_done, 1)
            with pe.Fori(0, TPG) as j:
                J = Index(g * TPG, j)
                xn = Index(n + 2, j * 2, j)

                def running_sums(head, ps):
                    for c in range(TT):
                        last = mm(ps[:, c * P:(c + 1) * P], parj[:, c, DA, head:head + 1].broadcast_to([P, P]),
                                  upper[:, :], start=True, stop=True, skip_group_check=True)
                    last.then_inc(cum_done, 1)

                up(xn)
                pe.wait_ge(parj_ready, J.count(1))
                pe.wait_ge(y_read, 5 * g + 1)
                running_sums(0, dn_ps[1])
                pe.wait_ge(y_read, J.count(g + 1))
                up(xn + 1)
                pe.wait_ge(bt_evac, g + 1)
                pe.wait_ge(silu_done, J.count(3 + 2 * g))
                for c in range(TT):
                    last = nc.tensor.transpose(dn_ps[0][:, c * P:(c + 1) * P], xsT[:, c * P:(c + 1) * P], ident[:, :])
                last.then_inc(xt_done, 1)
                pe.wait_ge(xd_ready, J.count(1))
                for c in range(TT):
                    last = mm(up_ps[1][:, c * P:(c + 1) * P], b_tok[:, c, :], x_dec[:, c, :], start=True, stop=True,
                              skip_group_check=True)
                last.then_inc(st_done, 1)
                running_sums(1, dn_ps[0])
                pe.wait_ge(scan_done, J.count(1))
                pe.wait_ge(up_free, (xn + 1).count(2, 2))
                for head in range(HPT):
                    pe.wait_ge(mc_ready, J.count(head + 1, HPT))
                    hs = slice(head * 64, (head + 1) * 64)
                    for c in range(TT):
                        cut = slice(c * P, (c + 1) * P)
                        if c:
                            mm(up_ps[0][hs, cut], state[:, c, hs], c_dec[:, cut], start=True, stop=False,
                               skip_group_check=True)
                        last = mm(up_ps[0][hs, cut], x_dt[:, c, hs], mt[:, cut], start=(c == 0), stop=True,
                                  skip_group_check=True)
                    last.then_inc(y_done, 1)
        for j in range(KT):
            pe.wait_ge(ysq, j + 1)
            for s in range(TT):
                col = (j // TPG) * TT + s
                last = mm(dn_ps[0][:, col:col + 1], (mt, c_dec)[j % 2][:, s * P:(s + 1) * P], ones[:, 0:1],
                          start=(j == 0 and s == 0), stop=(j % TPG == TPG - 1), skip_group_check=True)
            last.then_inc(ysq_used, 1)
        pe.wait_ge(rms_ready, 1)
        for m in range(KT // 2):
            down(Index(D_SSD + m), 2, Index(Q_SSD + 2 * m), Index(2 * m))

        pe.wait_ge(dn_free, TT * D_SGU)
        for b in range(2):
            for kp in range(KT // 2):
                q = Q_V + b * (KT // 2) + kp
                pe.wait_ge(wd_split, q + 1)
                for kk in range(2):
                    k = 2 * kp + kk
                    cut = slice(kk * HALF, (kk + 1) * HALF)
                    for s in range(TT):
                        if b and k == 0:
                            pe.wait_ge(v_evac, s + 1)
                        tok = slice(s * P, (s + 1) * P)
                        ps = (up_ps, dn_ps)[s // 4][s % 4 // 2][:, (s % 2) * HALF:(s % 2 + 1) * HALF]
                        last = three(ps, act_hi[:, k, tok], act_lo[:, k, tok], wd_hi[:, q % 2, cut],
                                     wd_lo[:, q % 2, cut], k == 0, k == KT - 1)
                        if k == KT - 1:
                            last.then_inc(v_done, 1)
                if k < KT - 1:
                    last.then_inc(v_piece, 1)
        pe.wait_ge(v_evac, 2 * TT)
        with pe.Fori(0, SGU_G // 2) as i:
            for u in range(2):
                g = Index(u, i * 2)
                up(Index(N_SGU + u, i * 2, i))
                pe.wait_ge(g_in, g.count(32, 32))
                if u:
                    pe.wait_ge(uy_ready, g.count(0))
                else:
                    pe.wait_ge(dn_free, Index(D_SGU, i).count(0, TT))
                nc.tensor.transpose(dn_ps[0][:, 0:P], ws[:, :], ident[:, :]).then_inc(ws_t, 1)
                for b in range(2):
                    mm(dn_ps[1][:, b * HALF:(b + 1) * HALF].rearrange("p (c t) -> p c t", t=P), ones[0:1, :],
                       bs[0:1, :].unsqueeze(1).broadcast_to([1, HALF // P, P]), start=True, stop=False,
                       skip_group_check=True)
                pe.wait_ge(ws_ready, g.count(1))
                pe.wait_ge(vg_ready, g.count(1))
                for b in range(TT):
                    last = mm(dn_ps[1][:, b * P:(b + 1) * P], v_g[:, b, :], wsT[:, :], start=False, stop=True,
                              skip_group_check=True)
                last.then_inc(mix_done, 1)
            down(Index(D_SGU, i), 2, Index(Q_SGU, i * 2, i), Index(KT, i * 2))

        def mlp(n0, q0, d0):
            with pe.Fori(0, F_FF // P // 2) as i:
                for u in range(2):
                    up(Index(n0 + u, i * 2, i))
                down(Index(d0, i), 2, Index(q0, i * 2, i), Index(q0 - KT, i * 2))

        transposes(acc, 1)
        mlp(N_MLP0, Q_MLP0, D_MLP0)
        transposes(acc, 2)

        with pe.Fori(0, DIFF_H // 2) as i:
            for u in range(2):
                H = Index(u, i * 2)
                for c in range(3):
                    up(Index(N_ATT + 3 * u + c, i * 6, i * 3))
                pe.wait_ge(up_free, Index(N_ATT + 3 * u + 2, i * 6, i * 3).count(2, 2))
                pe.wait_ge(dn_free, Index(D_ATT + u, i * 2).count(0, TT))
                for c in range(TT):
                    last = nc.tensor.transpose(dn_ps[0][:, c * P:(c + 1) * P], e01[:, 0, c * P:(c + 1) * P], ident[:, :])
                last.then_inc(vt_done, 1)

                def scores(s):
                    width = (s + 1) * P
                    for m in range(2):
                        d = slice(m * 64, (m + 1) * 64)
                        for at in range(0, width, HALF):
                            cut = slice(at, min(at + HALF, width))
                            last = three(dn_ps[m][:, cut], q_hi[d, s * P:(s + 1) * P], q_lo[d, s * P:(s + 1) * P],
                                         k_hi[d, cut], k_lo[d, cut], True, True)
                    last.then_inc(s_done, 1)

                pe.wait_ge(v_ready, H.count(1))
                for s in range(TT):
                    if s:
                        pe.wait_ge(s_biased, H.count(s, TT))
                    scores(s)
                    pe.wait_ge(attn_ready, H.count(s + 1, TT))
                    for c in range(s + 1):
                        last = nc.tensor.transpose(up_ps[0][:, c * P:(c + 1) * P], e01[:, 0, c * P:(c + 1) * P],
                                                   ident[:, :])
                    last.then_inc(pt_done, 1)
                    pe.wait_ge(pt_ready, H.count(s + 1, TT))
                    for c in range(s + 1):
                        last = three(up_ps[1][:, s * P:(s + 1) * P], v_hi[:, c, :], v_lo[:, c, :], pt_hi[:, c, :],
                                     pt_lo[:, c, :], c == 0, c == s)
                last.then_inc(o_done, 1)
                pe.wait_ge(osq_done, H.count(1))
                for s in range(TT):
                    last = mm(up_ps[0][:, s:s + 1], e01[:, 0, s * P:(s + 1) * P], ones[:, 0:1], start=True, stop=True,
                              skip_group_check=True)
                last.then_inc(osum_done, 1)
                pe.wait_ge(os_dve, H.count(1))
                down(Index(D_ATT + u, i * 2), 1, Index(Q_ATT + u, i * 2, i), Index(Q_ATT - KT + u, i * 2))
        transposes(acc, 3)
        mlp(N_MLP1, Q_MLP1, D_MLP1)

    @block.scalar
    def _(act):
        fn = nc.scalar.activation

        def round_up_weights(n):
            act.wait_ge(wu_in[n.slot], n.filled())
            if n.at >= 2:
                act.wait_ge(up_done, n.count(-2, 2))
            fn(wu_hi[:, n.slot], wu_raw[:, n.slot], ACT.Copy).then_inc(wu_rounded, 1)

        def round_strip(q):
            act.wait_ge(wd_in[q.slot], q.filled())
            fn(wd_hi[:, q.slot], wd_raw[:, q.slot], ACT.Copy).then_inc(wd_rounded, 1)

        def round_act(number, s):
            act.wait_ge(tr_done, TT * number + s + 1)
            fn(act_hi[:, :, s * P:(s + 1) * P], eight(up_ps[s % 2]), ACT.Copy).then_inc(tr_rounded, 1)

        def deviation(number, s):
            act.wait_ge(ln_var, TT * number + s + 1)
            m = moments[:, s % 2, 2:3]
            fn(m, m, ACT.Sqrt).then_inc(ln_std, 1)

        round_up_weights(Index(N_DT))
        for s in range(TT):
            round_act(0, s)
        act.wait_ge(par_t, 1)
        act.wait_ge(lam_dve, 1)
        fn(lam[:, 0:2], lam[:, 0:2], ACT.Exp).then_inc(lam_act, 1)
        fn(feat[:, :], dn_ps[0][:, 0:ROWS], ACT.Copy)
        fn(skip[:, :], dn_ps[0][:, HALF:HALF + KT], ACT.Copy).then_inc(feat_done, 1)
        round_up_weights(Index(N_DT + 1))
        for b in range(2):
            act.wait_ge(up_done, b + 1)
            fn(dtT[:, b * HALF:(b + 1) * HALF], up_ps[0][0:HEADS, b * HALF:(b + 1) * HALF], ACT.Identity,
               bias=dtb[:, 0:1]).then_inc(up_free, 1)
        act.wait_ge(dt_tok, 1)
        fn(sp[:, 0, :], dn_ps[1][:, 0:P], ACT.Abs).then_inc(act_step, 1)
        act.wait_ge(act_step, 1)
        fn(sp[:, 1, :], sp[:, 0, :], ACT.Exp, scale=-1.0).then_inc(sp_act, 1)
        fn(a_row[:, :], a_row[:, :], ACT.Exp).then_inc(sp_act, 1)
        act.wait_ge(sp_dve, 1)
        fn(sp[:, 3, :], sp[:, 2, :], ACT.Ln).then_inc(sp_act, 1)
        act.wait_ge(sp_dve, 2)
        fn(par[:, :, DECAY, :], par[:, :, DECAY, :], ACT.Exp).then_inc(sp_act, 1)
        fn(par[:, :, CHUNKDECAY, :], par[:, :, CHUNKDECAY, :], ACT.Exp).then_inc(sp_act, 1)

        def conv_in(n, conv):
            for b in range(2):
                act.wait_ge(up_done, n.count(b + 1, 2))
                if b == 0 and conv.at >= 1:
                    act.wait_ge(conv_done, conv.count(0))
                fn(cin[:, CONV - 1 + b * HALF:CONV - 1 + (b + 1) * HALF], up_ps[n.slot][:, b * HALF:(b + 1) * HALF],
                   ACT.Copy).then_inc(up_free, 1)

        def silu_conv(conv, x):
            act.wait_ge(conv_done, conv.count(1))
            fn(x, x, ACT.Silu).then_inc(silu_done, 1)

        act.wait_ge(par_ready, 2)
        for g in range(GROUPS):
            n = N_SSD + g * SSD_TILES
            round_up_weights(Index(n + 1))
            conv_in(Index(n), Index(6 * g))
            round_up_weights(Index(n + 2))
            silu_conv(Index(6 * g), xsT[:, :])
            conv_in(Index(n + 1), Index(6 * g + 1))
            silu_conv(Index(6 * g + 1), cT[:, :])
            act.wait_ge(bt_done, g + 1)
            fn(b_tok[:, :, :], eight(dn_ps[0]), ACT.Copy).then_inc(bt_evac, 1)
            with act.Fori(0, TPG) as j:
                J = Index(g * TPG, j)
                xn = Index(n + 2, j * 2, j)
                conv = Index(6 * g + 2, j)
                round_up_weights(xn + 1)
                conv_in(xn, conv)
                silu_conv(conv, xsT[:, :])
                round_up_weights(xn + 2)
                for head in range(HPT):
                    if head == 1:
                        for b in range(2):
                            act.wait_ge(up_done, (xn + 1).count(b + 1, 2))
                            fn(big[:, bass.ds(j + g * TPG, 1), b * HALF:(b + 1) * HALF],
                               up_ps[0][:, b * HALF:(b + 1) * HALF].unsqueeze(1), ACT.Silu).then_inc(up_free, 1)
                    act.wait_ge(cum_done, J.count(head + 1, HPT))
                    if head:
                        act.wait_ge(y_done, J.count(1, HPT))
                    else:
                        act.wait_ge(y_read, J.count(g + 1))
                    act.wait_ge(seg_done, J.count(head + 1, HPT))
                    fn(mt[:, :], mt[:, :], ACT.Exp).then_inc(mexp_done, 1)
                    fn(c_dec[:, :], dn_ps[1 - head][:, :], ACT.Exp).then_inc(cexp_done, 1)
        act.wait_ge(yg_ready, KT)
        for j in range(KT):
            if j >= 2:
                act.wait_ge(ysq_used, j - 1)
            fn((mt, c_dec)[j % 2][:, :], big[:, j, :], ACT.Square).then_inc(ysq, 1)
        act.wait_ge(rms_var, 1)
        fn(rms[:, :, :], rms[:, :, :], ACT.Sqrt).then_inc(rms_std, 1)
        for c in range(2):
            round_strip(Index(Q_SSD + c))
        act.wait_ge(acc_in, 16)
        for s in range(TT):
            fn(acc[:, s, :], acc[:, s, :], ACT.Copy, scale=ALPHA).then_inc(acc_ready, 1)
        for m in range(KT // 2):
            if m:
                act.wait_ge(dn_done, TT * (D_SSD + m))
            for c in range(2):
                j = 2 * m + c
                if m:
                    round_strip(Index(Q_SSD + j))
                fn(hid_hi[:, c, :], big[:, j, :], ACT.Copy, scale=feat[:, ROW_NW + j:ROW_NW + j + 1]
                   ).then_inc(hid_rounded, 1)

        def v_out(b):
            for s in range(TT):
                act.wait_ge(v_done, b * TT + s + 1)
                ps = (up_ps, dn_ps)[s // 4][s % 4 // 2][:, (s % 2) * HALF:(s % 2 + 1) * HALF]
                fn(big[:, s, b * HALF:(b + 1) * HALF], ps, ACT.Gelu).then_inc(v_evac, 1)

        for p in range(KT):
            if p < 2:
                act.wait_ge(dn_done, TT * D_SGU)
            else:
                wait_piece(act, p - 2)
            if p == KT // 2 + 1:
                v_out(0)
            round_strip(Index(Q_V + p))
        v_out(1)
        for s in range(TT):
            deviation(0, s)
        with act.Fori(0, SGU_G // 2) as i:
            for u in range(2):
                n = Index(N_SGU + u, i * 2, i)
                h = Index(KT + u, i * 2)
                round_up_weights(n + 1)
                act.wait_ge(dn_done, Index(D_SGU, i).count(0, TT))
                round_strip(Index(Q_SGU + u, i * 2, i))
                act.wait_ge(hid_ready, h.count(0))
                for b in range(2):
                    act.wait_ge(up_done, n.count(b + 1, 2))
                    fn(u_t[:, b * HALF:(b + 1) * HALF], up_ps[n.slot][:, b * HALF:(b + 1) * HALF], ACT.Gelu
                       ).then_inc(up_free, 1)
                act.wait_ge(uy_ready, Index(u, i * 2).count(1))
                fn(hid_hi[:, u, :], u_t[:, :], ACT.Copy).then_inc(hid_rounded, 1)

        def mlp(n0, q0, d0, l):
            def turn(i, last):
                for u in range(2):
                    n = Index(n0 + u, i * 2, i)
                    h = Index(q0 - KT + u, i * 2)
                    tile = Index(l * (F_FF // P) + u, i * 2)
                    if not (last and u):
                        round_up_weights(n + 1)
                    act.wait_ge(dn_done, Index(d0, i).count(0, TT))
                    round_strip(Index(q0 + u, i * 2, i))
                    act.wait_ge(hid_ready, h.count(0))
                    for b in range(2):
                        cut = slice(b * HALF, (b + 1) * HALF)
                        act.wait_ge(up_done, n.count(b + 1, 2))
                        fn(relu_h[:, b, :], up_ps[n.slot][:, cut], ACT.Relu).then_inc(up_free, 1)
                        act.wait_ge(up_free, n.count(b + 1, 2))
                        fn(hid_hi[:, u, cut], relu_h[:, b, :], ACT.Square).then_inc(sq_rounded, 1)

            turns = F_FF // P // 2
            with act.Fori(0, turns - l) as i:
                turn(i, False)
            if l:
                turn(turns - 1, True)

        def norm(number):
            deviation(number, 0)
            for s in range(TT):
                if s + 1 < TT:
                    deviation(number, s + 1)
                if number < 4:
                    round_act(number, s)
                    fn(acc[:, s, :], acc[:, s, :], ACT.Copy, scale=ALPHA).then_inc(acc_ready, 1)

        norm(1)
        mlp(N_MLP0, Q_MLP0, D_MLP0, 0)
        norm(2)

        with act.Fori(0, DIFF_H // 2) as i:
            for u in range(2):
                H = Index(u, i * 2)
                for c in range(3):
                    n = Index(N_ATT + 3 * u + c, i * 6, i * 3)
                    round_up_weights(n + 1)
                    if c == 0:
                        act.wait_ge(dn_done, Index(D_ATT + u - 1, i * 2).count(0, TT))
                        round_strip(Index(Q_ATT + u, i * 2, i))
                    if c < 2:
                        for b in range(2):
                            cut = slice(b * HALF, (b + 1) * HALF)
                            act.wait_ge(up_done, n.count(b + 1, 2))
                            fn((q_hi, k_hi)[c][:, cut], up_ps[n.slot][:, cut], ACT.Copy).then_inc(qkv_rounded, 1)
                act.wait_ge(vt_done, H.count(1))
                fn(v_hi[:, :, :], eight(dn_ps[0]), ACT.Copy).then_inc(vt_rounded, 1)
                for s in range(TT):
                    act.wait_ge(negmax, H.count(s + 1, TT))
                    for m in range(2):
                        e = e01[:, m, 0:(s + 1) * P]
                        last = fn(e, e, ACT.Exp, bias=cols[:, 2 + m:3 + m], scale=SCALE, accum_out=cols[:, 4 + m:5 + m])
                    last.then_inc(e_done, 1)
                    act.wait_ge(pt_done, H.count(s + 1, TT))
                    fn(pt_hi[:, 0:s + 1, :], eight(up_ps[0])[:, 0:s + 1, :], ACT.Copy).then_inc(pt_rounded, 1)
                act.wait_ge(o_done, H.count(1))
                fn(e01[:, 0, :], up_ps[1][:, :], ACT.Square).then_inc(osq_done, 1)
                fn(hid_hi[:, u, :], up_ps[1][:, :], ACT.Copy, scale=feat[:, ROW_SUB:ROW_SUB + 1]
                   ).then_inc(hid_rounded_att, 1)
                act.wait_ge(os_dve, H.count(1))
                fn(ostat[:, 1, :], ostat[:, 1, :], ACT.Sqrt).then_inc(os_std, 1)
        norm(3)
        mlp(N_MLP1, Q_MLP1, D_MLP1, 1)
        norm(4)

    @block.vector
    def _(dve):
        ts, tt, stt = nc.vector.tensor_scalar, nc.vector.tensor_tensor, nc.vector.scalar_tensor_tensor
        step = Chain(dve, dve_step)

        def split_up_weights(n):
            dve.wait_ge(wu_rounded, n.count(1))
            tt(wu_lo[:, n.slot], wu_raw[:, n.slot], wu_hi[:, n.slot], ALU.subtract).then_inc(wu_split, 1)

        def split_strip(q):
            dve.wait_ge(wd_rounded, q.count(1))
            tt(wd_lo[:, q.slot], wd_raw[:, q.slot], wd_hi[:, q.slot], ALU.subtract).then_inc(wd_split, 1)

        def split_act(number, s):
            dve.wait_ge(tr_rounded, TT * number + s + 1)
            cut = slice(s * P, (s + 1) * P)
            tt(act_lo[:, :, cut], eight(up_ps[s % 2]), act_hi[:, :, cut], ALU.subtract).then_inc(tr_split, 1)

        def add_down(d, scale=None):
            for s in range(TT):
                dve.wait_ge(dn_done, d.count(s + 1, TT))
                if d.at:
                    dve.wait_ge(dn_free, d.count(s - TT + 1, TT))
                if scale is None:
                    ins = tt(acc[:, s, :], dn_ps[s % 2][:, :], acc[:, s, :], ALU.add)
                else:
                    ins = stt(acc[:, s, :], dn_ps[s % 2][:, :], scale(s), acc[:, s, :], ALU.mult, ALU.add)
                ins.then_inc(dn_free, 1)

        def norm(number, src, gain, bias):
            def variance(s):
                m = moments[:, s % 2]
                for b in range(2):
                    last = nc.vector.bn_stats(stats[:, s % 2, b, :], src[:, s, b * HALF:(b + 1) * HALF])
                step(last)
                step(nc.vector.bn_aggr(m[:, 0:2], stats[:, s % 2].rearrange("p b c -> p (b c)")))
                ts(m[:, 2:3], m[:, 1:2], EPS, None, ALU.add).then_inc(ln_var, 1)

            if number:
                dve.wait_ge(dn_free, TT * (0, D_MLP0, D_ATT, D_MLP1, D_END)[number])
            else:
                dve.wait_ge(v_evac, 2 * TT)
            variance(0)
            dve.wait_ge(ln_in, 32 * (number + 1))
            for s in range(TT):
                if s + 1 < TT:
                    variance(s + 1)
                m = moments[:, s % 2]
                dve.wait_ge(ln_std, TT * number + s + 1)
                step(nc.vector.reciprocal(m[:, 3:4], m[:, 2:3]))
                step(ts(src[:, s, :], src[:, s, :], m[:, 0:1], m[:, 3:4], ALU.subtract, ALU.mult))
                step(tt(src[:, s, :], src[:, s, :], gain[:, :], ALU.mult))
                tt(src[:, s, :], src[:, s, :], bias[:, :], ALU.add).then_inc(ln_done, 1)
                if s and 0 < number < 4:
                    split_act(number, s - 1)
            if 0 < number < 4:
                split_act(number, TT - 1)

        dve.wait_ge(small_in, 16 * SMALL)
        for i in range(2):
            last = nc.vector.tensor_tensor_reduce(lrow[:, 2 * i, :], lrow[:, 2 * i, :], lrow[:, 2 * i + 1, :], 1.0, 0.0,
                                                  ALU.mult, ALU.add, lam[:, i:i + 1])
        last.then_inc(lam_dve, 1)
        nc.vector.tensor_copy(d_rep[:, :].rearrange("j (h p) -> j h p", h=HPT),
                              d_rows[:, :].unsqueeze(2).broadcast_to([KT, HPT, 64])).then_inc(feat_ready, 1)
        split_up_weights(Index(N_DT))
        for s in range(TT):
            split_act(0, s)
        dve.wait_ge(lam_act, 1)
        step(tt(lam[:, 2:3], lam[:, 0:1], lam[:, 1:2], ALU.subtract))
        step(ts(lam[:, 3:4], lam[:, 2:3], LAMBDA_INIT, -1.0, ALU.add, ALU.mult))
        split_up_weights(Index(N_DT + 1))
        e, one_e, ln_e, rest, none = (sp[:, i, :] for i in (1, 2, 3, 4, 5))
        dve.wait_ge(sp_act, 1)
        ts(one_e, e, 1.0, None, ALU.add).then_inc(sp_dve, 1)
        dve.wait_ge(sp_dve, 1)
        step(ts(rest, one_e, -1.0, None, ALU.add))
        step(ts(none, rest, 0.0, None, ALU.is_equal))
        step(tt(rest, rest, none, ALU.add))
        step(nc.vector.reciprocal(rest, rest))
        step(tt(rest, rest, e, ALU.mult))
        dve.wait_ge(sp_act, 3)
        step(tt(ln_e, ln_e, rest, ALU.mult))
        step(tt(none, none, e, ALU.mult))
        step(tt(ln_e, ln_e, none, ALU.add))

        def ch(x):
            return x.rearrange("p (c h) -> p c h", h=HEADS)

        step(stt(par[:, :, DT, :], ch(dn_ps[1][:, 0:P]), 0.0, ch(ln_e), ALU.max, ALU.add))
        stt(par[:, :, DA, :], par[:, :, DT, :], -1.0, a_row[:, :].unsqueeze(1).broadcast_to([P, TT, HEADS]),
            ALU.mult, ALU.mult).then_inc(par_ready, 1)
        dve.wait_ge(dec_mm, 1)
        step(nc.vector.tensor_copy(par[:, :, ACS, :], ch(dn_ps[0][:, 0:P])))
        tt(par[:, :, DECAY, :], ch(dn_ps[0][:, P:2 * P]), par[:, :, ACS, :], ALU.subtract)
        nc.vector.tensor_copy(par[:, :, CHUNKDECAY, :], ch(dn_ps[0][:, P:2 * P])).then_inc(sp_dve, 1)
        dve.wait_ge(sp_act, 5)
        tt(par[:, :, DECAY, :], par[:, :, DECAY, :], par[:, :, DT, :], ALU.mult).then_inc(par_ready, 1)

        def feature_params(tile):
            step(nc.vector.tensor_copy(parf[:, 0:CONV + 1], feat[:, 0:ROW_NW].rearrange("p (k f) -> p k f", f=12)
                                       [:, :, bass.ds(tile, 1)].squeeze(2)))

        def conv(n, x):
            dve.wait_ge(up_free, n.count(2, 2))
            step(ts(x, cin[:, 0:SEQ], parf[:, 0:1], parf[:, CONV:CONV + 1], ALU.mult, ALU.add))
            for k in range(1, CONV):
                ins = stt(x, cin[:, k:k + SEQ], parf[:, k:k + 1], x, ALU.mult, ALU.add)
                step(ins) if k < CONV - 1 else ins.then_inc(conv_done, 1)

        dve.wait_ge(par_ready, 2)
        step(nc.vector.memset(cin[:, 0:CONV - 1], 0.0))
        for g in range(GROUPS):
            n = N_SSD + g * SSD_TILES
            split_up_weights(Index(n + 1))
            feature_params(KT + g)
            conv(Index(n), xsT[:, :])
            split_up_weights(Index(n + 2))
            dve.wait_ge(conv_done, 6 * g + 1)
            feature_params(KT + GROUPS + g)
            conv(Index(n + 1), cT[:, :])
            dve.wait_ge(bt_done, g + 1)
            nc.vector.tensor_copy(cb[:, :], dn_ps[1][:, :]).then_inc(y_read, 1)
            with step.loop(TPG, 11) as j:
                J = Index(g * TPG, j)
                xn = Index(n + 2, j * 2, j)
                split_up_weights(xn + 1)
                nc.vector.tensor_copy(parj[:, :, :, :], par[:, :, :, bass.ds(j * HPT + g * TPG * HPT, HPT)]
                                      ).then_inc(parj_ready, 1)
                step(nc.vector.tensor_copy(parf[:, 5:6], skip[:, bass.ds(j + g * TPG, 1)]))
                feature_params(j + g * TPG)
                conv(xn, xsT[:, :])
                split_up_weights(xn + 2)
                dve.wait_ge(parj_ready, J.count(1))
                for head in range(HPT):
                    dve.wait_ge(cum_done, J.count(head + 1, HPT))
                    if head:
                        dve.wait_ge(y_done, J.count(1, HPT))
                    for c in range(TT):
                        cut = slice(c * P, (c + 1) * P)
                        last = stt(mt[:, cut], dn_ps[1 - head][:, cut], parj[:, c, ACS, head:head + 1], negmask[:, :],
                                   ALU.subtract, ALU.add)
                    last.then_inc(seg_done, 1)
                    if head == 0:
                        dve.wait_ge(xt_done, J.count(1))
                        for x, kind in ((x_dt, DT), (x_dec, DECAY)):
                            last = tt(x[:, :, :].rearrange("p c (h e) -> p c h e", h=HPT),
                                      dn_ps[0][:, :].rearrange("p (c h e) -> p c h e", c=TT, h=HPT),
                                      parj[:, :, kind, :].unsqueeze(3).broadcast_to([P, TT, HPT, 64]), ALU.mult)
                        last.then_inc(xd_ready, 1)
                        dve.wait_ge(st_done, J.count(1))
                        step(nc.vector.tensor_copy(state[:, 1, :], up_ps[1][:, 0:P]))
                        for c in range(2, TT):
                            for hh in range(HPT):
                                hs = slice(hh * 64, (hh + 1) * 64)
                                ins = stt(state[:, c, hs], state[:, c - 1, hs],
                                          parj[:, c - 1, CHUNKDECAY, hh:hh + 1],
                                          up_ps[1][:, (c - 1) * P + hh * 64:(c - 1) * P + (hh + 1) * 64],
                                          ALU.mult, ALU.add)
                            step(ins) if c < TT - 1 else ins.then_inc(scan_done, 1)
                    dve.wait_ge(mexp_done, J.count(head + 1, HPT))
                    tt(mt[:, :], mt[:, :], cb[:, :], ALU.mult)
                    dve.wait_ge(cexp_done, J.count(head + 1, HPT))
                    tt(c_dec[:, :], c_dec[:, :], cT[:, :], ALU.mult).then_inc(mc_ready, 1)
                dve.wait_ge(y_done, J.count(HPT, HPT))
                stt(xsT[:, :], xsT[:, :], parf[:, 5:6], up_ps[0][:, :], ALU.mult, ALU.add).then_inc(y_read, 1)
                dve.wait_ge(y_read, J.count(g + 2))
                dve.wait_ge(up_free, (xn + 1).count(2, 2))
                y = big[:, bass.ds(j + g * TPG, 1), :].squeeze(1)
                tt(y, y, xsT[:, :], ALU.mult).then_inc(yg_ready, 1)
        dve.wait_ge(ysq_used, KT)
        ts(rms[:, :, :].rearrange("p g s -> p (g s)"), dn_ps[0][:, 0:GROUPS * TT], 1.0 / (TPG * P), EPS,
           ALU.mult, ALU.add).then_inc(rms_var, 1)
        dve.wait_ge(rms_std, 1)
        nc.vector.reciprocal(rms[:, :, :], rms[:, :, :]).then_inc(rms_ready, 1)
        dve.wait_ge(rms_ready, 1)
        for m in range(KT // 2):
            for c in range(2):
                j = 2 * m + c
                split_strip(Index(Q_SSD + j))
                dve.wait_ge(hid_rounded, j + 1)
                stt(hid_lo[:, c, :], big[:, j, :], feat[:, ROW_NW + j:ROW_NW + j + 1], hid_hi[:, c, :],
                    ALU.mult, ALU.subtract).then_inc(hid_ready, 1)
            if m == 0:
                dve.wait_ge(acc_ready, TT)
            add_down(Index(D_SSD + m), lambda s: rms[:, m // 2, s:s + 1])

        for p in range(KT):
            split_strip(Index(Q_V + p))
        norm(0, big, vgam, vbet)
        step(nc.vector.memset(wsT[64:P, 0:64], 0.0))
        with dve.Fori(0, SGU_G // 2) as i:
            for u in range(2):
                n = Index(N_SGU + u, i * 2, i)
                g = Index(u, i * 2)
                split_up_weights(n + 1)
                split_strip(Index(Q_SGU + u, i * 2, i))
                dve.wait_ge(ws_t, g.count(1))
                nc.vector.tensor_copy(wsT[0:64, :], dn_ps[0][0:64, 0:P])
                nc.vector.tensor_copy(wsT[64:P, 64:P], dn_ps[0][64:P, 64:P]).then_inc(ws_ready, 1)
                dve.wait_ge(up_free, n.count(2, 2))
                dve.wait_ge(mix_done, g.count(1))
                tt(u_t[:, :], u_t[:, :], dn_ps[1][:, :], ALU.mult).then_inc(uy_ready, 1)
                dve.wait_ge(hid_rounded, Index(KT + u, i * 2).count(1))
                tt(hid_lo[:, u, :], u_t[:, :], hid_hi[:, u, :], ALU.subtract).then_inc(hid_ready, 1)
            add_down(Index(D_SGU, i))
        norm(1, acc, gam, bet)

        def mlp(n0, q0, d0, l):
            dve.wait_ge(acc_ready, TT * (1 + n0_round[n0]))

            def turn(i, last):
                for u in range(2):
                    n = Index(n0 + u, i * 2, i)
                    tile = Index(l * (F_FF // P) + u, i * 2)
                    if not (last and u):
                        split_up_weights(n + 1)
                    split_strip(Index(q0 + u, i * 2, i))
                    for b in range(2):
                        cut = slice(b * HALF, (b + 1) * HALF)
                        dve.wait_ge(up_free, n.count(b + 1, 2))
                        tt(sq_h[:, b, :], relu_h[:, b, :], relu_h[:, b, :], ALU.mult).then_inc(sq_done, 1)
                        dve.wait_ge(sq_done, tile.count(b + 1, 2))
                        dve.wait_ge(sq_rounded, tile.count(b + 1, 2))
                        ins = tt(hid_lo[:, u, cut], sq_h[:, b, :], hid_hi[:, u, cut], ALU.subtract)
                    ins.then_inc(hid_ready, 1)
                add_down(Index(d0, i))

            turns = F_FF // P // 2
            with dve.Fori(0, turns - l) as i:
                turn(i, False)
            if l:
                turn(turns - 1, True)

        n0_round = {N_MLP0: 1, N_MLP1: 3}
        mlp(N_MLP0, Q_MLP0, D_MLP0, 0)
        norm(2, acc, gam, bet)

        dve.wait_ge(tab_iota, 1)
        step(ts(e01[:, 0, :], tab[:, :], -0.5 / SCALE, None, ALU.mult))
        step(stt(tab[:, :], tab[:, :], 0.5 / SCALE, e01[:, 0, :], ALU.mult, ALU.min))
        step(nc.vector.memset(tab[0:64, SEQ - 64:SEQ], NEG))
        dve.wait_ge(acc_ready, 3 * TT)
        with step.loop(DIFF_H // 2, 2 * (2 * TT + 4)) as i:
            for u in range(2):
                H = Index(u, i * 2)
                split_n = Index(N_ATT + 3 * u, i * 6, i * 3)
                for c in range(3):
                    split_up_weights(split_n + (c + 1))
                    if c == 0:
                        split_strip(Index(Q_ATT + u, i * 2, i))
                    ps = up_ps[(split_n + c).slot]
                    for b in range(2):
                        cut = slice(b * HALF, (b + 1) * HALF)
                        if c < 2:
                            dve.wait_ge(qkv_rounded, H.count(2 * c + b + 1, 4))
                            tt((q_lo, k_lo)[c][:, cut], ps[:, cut], (q_hi, k_hi)[c][:, cut], ALU.subtract
                               ).then_inc(up_free, 1)
                        else:
                            dve.wait_ge(up_done, (split_n + c).count(b + 1, 2))
                            nc.vector.tensor_copy(e01[:, 0, cut], ps[:, cut]).then_inc(up_free, 1)
                dve.wait_ge(vt_rounded, H.count(1))
                tt(v_lo[:, :, :], eight(dn_ps[0]), v_hi[:, :, :], ALU.subtract).then_inc(v_ready, 1)
                for s in range(TT):
                    w = (s + 1) * P
                    if s:
                        dve.wait_ge(pt_done, H.count(s, TT))
                    dve.wait_ge(s_done, H.count(s + 1, TT))
                    nc.vector.memset(spare[:, :], 0.0)
                    for m in range(2):
                        last = nc.vector.tensor_tensor_reduce(e01[:, m, 0:w], dn_ps[m][:, 0:w], tab[:, SEQ - w:SEQ], 1.0,
                                                              -3e38, ALU.add, ALU.max, cols[:, m:m + 1])
                    last.then_inc(s_biased, 1)
                    dve.wait_ge(s_biased, H.count(s + 1, TT))
                    ts(cols[:, 2:4], cols[:, 0:2], -SCALE, None, ALU.mult).then_inc(negmax, 1)
                    dve.wait_ge(e_done, H.count(s + 1, TT))
                    nc.vector.reciprocal(inv0[:, s:s + 1], cols[:, 4:5])
                    step(nc.vector.reciprocal(cols[:, 6:7], cols[:, 5:6]))
                    step(stt(cols[:, 7:8], cols[:, 4:5], lam[:, 3:4], cols[:, 6:7], ALU.mult, ALU.mult))
                    stt(e01[:, 0, 0:w], e01[:, 1, 0:w], cols[:, 7:8], e01[:, 0, 0:w], ALU.mult, ALU.add
                        ).then_inc(attn_ready, 1)
                    dve.wait_ge(pt_rounded, H.count(s + 1, TT))
                    tt(pt_lo[:, 0:s + 1, :], eight(up_ps[0])[:, 0:s + 1, :], pt_hi[:, 0:s + 1, :], ALU.subtract
                       ).then_inc(pt_ready, 1)
                ts(tab[:, :], tab[:, :], 0.5, None, ALU.mult)
                dve.wait_ge(hid_rounded_att, H.count(1))
                stt(hid_lo[:, u, :], up_ps[1][:, :], feat[:, ROW_SUB:ROW_SUB + 1], hid_hi[:, u, :],
                    ALU.mult, ALU.subtract).then_inc(hid_ready, 1)
                dve.wait_ge(osum_done, H.count(1))
                step(tt(ostat[:, 0, :], up_ps[0][:, 0:TT], inv0[:, :], ALU.mult))
                step(tt(ostat[:, 1, :], ostat[:, 0, :], inv0[:, :], ALU.mult))
                ts(ostat[:, 1, :], ostat[:, 1, :], 1.0 / P, EPS, ALU.mult, ALU.add).then_inc(os_dve, 1)
                dve.wait_ge(os_std, H.count(1))
                step(nc.vector.reciprocal(ostat[:, 1, :], ostat[:, 1, :]))
                step(stt(ostat[:, 2, :], ostat[:, 1, :], 1.0 - LAMBDA_INIT, inv0[:, :], ALU.mult, ALU.mult))
                add_down(Index(D_ATT + u, i * 2), lambda s: ostat[:, 2, s:s + 1])
        norm(3, acc, gam, bet)
        mlp(N_MLP1, Q_MLP1, D_MLP1, 1)
        norm(4, acc, gam, bet)


_INS = ['x', 'even_w_in', 'even_conv_w', 'even_conv_b', 'even_dt_bias', 'even_a_log', 'even_d', 'even_ssd_norm_w',
        'even_sgu_ln_g', 'even_sgu_ln_b', 'even_sgu_w', 'even_sgu_b', 'even_w_out', 'odd_w_qkv', 'odd_lambda_q1',
        'odd_lambda_k1', 'odd_lambda_q2', 'odd_lambda_k2', 'odd_subln_w', 'odd_w_out', 'ln_mix_g', 'ln_mix_b',
        'ln_ffn_g', 'ln_ffn_b', 'mlp_w_up', 'mlp_w_down']


def kernel(**inputs):
    import numpy as np
    import concourse.bacc as bacc
    from concourse.bass_utils import run_bass_kernel_spmd

    nc = bacc.Bacc("TRN2", target_bir_lowering=False, num_devices=1)
    arrays, aps = {}, {}
    for name in _INS:
        a = np.ascontiguousarray(inputs[name])
        arrays[f"in_{name}"] = a
        aps[name] = nc.dram_tensor(f"in_{name}", a.shape, mybir.dt.from_np(a.dtype), kind="ExternalInput").ap()
    out = nc.dram_tensor("out", arrays["in_x"].shape, F32, kind="ExternalOutput").ap()
    build(nc, aps, out)
    result = run_bass_kernel_spmd(nc, [arrays], core_ids=[0])
    return result.results[0]["out"]
```

```python
import math
from contextlib import ExitStack, contextmanager

import concourse.bass as bass
from concourse import mybir

F32 = mybir.dt.float32
F32R = mybir.dt.float32r
ALU = mybir.AluOpType
ACT = mybir.ActivationFunctionType

P = 128
D = 1024
SEQ = 1024
KT = D // P
TT = SEQ // P
HALF = 512
F_FF = 4 * D
HEADS = 16
HPT = 2
GROUPS = 2
TPG = KT // GROUPS
CONV = 4
CHUNK = 64
QK = D
SGU_G = 8
DIFF_H = 8
ALPHA = 4.0 ** 0.25
EPS = 1e-5
LAMBDA_INIT = 0.8 - 0.6 * math.exp(-0.3)
SCALE = 64 ** -0.5
NEG = -1e30
SHARED = 46400 // 4 + TT * D

COL_Z, COL_X = 0, D
COL_B = 2 * D
COL_C = COL_B + GROUPS * P
COL_DT = COL_C + GROUPS * P
COL_U = COL_DT + HEADS
COL_V = COL_U + D

N_DT, N_SSD = 0, 1
SSD_TILES = 2 + 2 * TPG
N_SGU = N_SSD + GROUPS * SSD_TILES
N_MLP0 = N_SGU + SGU_G
N_ATT = N_MLP0 + F_FF // P
N_MLP1 = N_ATT + 3 * DIFF_H
N_END = N_MLP1 + F_FF // P
Q_SSD = 0
Q_V = Q_SSD + KT
Q_SGU = Q_V + KT
Q_MLP0 = Q_SGU + SGU_G
Q_ATT = Q_MLP0 + F_FF // P
Q_MLP1 = Q_ATT + DIFF_H
Q_END = Q_MLP1 + F_FF // P
D_SSD = 0
D_SGU = D_SSD + KT // 2
D_MLP0 = D_SGU + SGU_G // 2
D_MLP1 = D_MLP0 + F_FF // P // 2
D_END = D_MLP1 + F_FF // P // 2

H_SGU = KT
H_MLP0 = H_SGU + SGU_G
H_MLP1 = H_MLP0 + F_FF // P

ROW_CW, ROW_CB, ROW_NW, ROW_SUB = 0, CONV * 12, CONV * 12 + 12, CONV * 12 + 20
ROWS = ROW_SUB + 1
SMALL = 11
DA, ACS, DT, DECAY, CHUNKDECAY = range(5)

ORDER = [7, 0, 6, 1, 5, 2, 4, 3]
BLOCKS = TT + 1
GROUP = ((0, 1, 6, 7), (2, 3, 4, 5))
UP_AT = {0: (0, 0), 1: (0, 1), 2: (1, 0), 3: (1, 1), 5: (2, 0), 7: (2, 1)}
UNITS = [(s, b) for gr in GROUP for s in gr for b in range(2)]
UNITS_AT = {0: (0, 0), 1: (0, 3), 2: (3, 6), 3: (6, 8), 4: (8, 10), 5: (10, 12), 6: (12, 14), 7: (14, 16)}


class Chain:

    def __init__(self, eng, sem):
        self.eng, self.sem, self.k, self.off = eng, sem, 0, 0

    def __call__(self, ins):
        ins.then_inc(self.sem, 1)
        self.k += 1
        self.eng.wait_ge(self.sem, self.off + self.k)

    @contextmanager
    def loop(self, times, steps):
        with self.eng.Fori(0, times) as i:
            off, k = self.off, self.k
            if steps:
                self.off = self.off + i * steps
            yield i
            assert self.k - k == steps, (self.k - k, steps)
            self.off, self.k = off, k + steps * times


class Index:

    def __init__(self, at, off=0, half=0):
        self.at, self.off, self.half = at, off, half

    def __add__(self, k):
        return Index(self.at + k, self.off, self.half)

    def count(self, k, per=1):
        return self.off * per + (self.at * per + k)

    @property
    def slot(self):
        return self.at % 2

    def filled(self):
        return self.half * 16 + 16 * (self.at // 2 + 1)


def build(nc, t, out):
    with ExitStack() as ctx:
        program(nc, ctx, t, out)


def program(nc, ctx, t, out):
    def sb(name, shape, dt=F32, at=None):
        return (at or ctx).enter_context(nc.sbuf_tensor(name, shape, dt))

    def sem(name):
        return ctx.enter_context(nc.semaphore(name))

    act_hi = sb("act_hi", [P, KT, SEQ], F32R)
    act_lo = sb("act_lo", [P, KT, SEQ], F32R)
    hid_hi = sb("hid_hi", [P, 2, SEQ], F32R)
    hid_lo = sb("hid_lo", [P, 2, SEQ], F32R)
    wu_raw = sb("wu_raw", [P, 2, KT, P])
    wu_hi = sb("wu_hi", [P, 2, KT, P], F32R)
    wu_lo = sb("wu_lo", [P, 2, KT, P], F32R)
    wd_raw = sb("wd_raw", [P, 2, D])
    wd_hi = sb("wd_hi", [P, 2, D], F32R)
    wd_lo = sb("wd_lo", [P, 2, D], F32R)
    ident = sb("ident", [P, P])
    ones = sb("ones", [P, P])
    feat = sb("feat", [P, ROWS])
    skip = sb("skip", [P, KT])
    stats = sb("stats", [P, 2, 2, 6])
    moments = sb("moments", [P, 2, 4])
    rms = sb("rms", [P, GROUPS, TT])
    lam = sb("lam", [P, 8])
    cols = sb("cols", [P, 8])
    spare = sb("spare", [P, 1])
    inv0 = sb("inv0", [P, 2, TT])
    ostat = sb("ostat", [P, 3, TT])

    def share(*tensors, at=None):
        at = at or ctx
        return [sb(name, shape, dt, at) for name, shape, dt in tensors]

    at = ExitStack()
    big, = share(("big", [P, TT, D], F32), at=at)
    ssd_at = ExitStack()
    upper, negmask, par, parj, parf = share(
        ("upper", [P, P], F32),
        ("negmask", [P, P], F32),
        ("par", [P, TT, 5, HEADS], F32), ("parj", [P, TT, 5, HPT], F32), ("parf", [P, 8], F32), at=ssd_at)
    tmp_at = ExitStack()
    rows, d_rows, d_rep, dtT, dtb, sp, a_row, lrow = share(
        ("rows", [ROWS, P], F32), ("d_rows", [KT, 2], F32), ("d_rep", [KT, P], F32), ("dtT", [HEADS, SEQ], F32),
        ("dtb", [HEADS, 1], F32), ("sp", [P, 6, P], F32), ("a_row", [P, HEADS], F32), ("lrow", [P, 4, 64], F32),
        at=tmp_at)
    tmp_at.close()
    cT, b_tok, cb, cin, xsT, x_dt, x_dec, c_dec, mt, state = share(
        ("cT", [P, SEQ], F32), ("b_tok", [P, TT, P], F32), ("cb", [P, SEQ], F32), ("cin", [P, CONV - 1 + SEQ], F32),
        ("xsT", [P, SEQ], F32), ("x_dt", [P, TT, P], F32), ("x_dec", [P, TT, P], F32), ("c_dec", [P, SEQ], F32),
        ("mt", [P, SEQ], F32), ("state", [P, TT, P], F32), at=tmp_at)
    tmp_at.close()
    ssd_at.close()
    vgam, vbet = share(("vgam", [P, D], F32), ("vbet", [P, D], F32), at=tmp_at)
    tmp_at.close()
    u_t, v_g, ws, wsT, bs = share(("u_t", [P, SEQ], F32), ("v_g", [P, TT, P], F32), ("ws", [P, P], F32),
                                  ("wsT", [P, P], F32), ("bs", [P, P], F32), at=tmp_at)
    tmp_at.close()
    at.close()
    relu_h, sq_h, gam, bet = share(("relu_h", [P, 2, HALF], F32), ("sq_h", [P, 2, HALF], F32),
                                   ("gam", [P, D], F32), ("bet", [P, D], F32), at=at)
    at.close()
    q_hi, q_lo, k_hi, k_lo, v_hi, v_lo, pt_hi, pt_lo = share(
        *[(f"{x}_{y}", [P, SEQ], F32R) for x in "qk" for y in ("hi", "lo")],
        *[(f"{x}_{y}", [P, TT, P], F32R) for x in ("v", "pt") for y in ("hi", "lo")], at=at)
    tab, e01 = share(("tab", [P, SEQ], F32), ("e01", [P, 2, BLOCKS * P], F32), at=at)
    at.close()
    sb("shared", [P, SHARED - TT * D])
    acc = sb("acc", [P, TT, D])
    qs = ((q_hi, q_lo), (hid_hi[:, 1, :], hid_lo[:, 1, :]))
    ks = ((k_hi, k_lo), (wd_hi[:, 1, :], wd_lo[:, 1, :]))
    vT = wd_raw[:, 1, :]
    osq = wd_raw[:, 1, 0:HALF]

    up_ps = [ctx.enter_context(nc.psum_tensor(f"up_ps{i}", [P, SEQ], F32)) for i in range(2)]
    dn_ps = [ctx.enter_context(nc.psum_tensor(f"dn_ps{i}", [P, SEQ], F32)) for i in range(2)]

    x_in = [sem(f"x_in{i}") for i in range(4)]
    small_in = sem("small_in")
    consts = sem("consts")
    acc_in = sem("acc_in")
    wu_in = [sem("wu_in0"), sem("wu_in1")]
    wu_rounded = sem("wu_rounded")
    wu_split = sem("wu_split")
    wd_in = [sem("wd_in0"), sem("wd_in1")]
    wd_rounded = sem("wd_rounded")
    wd_split = sem("wd_split")
    up_done = sem("up_done")
    up_free = sem("up_free")
    dn_done = sem("dn_done")
    dn_free = sem("dn_free")
    hid_rounded = sem("hid_rounded")
    hid_ready = sem("hid_ready")
    tr_done = sem("tr_done")
    tr_rounded = sem("tr_rounded")
    tr_split = sem("tr_split")
    acc_ready = sem("acc_ready")
    ln_in = sem("ln_in")
    ln_var = sem("ln_var")
    ln_std = sem("ln_std")
    ln_done = sem("ln_done")
    dve_step = sem("dve_step")
    act_step = sem("act_step")
    par_t = sem("par_t")
    feat_ready = sem("feat_ready")
    feat_done = sem("feat_done")
    lam_act = sem("lam_act")
    sq_rounded = sem("sq_rounded")
    hid_rounded_att = sem("hid_rounded_att")
    dt_tok = sem("dt_tok")
    sp_dve = sem("sp_dve")
    sp_act = sem("sp_act")
    dec_mm = sem("dec_mm")
    par_ready = sem("par_ready")
    cin_ready = sem("cin_ready")
    conv_done = sem("conv_done")
    silu_done = sem("silu_done")
    bt_done = sem("bt_done")
    bt_evac = sem("bt_evac")
    y_read = sem("y_read")
    sq_done = sem("sq_done")
    parj_ready = sem("parj_ready")
    conv_step = sem("conv_step")
    xt_done = sem("xt_done")
    xd_ready = sem("xd_ready")
    st_done = sem("st_done")
    scan_done = sem("scan_done")
    cum_done = sem("cum_done")
    seg_done = sem("seg_done")
    cexp_done = sem("cexp_done")
    mexp_done = sem("mexp_done")
    mc_ready = sem("mc_ready")
    y_done = sem("y_done")
    yg_ready = sem("yg_ready")
    ysq = sem("ysq")
    ysq_used = sem("ysq_used")
    rms_var = sem("rms_var")
    rms_std = sem("rms_std")
    rms_ready = sem("rms_ready")
    v_done = sem("v_done")
    v_evac = sem("v_evac")
    v_piece = sem("v_piece")
    g_in = sem("g_in")
    vg_ready = sem("vg_ready")
    ws_t = sem("ws_t")
    ws_ready = sem("ws_ready")
    mix_done = sem("mix_done")
    uy_ready = sem("uy_ready")
    tab_iota = sem("tab_iota")
    lam_dve = sem("lam_dve")
    qkv_rounded = sem("qkv_rounded")
    vt_done = sem("vt_done")
    vt_rounded = sem("vt_rounded")
    v_ready = sem("v_ready")
    s_done = sem("s_done")
    ptb_done = sem("ptb_done")
    ptb_rounded = sem("ptb_rounded")
    ptb_ready = sem("ptb_ready")
    o_read = sem("o_read")
    du_done = sem("du_done")
    du_free = sem("du_free")
    s_biased = sem("s_biased")
    negmax = sem("negmax")
    e_done = sem("e_done")
    attn_ready = sem("attn_ready")
    pt_done = sem("pt_done")
    pt_rounded = sem("pt_rounded")
    pt_ready = sem("pt_ready")
    o_done = sem("o_done")
    osq_done = sem("osq_done")
    osum_done = sem("osum_done")
    os_dve = sem("os_dve")
    os_ready = sem("os_ready")
    os_std = sem("os_std")
    out_sent = sem("out_sent")

    w_in, w_out0 = t["even_w_in"][0], t["even_w_out"][0]
    w_qkv, w_out1 = t["odd_w_qkv"][0], t["odd_w_out"][0]
    x_tok = t["x"][0].rearrange("(t p) d -> p t d", p=P)
    out_tok = out[0].rearrange("(t p) d -> p t d", p=P)

    def halves(x):
        return x.rearrange("p (b n) -> p b n", b=2)

    def eight(ps):
        return ps[:, :].rearrange("p (k n) -> p k n", k=KT)

    def mlp_load(eng, load, l, n0):
        with eng.Fori(0, F_FF // P // 2) as i:
            for u in range(2):
                load(Index(n0 + u, i * 2, i), t["mlp_w_up"][l], (i * 2 + u) * P)

    def mlp_strips(eng, strip, l, q0):
        with eng.Fori(0, F_FF // P // 2) as i:
            for u in range(2):
                strip(Index(q0 + u, i * 2, i), t["mlp_w_down"][l], i * 2 * P + u * P)

    def ln_load(eng, number, gname, bname, l):
        eng.wait_ge(ln_done, TT * number)
        eng.dma_start(gam[:, :], t[gname][l].partition_broadcast(P)).then_inc(ln_in, 16)
        eng.dma_start(bet[:, :], t[bname][l].partition_broadcast(P)).then_inc(ln_in, 16)

    def wait_piece(eng, p):
        if p % 4 == 3:
            eng.wait_ge(v_done, TT * (p // 4 + 1))
        else:
            eng.wait_ge(v_piece, p // 4 * 3 + p % 4 + 1)

    def ebuf(s):
        w = (s + 1) * P
        return slice(0, w) if s >= 4 else slice(BLOCKS * P - w, BLOCKS * P)

    def four(ps):
        return ps.rearrange("p (k n) -> p k n", k=4)

    def hid_group(hid, gr):
        pairs = hid[:, 0, :].rearrange("p (a n) -> p a n", n=2 * P)
        return pairs[:, 0:4:3, :] if gr == 0 else pairs[:, 1:3, :]

    def group_ps(ps, gr):
        return ps.rearrange("p (a n) -> p a n", n=2 * P)

    block = ctx.enter_context(nc.Block())

    @block.sync
    def _(sp_):
        def load(n, w, col):
            if n.at >= 2:
                sp_.wait_ge(wu_split, n.count(-1))
            sp_.dma_start(wu_raw[:, n.slot], w.rearrange("(k p) n -> p k n", p=P)[:, :, bass.ds(col, P)]
                          ).then_inc(wu_in[n.slot], 16)

        for i in range(4):
            sp_.dma_start(big[:, 2 * i:2 * i + 2, :], x_tok[:, 2 * i:2 * i + 2, :]).then_inc(x_in[i], 16)
        load(Index(N_DT), w_in, COL_DT)
        for g in range(GROUPS):
            n = N_SSD + g * SSD_TILES
            load(Index(n), w_in, COL_B + g * P)
            load(Index(n + 1), w_in, COL_C + g * P)
            with sp_.Fori(0, TPG) as j:
                load(Index(n + 2, j * 2, j), w_in, (j + g * TPG) * P + COL_X)
                load(Index(n + 3, j * 2, j), w_in, j * HPT * (P // HPT) + (COL_Z + g * TPG * P))
        with sp_.Fori(0, SGU_G // 2) as i:
            for u in range(2):
                load(Index(N_SGU + u, i * 2, i), w_in, (i * 2 + u) * P + COL_U)
        mlp_load(sp_, load, 0, N_MLP0)
        with sp_.Fori(0, DIFF_H // 2) as i:
            for u in range(2):
                for c in range(3):
                    load(Index(N_ATT + 3 * u + c, i * 6, i * 3), w_qkv, (i * 2 + (u + c * QK // P)) * P)
        mlp_load(sp_, load, 1, N_MLP1)
        for s in range(TT):
            sp_.wait_ge(ln_done, TT * 4 + s + 1)
            sp_.dma_start(out_tok[:, s, :], acc[:, s, :]).then_inc(out_sent, 16)
        sp_.wait_ge(out_sent, 16 * TT)

    @block.gpsimd
    def _(pool):
        def strip(q, w, row):
            if q.at >= 2:
                pool.wait_ge(wd_split, q.count(-1))
            pool.dma_start(wd_raw[:, q.slot], w[bass.ds(row, P), :]).then_inc(wd_in[q.slot], 16)

        small = [
            (rows[ROW_CW:ROW_CB], t["even_conv_w"][0].rearrange("k (t p) -> (k t) p", p=P)),
            (rows[ROW_CB:ROW_NW], t["even_conv_b"][0].rearrange("(t p) -> t p", p=P)),
            (rows[ROW_NW:ROW_SUB], t["even_ssd_norm_w"][0].rearrange("(t p) -> t p", p=P)),
            (rows[ROW_SUB:ROWS], t["odd_subln_w"]),
            (d_rows[:, :], t["even_d"][0].rearrange("(j h) -> j h", h=HPT)),
            (dtb[:, :], t["even_dt_bias"][0].rearrange("(h o) -> h o", o=1)),
            (a_row[:, :], t["even_a_log"][0].partition_broadcast(P)),
        ] + [(lrow[:, i, :], t[name][0].partition_broadcast(P)) for i, name in
             enumerate(("odd_lambda_q1", "odd_lambda_k1", "odd_lambda_q2", "odd_lambda_k2"))]
        assert len(small) == SMALL
        for dst, src in small:
            pool.dma_start(dst, src).then_inc(small_in, 16)
        nc.gpsimd.memset(ident[:, :], 0.0).then_inc(consts, 1)
        nc.gpsimd.memset(upper[:, :], 1.0).then_inc(consts, 1)
        nc.gpsimd.memset(negmask[:, :], 0.0).then_inc(consts, 1)
        nc.gpsimd.memset(ones[:, :], 1.0).then_inc(consts, 1)
        pool.wait_ge(consts, 4)
        nc.gpsimd.affine_select(out=ident[:, :], in_=ident[:, :], compare_op=ALU.not_equal, fill=1.0, base=0,
                                pattern=[[-1, P]], channel_multiplier=1).then_inc(consts, 1)
        for m, fill in ((upper, 0.0), (negmask, NEG)):
            nc.gpsimd.affine_select(out=m[:, :], in_=m[:, :], compare_op=ALU.is_ge, fill=fill, base=0,
                                    pattern=[[1, P]], channel_multiplier=-1).then_inc(consts, 1)

        for j in range(2):
            strip(Index(Q_SSD + j), w_out0, j * P)
        pool.wait_ge(rms_ready, 1)
        pool.dma_start(acc[:, :, :], x_tok).then_inc(acc_in, 16)
        pool.dma_start(vgam[:, :], t["even_sgu_ln_g"][0].partition_broadcast(P)).then_inc(ln_in, 16)
        pool.dma_start(vbet[:, :], t["even_sgu_ln_b"][0].partition_broadcast(P)).then_inc(ln_in, 16)
        for j in range(2, KT):
            strip(Index(Q_SSD + j), w_out0, j * P)
        for b in range(2):
            for kp in range(KT // 2):
                q = Q_V + b * (KT // 2) + kp
                pool.wait_ge(wd_split, q - 1)
                pool.dma_start(halves(wd_raw[:, q % 2]),
                               w_in[2 * kp * P:2 * (kp + 1) * P, COL_V + b * HALF:COL_V + (b + 1) * HALF]
                               .rearrange("(k p) n -> p k n", p=P)).then_inc(wd_in[q % 2], 16)
        pool.wait_ge(ln_done, TT)
        with pool.Fori(0, SGU_G // 2) as i:
            for u in range(2):
                g = i * 2 + u
                pool.dma_start(ws[:, :], t["even_sgu_w"][0].rearrange("g t s -> (g t) s")[bass.ds(g * P, P), :]
                               ).then_inc(g_in, 16)
                pool.dma_start(bs[0:1, :], t["even_sgu_b"][0][bass.ds(g, 1), :]).then_inc(g_in, 16)
                nc.gpsimd.tensor_copy(v_g[:, :, :], big[:, :, bass.ds(g * P, P)]).then_inc(vg_ready, 1)
                strip(Index(Q_SGU + u, i * 2, i), w_out0, i * 2 * P + (D + u * P))
                pool.wait_ge(mix_done, g + 1)
        ln_load(pool, 1, "ln_mix_g", "ln_mix_b", 0)
        mlp_strips(pool, strip, 0, Q_MLP0)
        nc.gpsimd.iota(tab[:, :], pattern=[[-1, SEQ]], base=SEQ - P, channel_multiplier=1,
                       allow_small_or_imprecise_dtypes=True).then_inc(tab_iota, 1)
        ln_load(pool, 2, "ln_ffn_g", "ln_ffn_b", 0)

        def att_strip(q, row):
            pool.wait_ge(wd_split, q.count(0))
            pool.dma_start(wd_raw[:, 0], w_out1[bass.ds(row, P), :]).then_inc(wd_in[q.slot], 16)

        with pool.Fori(0, DIFF_H // 2) as i:
            for u in range(2):
                att_strip(Index(Q_ATT + u, i * 2, i), i * 2 * P + u * P)
        pool.wait_ge(du_done, 2 * TT * DIFF_H)
        pool.wait_ge(wd_split, Q_MLP1)
        ln_load(pool, 3, "ln_mix_g", "ln_mix_b", 1)
        mlp_strips(pool, strip, 1, Q_MLP1)
        ln_load(pool, 4, "ln_ffn_g", "ln_ffn_b", 1)

    @block.tensor
    def _(pe):
        mm = nc.tensor.matmul

        def three(ps, hi, lo, mhi, mlo, start, stop):
            mm(ps, hi, mhi, start=start, stop=False)
            mm(ps, hi, mlo, start=False, stop=False)
            return mm(ps, lo, mhi, start=False, stop=stop)

        def up(n):
            pe.wait_ge(wu_split, n.count(1))
            for b in range(2):
                if n.at >= 2:
                    pe.wait_ge(up_free, n.count(b - 3, 2))
                for k in range(KT):
                    cut = slice(b * HALF, (b + 1) * HALF)
                    last = three(up_ps[n.slot][:, cut], wu_hi[:, n.slot, k, :], wu_lo[:, n.slot, k, :],
                                 act_hi[:, k, cut], act_lo[:, k, cut], k == 0, k == KT - 1)
                last.then_inc(up_done, 1)

        def down(d, width, q, h):
            pe.wait_ge(wd_split, q.count(width))
            for s in range(TT):
                if 8 * d.at + s >= 2:
                    pe.wait_ge(dn_free, d.count(s - 1, TT))
                for c in range(width):
                    if s == 0:
                        pe.wait_ge(hid_ready, h.count(c + 1))
                    w, row, tok = (q + c).slot, (c if width == 2 else q.slot), slice(s * P, (s + 1) * P)
                    for st, mv in ((hid_hi, wd_hi), (hid_hi, wd_lo), (hid_lo, wd_hi)):
                        for b in range(2):
                            cut = slice(b * HALF, (b + 1) * HALF)
                            last = mm(dn_ps[s % 2][:, cut], st[:, row, tok], mv[:, w, cut],
                                      start=(c == 0 and (st, mv) == (hid_hi, wd_hi)),
                                      stop=(c == width - 1 and st is hid_lo))
                last.then_inc(dn_done, 1)

        def transposes(src, number):
            for s in range(TT):
                if s >= 2:
                    pe.wait_ge(tr_split, TT * number + s - 1)
                if number == 0:
                    pe.wait_ge(x_in[s // 2], 16)
                else:
                    pe.wait_ge(ln_done, TT * number + s + 1)
                for k in range(KT):
                    last = nc.tensor.transpose(up_ps[s % 2][:, k * P:(k + 1) * P], src[:, s, k * P:(k + 1) * P],
                                               ident[:, :])
                last.then_inc(tr_done, 1)
            pe.wait_ge(tr_split, TT * (number + 1))

        pe.wait_ge(consts, 7)
        transposes(big, 0)

        pe.wait_ge(small_in, 16 * SMALL)
        nc.tensor.transpose(dn_ps[0][:, 0:ROWS], rows[:, :], ident[0:ROWS, 0:ROWS])
        pe.wait_ge(feat_ready, 1)
        nc.tensor.transpose(dn_ps[0][:, HALF:HALF + KT], d_rep[:, :], ident[0:KT, 0:KT]).then_inc(par_t, 1)
        up(Index(N_DT))
        pe.wait_ge(up_free, 2)
        for c in range(TT):
            last = nc.tensor.transpose(dn_ps[1][:, c * HEADS:(c + 1) * HEADS], dtT[:, c * P:(c + 1) * P],
                                       ident[0:HEADS, 0:HEADS])
        last.then_inc(dt_tok, 1)
        pe.wait_ge(par_ready, 1)
        pe.wait_ge(feat_done, 1)
        for i, m in enumerate((upper, ones)):
            last = mm(dn_ps[0][:, i * P:(i + 1) * P].rearrange("p (c h) -> p c h", c=TT), m[:, :], par[:, :, DA, :],
                      start=True, stop=True, skip_group_check=True)
        last.then_inc(dec_mm, 1)

        for g in range(GROUPS):
            n = N_SSD + g * SSD_TILES
            up(Index(n))
            if g:
                pe.wait_ge(y_read, 5 * g)
            up(Index(n + 1))
            pe.wait_ge(silu_done, 6 * g + 1)
            if g == 0:
                pe.wait_ge(par_ready, 2)
            for c in range(TT):
                nc.tensor.transpose(dn_ps[0][:, c * P:(c + 1) * P], xsT[:, c * P:(c + 1) * P], ident[:, :])
            pe.wait_ge(silu_done, 6 * g + 2)
            for c in range(TT):
                cut = slice(c * P, (c + 1) * P)
                last = mm(dn_ps[1][:, cut], xsT[:, cut], cT[:, cut], start=True, stop=True, skip_group_check=True)
            last.then_inc(bt_done, 1)
            with pe.Fori(0, TPG) as j:
                J = Index(g * TPG, j)
                xn = Index(n + 2, j * 2, j)

                def running_sums(head, ps):
                    for c in range(TT):
                        last = mm(ps[:, c * P:(c + 1) * P], parj[:, c, DA, head:head + 1].broadcast_to([P, P]),
                                  upper[:, :], start=True, stop=True, skip_group_check=True)
                    last.then_inc(cum_done, 1)

                up(xn)
                pe.wait_ge(parj_ready, J.count(1))
                pe.wait_ge(y_read, 5 * g + 1)
                running_sums(0, dn_ps[1])
                pe.wait_ge(y_read, J.count(g + 1))
                up(xn + 1)
                pe.wait_ge(bt_evac, g + 1)
                pe.wait_ge(silu_done, J.count(3 + 2 * g))
                for c in range(TT):
                    last = nc.tensor.transpose(dn_ps[0][:, c * P:(c + 1) * P], xsT[:, c * P:(c + 1) * P], ident[:, :])
                last.then_inc(xt_done, 1)
                pe.wait_ge(xd_ready, J.count(1))
                for c in range(TT):
                    last = mm(up_ps[1][:, c * P:(c + 1) * P], b_tok[:, c, :], x_dec[:, c, :], start=True, stop=True,
                              skip_group_check=True)
                last.then_inc(st_done, 1)
                running_sums(1, dn_ps[0])
                pe.wait_ge(scan_done, J.count(1))
                pe.wait_ge(up_free, (xn + 1).count(2, 2))
                for head in range(HPT):
                    pe.wait_ge(mc_ready, J.count(head + 1, HPT))
                    hs = slice(head * 64, (head + 1) * 64)
                    for c in range(TT):
                        cut = slice(c * P, (c + 1) * P)
                        if c:
                            mm(up_ps[0][hs, cut], state[:, c, hs], c_dec[:, cut], start=True, stop=False,
                               skip_group_check=True)
                        last = mm(up_ps[0][hs, cut], x_dt[:, c, hs], mt[:, cut], start=(c == 0), stop=True,
                                  skip_group_check=True)
                    last.then_inc(y_done, 1)
        for j in range(KT):
            pe.wait_ge(ysq, j + 1)
            for s in range(TT):
                col = (j // TPG) * TT + s
                last = mm(dn_ps[0][:, col:col + 1], (mt, c_dec)[j % 2][:, s * P:(s + 1) * P], ones[:, 0:1],
                          start=(j == 0 and s == 0), stop=(j % TPG == TPG - 1), skip_group_check=True)
            last.then_inc(ysq_used, 1)
        pe.wait_ge(rms_ready, 1)
        for m in range(KT // 2):
            down(Index(D_SSD + m), 2, Index(Q_SSD + 2 * m), Index(2 * m))

        pe.wait_ge(dn_free, TT * D_SGU)
        for b in range(2):
            for kp in range(KT // 2):
                q = Q_V + b * (KT // 2) + kp
                pe.wait_ge(wd_split, q + 1)
                for kk in range(2):
                    k = 2 * kp + kk
                    cut = slice(kk * HALF, (kk + 1) * HALF)
                    for s in range(TT):
                        if b and k == 0:
                            pe.wait_ge(v_evac, s + 1)
                        tok = slice(s * P, (s + 1) * P)
                        ps = (up_ps, dn_ps)[s // 4][s % 4 // 2][:, (s % 2) * HALF:(s % 2 + 1) * HALF]
                        last = three(ps, act_hi[:, k, tok], act_lo[:, k, tok], wd_hi[:, q % 2, cut],
                                     wd_lo[:, q % 2, cut], k == 0, k == KT - 1)
                        if k == KT - 1:
                            last.then_inc(v_done, 1)
                if k < KT - 1:
                    last.then_inc(v_piece, 1)
        pe.wait_ge(v_evac, 2 * TT)
        with pe.Fori(0, SGU_G // 2) as i:
            for u in range(2):
                g = Index(u, i * 2)
                up(Index(N_SGU + u, i * 2, i))
                pe.wait_ge(g_in, g.count(32, 32))
                if u:
                    pe.wait_ge(uy_ready, g.count(0))
                else:
                    pe.wait_ge(dn_free, Index(D_SGU, i).count(0, TT))
                nc.tensor.transpose(dn_ps[0][:, 0:P], ws[:, :], ident[:, :]).then_inc(ws_t, 1)
                for b in range(2):
                    mm(dn_ps[1][:, b * HALF:(b + 1) * HALF].rearrange("p (c t) -> p c t", t=P), ones[0:1, :],
                       bs[0:1, :].unsqueeze(1).broadcast_to([1, HALF // P, P]), start=True, stop=False,
                       skip_group_check=True)
                pe.wait_ge(ws_ready, g.count(1))
                pe.wait_ge(vg_ready, g.count(1))
                for b in range(TT):
                    last = mm(dn_ps[1][:, b * P:(b + 1) * P], v_g[:, b, :], wsT[:, :], start=False, stop=True,
                              skip_group_check=True)
                last.then_inc(mix_done, 1)
            down(Index(D_SGU, i), 2, Index(Q_SGU, i * 2, i), Index(H_SGU, i * 2))

        def mlp(n0, q0, d0, h0):
            with pe.Fori(0, F_FF // P // 2) as i:
                for u in range(2):
                    up(Index(n0 + u, i * 2, i))
                down(Index(d0, i), 2, Index(q0, i * 2, i), Index(h0, i * 2))

        transposes(acc, 1)
        mlp(N_MLP0, Q_MLP0, D_MLP0, H_MLP0)
        transposes(acc, 2)

        pt_ps, o_ps = up_ps[0][:, 0:HALF], up_ps[0][:, HALF:SEQ]
        fill_ps, unit_ps = up_ps[1][:, 0:HALF], up_ps[1][:, HALF:SEQ]

        def up_half(n, b):
            if b == 0:
                pe.wait_ge(wu_split, n.count(1))
            pe.wait_ge(up_free, n.count(b, 2))
            for k in range(KT):
                last = three(fill_ps, wu_hi[:, n.slot, k, :], wu_lo[:, n.slot, k, :],
                             act_hi[:, k, b * HALF:(b + 1) * HALF], act_lo[:, k, b * HALF:(b + 1) * HALF],
                             k == 0, k == KT - 1)
            last.then_inc(up_done, 1)

        def scores(parity, k):
            s = ORDER[k]
            width = (s + 1) * P
            (qh, ql), (kh, kl) = qs[parity], ks[parity]
            for m in range(2):
                d = slice(m * 64, (m + 1) * 64)
                for at in range(0, width, HALF):
                    cut = slice(at, min(at + HALF, width))
                    last = three(dn_ps[m][:, cut], qh[d, s * P:(s + 1) * P], ql[d, s * P:(s + 1) * P],
                                 kh[d, cut], kl[d, cut], True, True)
            last.then_inc(s_done, 1)

        def units(H, at, to):
            for x in range(at, to):
                s, b = UNITS[x]
                pe.wait_ge(du_free, H.count(x, 2 * TT)) if H.at or x else None
                for st, mv in ((hid_hi, wd_hi), (hid_hi, wd_lo), (hid_lo, wd_hi)):
                    last = mm(unit_ps, st[:, 0, s * P:(s + 1) * P], mv[:, 0, b * HALF:(b + 1) * HALF],
                              start=(mv is wd_hi and st is hid_hi), stop=(st is hid_lo))
                last.then_inc(du_done, 1)

        def sums_of_squares(H, gr):
            pe.wait_ge(osq_done, H.count(gr + 1, 2))
            for c in range(4):
                last = mm(unit_ps[:, c:c + 1], osq[:, c * P:(c + 1) * P], ones[:, 0:1], start=True, stop=True,
                          skip_group_check=True)
            last.then_inc(osum_done, 1)

        def head(H, parity, n, down, more):
            prev = H + -1
            for k in range(TT):
                s = ORDER[k]
                K = k
                if k < TT - 1 or more:
                    pe.wait_ge(s_biased, H.count(K + 1, TT))
                    if k == TT - 1:
                        pe.wait_ge(up_free, n.count(4, 2))
                        scores(1 - parity, 0)
                    else:
                        scores(parity, k + 1)
                if k == 0:
                    pe.wait_ge(up_free, n.count(0, 2))
                    if down:
                        pe.wait_ge(du_free, prev.count(0, 2 * TT)) if prev.at else None
                    for c in range(TT):
                        last = nc.tensor.transpose(up_ps[1][:, c * P:(c + 1) * P], vT[:, c * P:(c + 1) * P],
                                                   ident[:, :])
                    last.then_inc(vt_done, 1)
                pe.wait_ge(attn_ready, H.count(K + 1, TT))
                e = e01[:, 0, ebuf(s)]
                for c in range(min(s + 1, 4)):
                    last = nc.tensor.transpose(pt_ps[:, c * P:(c + 1) * P], e[:, c * P:(c + 1) * P], ident[:, :])
                last.then_inc(pt_done, 1)
                if k == 0:
                    pe.wait_ge(v_ready, H.count(1))
                    if down:
                        sums_of_squares(prev, 1)
                at, to = UNITS_AT[k] if down else (0, 0)
                if k == 1 and down:
                    pe.wait_ge(os_dve, prev.count(2, 2))
                    pe.wait_ge(o_read, prev.count(2, 2))
                    pe.wait_ge(wd_split, Index(Q_ATT - 1, H.off).count(H.at))
                if k == 4:
                    if down:
                        pe.wait_ge(du_free, prev.count(8, 2 * TT))
                    sums_of_squares(H, 0)
                    if down:
                        pe.wait_ge(os_dve, H.count(1, 2))
                units(prev, at, min(at + 1, to))
                if more and k in UP_AT:
                    c, b = UP_AT[k]
                    up_half(n + c, b)
                if s >= 4:
                    pe.wait_ge(pt_ready, H.count(K + 1, TT))
                    for c in range(4, s + 1):
                        last = nc.tensor.transpose(pt_ps[:, (c - 4) * P:(c - 3) * P], e[:, c * P:(c + 1) * P],
                                                   ident[:, :])
                    last.then_inc(ptb_done, 1)
                units(prev, at + 1, min(at + 2, to))
                if s < 4:
                    pe.wait_ge(pt_ready, H.count(K + 1, TT))
                if k == 4:
                    pe.wait_ge(o_read, H.count(1, 2))
                if k == 0 and down:
                    pe.wait_ge(o_read, prev.count(2, 2))
                col = GROUP[k // 4].index(s) * P
                for c in range(s + 1):
                    if c == 4:
                        pe.wait_ge(ptb_ready, H.count(k // 2 + 1, 4))
                    last = three(o_ps[:, col:col + P], v_hi[:, c, :], v_lo[:, c, :], pt_hi[:, c, :], pt_lo[:, c, :],
                                 c == 0, c == s)
                if k % 4 == 3:
                    last.then_inc(o_done, 1)
                units(prev, at + 2, to)

        for c in range(3):
            for b in range(2):
                up_half(Index(N_ATT + c), b)
        pe.wait_ge(up_free, 2 * N_ATT + 4)
        scores(0, 0)
        head(Index(0), 0, Index(N_ATT + 3), False, True)
        with pe.Fori(0, DIFF_H // 2 - 1) as i:
            for u in range(2):
                head(Index(1 + u, i * 2), 1 - u, Index(N_ATT + 6 + 3 * u, i * 6, i * 3), True, True)
        head(Index(DIFF_H - 1), 1, Index(N_MLP1), True, False)
        last_head = Index(DIFF_H - 1)
        pe.wait_ge(du_free, last_head.count(0, 2 * TT))
        sums_of_squares(last_head, 1)
        pe.wait_ge(os_dve, last_head.count(2, 2))
        pe.wait_ge(wd_split, Q_MLP1)
        units(last_head, 0, 2 * TT)
        transposes(acc, 3)
        mlp(N_MLP1, Q_MLP1, D_MLP1, H_MLP1)

    @block.scalar
    def _(act):
        fn = nc.scalar.activation

        def round_up_weights(n):
            act.wait_ge(wu_in[n.slot], n.filled())
            if n.at >= 2:
                act.wait_ge(up_done, n.count(-2, 2))
            fn(wu_hi[:, n.slot], wu_raw[:, n.slot], ACT.Copy).then_inc(wu_rounded, 1)

        def round_strip(q):
            act.wait_ge(wd_in[q.slot], q.filled())
            fn(wd_hi[:, q.slot], wd_raw[:, q.slot], ACT.Copy).then_inc(wd_rounded, 1)

        def round_act(number, s):
            act.wait_ge(tr_done, TT * number + s + 1)
            fn(act_hi[:, :, s * P:(s + 1) * P], eight(up_ps[s % 2]), ACT.Copy).then_inc(tr_rounded, 1)

        def deviation(number, s):
            act.wait_ge(ln_var, TT * number + s + 1)
            m = moments[:, s % 2, 2:3]
            fn(m, m, ACT.Sqrt).then_inc(ln_std, 1)

        round_up_weights(Index(N_DT))
        for s in range(TT):
            round_act(0, s)
        act.wait_ge(par_t, 1)
        act.wait_ge(lam_dve, 1)
        fn(lam[:, 0:2], lam[:, 0:2], ACT.Exp).then_inc(lam_act, 1)
        fn(feat[:, :], dn_ps[0][:, 0:ROWS], ACT.Copy)
        fn(skip[:, :], dn_ps[0][:, HALF:HALF + KT], ACT.Copy).then_inc(feat_done, 1)
        round_up_weights(Index(N_DT + 1))
        for b in range(2):
            act.wait_ge(up_done, b + 1)
            fn(dtT[:, b * HALF:(b + 1) * HALF], up_ps[0][0:HEADS, b * HALF:(b + 1) * HALF], ACT.Identity,
               bias=dtb[:, 0:1]).then_inc(up_free, 1)
        act.wait_ge(dt_tok, 1)
        fn(sp[:, 0, :], dn_ps[1][:, 0:P], ACT.Abs).then_inc(act_step, 1)
        act.wait_ge(act_step, 1)
        fn(sp[:, 1, :], sp[:, 0, :], ACT.Exp, scale=-1.0).then_inc(sp_act, 1)
        fn(a_row[:, :], a_row[:, :], ACT.Exp).then_inc(sp_act, 1)
        act.wait_ge(sp_dve, 1)
        fn(sp[:, 3, :], sp[:, 2, :], ACT.Ln).then_inc(sp_act, 1)
        act.wait_ge(sp_dve, 2)
        fn(par[:, :, DECAY, :], par[:, :, DECAY, :], ACT.Exp).then_inc(sp_act, 1)
        fn(par[:, :, CHUNKDECAY, :], par[:, :, CHUNKDECAY, :], ACT.Exp).then_inc(sp_act, 1)

        def conv_in(n, conv):
            for b in range(2):
                act.wait_ge(up_done, n.count(b + 1, 2))
                if b == 0 and conv.at >= 1:
                    act.wait_ge(conv_done, conv.count(0))
                fn(cin[:, CONV - 1 + b * HALF:CONV - 1 + (b + 1) * HALF], up_ps[n.slot][:, b * HALF:(b + 1) * HALF],
                   ACT.Copy).then_inc(up_free, 1)

        def silu_conv(conv, x):
            act.wait_ge(conv_done, conv.count(1))
            fn(x, x, ACT.Silu).then_inc(silu_done, 1)

        act.wait_ge(par_ready, 2)
        for g in range(GROUPS):
            n = N_SSD + g * SSD_TILES
            round_up_weights(Index(n + 1))
            conv_in(Index(n), Index(6 * g))
            round_up_weights(Index(n + 2))
            silu_conv(Index(6 * g), xsT[:, :])
            conv_in(Index(n + 1), Index(6 * g + 1))
            silu_conv(Index(6 * g + 1), cT[:, :])
            act.wait_ge(bt_done, g + 1)
            fn(b_tok[:, :, :], eight(dn_ps[0]), ACT.Copy).then_inc(bt_evac, 1)
            with act.Fori(0, TPG) as j:
                J = Index(g * TPG, j)
                xn = Index(n + 2, j * 2, j)
                conv = Index(6 * g + 2, j)
                round_up_weights(xn + 1)
                conv_in(xn, conv)
                silu_conv(conv, xsT[:, :])
                round_up_weights(xn + 2)
                for head in range(HPT):
                    if head == 1:
                        for b in range(2):
                            act.wait_ge(up_done, (xn + 1).count(b + 1, 2))
                            fn(big[:, bass.ds(j + g * TPG, 1), b * HALF:(b + 1) * HALF],
                               up_ps[0][:, b * HALF:(b + 1) * HALF].unsqueeze(1), ACT.Silu).then_inc(up_free, 1)
                    act.wait_ge(cum_done, J.count(head + 1, HPT))
                    if head:
                        act.wait_ge(y_done, J.count(1, HPT))
                    else:
                        act.wait_ge(y_read, J.count(g + 1))
                    act.wait_ge(seg_done, J.count(head + 1, HPT))
                    fn(mt[:, :], mt[:, :], ACT.Exp).then_inc(mexp_done, 1)
                    fn(c_dec[:, :], dn_ps[1 - head][:, :], ACT.Exp).then_inc(cexp_done, 1)
        act.wait_ge(yg_ready, KT)
        for j in range(KT):
            if j >= 2:
                act.wait_ge(ysq_used, j - 1)
            fn((mt, c_dec)[j % 2][:, :], big[:, j, :], ACT.Square).then_inc(ysq, 1)
        act.wait_ge(rms_var, 1)
        fn(rms[:, :, :], rms[:, :, :], ACT.Sqrt).then_inc(rms_std, 1)
        for c in range(2):
            round_strip(Index(Q_SSD + c))
        act.wait_ge(acc_in, 16)
        for s in range(TT):
            fn(acc[:, s, :], acc[:, s, :], ACT.Copy, scale=ALPHA).then_inc(acc_ready, 1)
        for m in range(KT // 2):
            if m:
                act.wait_ge(dn_done, TT * (D_SSD + m))
            for c in range(2):
                j = 2 * m + c
                if m:
                    round_strip(Index(Q_SSD + j))
                fn(hid_hi[:, c, :], big[:, j, :], ACT.Copy, scale=feat[:, ROW_NW + j:ROW_NW + j + 1]
                   ).then_inc(hid_rounded, 1)

        def v_out(b):
            for s in range(TT):
                act.wait_ge(v_done, b * TT + s + 1)
                ps = (up_ps, dn_ps)[s // 4][s % 4 // 2][:, (s % 2) * HALF:(s % 2 + 1) * HALF]
                fn(big[:, s, b * HALF:(b + 1) * HALF], ps, ACT.Gelu).then_inc(v_evac, 1)

        for p in range(KT):
            if p < 2:
                act.wait_ge(dn_done, TT * D_SGU)
            else:
                wait_piece(act, p - 2)
            if p == KT // 2 + 1:
                v_out(0)
            round_strip(Index(Q_V + p))
        v_out(1)
        for s in range(TT):
            deviation(0, s)
        with act.Fori(0, SGU_G // 2) as i:
            for u in range(2):
                n = Index(N_SGU + u, i * 2, i)
                h = Index(KT + u, i * 2)
                round_up_weights(n + 1)
                act.wait_ge(dn_done, Index(D_SGU, i).count(0, TT))
                round_strip(Index(Q_SGU + u, i * 2, i))
                act.wait_ge(hid_ready, h.count(0))
                for b in range(2):
                    act.wait_ge(up_done, n.count(b + 1, 2))
                    fn(u_t[:, b * HALF:(b + 1) * HALF], up_ps[n.slot][:, b * HALF:(b + 1) * HALF], ACT.Gelu
                       ).then_inc(up_free, 1)
                act.wait_ge(uy_ready, Index(u, i * 2).count(1))
                fn(hid_hi[:, u, :], u_t[:, :], ACT.Copy).then_inc(hid_rounded, 1)

        def mlp(n0, q0, d0, h0, l):
            def turn(i, last):
                for u in range(2):
                    n = Index(n0 + u, i * 2, i)
                    h = Index(h0 + u, i * 2)
                    tile = Index(l * (F_FF // P) + u, i * 2)
                    if not (last and u):
                        round_up_weights(n + 1)
                    act.wait_ge(dn_done, Index(d0, i).count(0, TT))
                    round_strip(Index(q0 + u, i * 2, i))
                    act.wait_ge(hid_ready, h.count(0))
                    for b in range(2):
                        cut = slice(b * HALF, (b + 1) * HALF)
                        act.wait_ge(up_done, n.count(b + 1, 2))
                        fn(relu_h[:, b, :], up_ps[n.slot][:, cut], ACT.Relu).then_inc(up_free, 1)
                        act.wait_ge(up_free, n.count(b + 1, 2))
                        fn(hid_hi[:, u, cut], relu_h[:, b, :], ACT.Square).then_inc(sq_rounded, 1)

            turns = F_FF // P // 2
            with act.Fori(0, turns - l) as i:
                turn(i, False)
            if l:
                turn(turns - 1, True)

        def norm(number):
            deviation(number, 0)
            for s in range(TT):
                if s + 1 < TT:
                    deviation(number, s + 1)
                if number < 4:
                    round_act(number, s)
                    fn(acc[:, s, :], acc[:, s, :], ACT.Copy, scale=ALPHA).then_inc(acc_ready, 1)

        norm(1)
        mlp(N_MLP0, Q_MLP0, D_MLP0, H_MLP0, 0)
        norm(2)

        pt_ps, o_ps = up_ps[0][:, 0:HALF], up_ps[0][:, HALF:SEQ]
        fill_ps = up_ps[1][:, 0:HALF]

        def half_out(n, c, b, parity):
            if c < 2:
                act.wait_ge(up_done, (n + c).count(b + 1, 2))
                fn((qs, ks)[c][parity][0][:, b * HALF:(b + 1) * HALF], fill_ps, ACT.Copy).then_inc(qkv_rounded, 1)

        def weights(H, k, parity):
            act.wait_ge(negmax, H.count(k + 1, TT))
            for m in range(2):
                e = e01[:, m, ebuf(ORDER[k])]
                last = fn(e, e, ACT.Exp, bias=cols[:, 2 + m:3 + m], scale=SCALE, accum_out=cols[:, 4 + m:5 + m])
            last.then_inc(e_done, 1)

        def group_out(H, gr):
            act.wait_ge(o_done, H.count(gr + 1, 2))
            fn(osq, o_ps, ACT.Square).then_inc(osq_done, 1)
            fn(hid_group(hid_hi, gr), group_ps(o_ps, gr), ACT.Copy, scale=feat[:, ROW_SUB:ROW_SUB + 1]
               ).then_inc(hid_rounded_att, 1)

        def deviations(H):
            act.wait_ge(os_ready, H.count(1))
            fn(ostat[:, 1, :], ostat[:, 1, :], ACT.Sqrt).then_inc(os_std, 1)

        def head(H, parity, n, down, more, filled):
            prev = H + -1
            for k in range(TT):
                if k and more and k - 1 in UP_AT:
                    half_out(n, *UP_AT[k - 1], 1 - parity)
                if k == 0:
                    act.wait_ge(vt_done, H.count(1))
                    fn(v_hi[:, :, :], eight(up_ps[1]), ACT.Copy).then_inc(vt_rounded, 1)
                    if down:
                        group_out(prev, 1)
                if k == 4:
                    group_out(H, 0)
                act.wait_ge(pt_done, H.count(k + 1, TT))
                w = min(ORDER[k] + 1, 4)
                fn(pt_hi[:, 0:w, :], four(pt_ps)[:, 0:w, :], ACT.Copy).then_inc(pt_rounded, 1)
                if k < TT - 1:
                    weights(H, k + 1, parity)
                elif more:
                    weights(H + 1, 0, 1 - parity)
                if k == 0 and down:
                    deviations(prev)
                    if prev.at:
                        act.wait_ge(du_done, prev.count(0, 2 * TT))
                    round_att_strip(prev)
                if ORDER[k] >= 4:
                    act.wait_ge(ptb_done, H.count(k // 2 + 1, 4))
                    w = ORDER[k] + 1
                    fn(pt_hi[:, 4:w, :], four(pt_ps)[:, 0:w - 4, :], ACT.Copy).then_inc(ptb_rounded, 1)
                if more and k in UP_AT and UP_AT[k][1] == 0:
                    round_up_weights(n + (UP_AT[k][0] + 1))

        def round_att_strip(H):
            q = Index(Q_ATT + H.at, H.off, H.half)
            act.wait_ge(wd_in[q.slot], q.filled())
            fn(wd_hi[:, 0], wd_raw[:, 0], ACT.Copy).then_inc(wd_rounded, 1)

        for c in range(3):
            n = Index(N_ATT)
            round_up_weights(n + (c + 1))
            for b in range(2):
                half_out(n, c, b, 0)
        weights(Index(0), 0, 0)
        head(Index(0), 0, Index(N_ATT + 3), False, True, False)
        with act.Fori(0, DIFF_H // 2 - 1) as i:
            for u in range(2):
                head(Index(1 + u, i * 2, i), 1 - u, Index(N_ATT + 6 + 3 * u, i * 6, i * 3), True, True, True)
        last_head = Index(DIFF_H - 1)
        head(last_head, 1, Index(N_MLP1), True, False, True)
        group_out(last_head, 1)
        deviations(last_head)
        act.wait_ge(du_done, last_head.count(0, 2 * TT))
        round_att_strip(last_head)
        norm(3)
        mlp(N_MLP1, Q_MLP1, D_MLP1, H_MLP1, 1)
        norm(4)

    @block.vector
    def _(dve):
        ts, tt, stt = nc.vector.tensor_scalar, nc.vector.tensor_tensor, nc.vector.scalar_tensor_tensor
        step = Chain(dve, dve_step)

        def split_up_weights(n):
            dve.wait_ge(wu_rounded, n.count(1))
            tt(wu_lo[:, n.slot], wu_raw[:, n.slot], wu_hi[:, n.slot], ALU.subtract).then_inc(wu_split, 1)

        def split_strip(q):
            dve.wait_ge(wd_rounded, q.count(1))
            tt(wd_lo[:, q.slot], wd_raw[:, q.slot], wd_hi[:, q.slot], ALU.subtract).then_inc(wd_split, 1)

        def split_act(number, s):
            dve.wait_ge(tr_rounded, TT * number + s + 1)
            cut = slice(s * P, (s + 1) * P)
            tt(act_lo[:, :, cut], eight(up_ps[s % 2]), act_hi[:, :, cut], ALU.subtract).then_inc(tr_split, 1)

        def add_down(d, scale=None):
            for s in range(TT):
                dve.wait_ge(dn_done, d.count(s + 1, TT))
                if d.at:
                    dve.wait_ge(dn_free, d.count(s - TT + 1, TT))
                if scale is None:
                    ins = tt(acc[:, s, :], dn_ps[s % 2][:, :], acc[:, s, :], ALU.add)
                else:
                    ins = stt(acc[:, s, :], dn_ps[s % 2][:, :], scale(s), acc[:, s, :], ALU.mult, ALU.add)
                ins.then_inc(dn_free, 1)

        def norm(number, src, gain, bias):
            def variance(s):
                m = moments[:, s % 2]
                for b in range(2):
                    last = nc.vector.bn_stats(stats[:, s % 2, b, :], src[:, s, b * HALF:(b + 1) * HALF])
                step(last)
                step(nc.vector.bn_aggr(m[:, 0:2], stats[:, s % 2].rearrange("p b c -> p (b c)")))
                ts(m[:, 2:3], m[:, 1:2], EPS, None, ALU.add).then_inc(ln_var, 1)

            if number:
                dve.wait_ge(*{1: (dn_free, TT * D_MLP0), 2: (dn_free, TT * D_MLP1), 3: (du_free, 2 * TT * DIFF_H),
                               4: (dn_free, TT * D_END)}[number])
            else:
                dve.wait_ge(v_evac, 2 * TT)
            variance(0)
            dve.wait_ge(ln_in, 32 * (number + 1))
            for s in range(TT):
                if s + 1 < TT:
                    variance(s + 1)
                m = moments[:, s % 2]
                dve.wait_ge(ln_std, TT * number + s + 1)
                step(nc.vector.reciprocal(m[:, 3:4], m[:, 2:3]))
                step(ts(src[:, s, :], src[:, s, :], m[:, 0:1], m[:, 3:4], ALU.subtract, ALU.mult))
                step(tt(src[:, s, :], src[:, s, :], gain[:, :], ALU.mult))
                tt(src[:, s, :], src[:, s, :], bias[:, :], ALU.add).then_inc(ln_done, 1)
                if s and 0 < number < 4:
                    split_act(number, s - 1)
            if 0 < number < 4:
                split_act(number, TT - 1)

        dve.wait_ge(small_in, 16 * SMALL)
        for i in range(2):
            last = nc.vector.tensor_tensor_reduce(lrow[:, 2 * i, :], lrow[:, 2 * i, :], lrow[:, 2 * i + 1, :], 1.0, 0.0,
                                                  ALU.mult, ALU.add, lam[:, i:i + 1])
        last.then_inc(lam_dve, 1)
        nc.vector.tensor_copy(d_rep[:, :].rearrange("j (h p) -> j h p", h=HPT),
                              d_rows[:, :].unsqueeze(2).broadcast_to([KT, HPT, 64])).then_inc(feat_ready, 1)
        split_up_weights(Index(N_DT))
        for s in range(TT):
            split_act(0, s)
        dve.wait_ge(lam_act, 1)
        step(tt(lam[:, 2:3], lam[:, 0:1], lam[:, 1:2], ALU.subtract))
        step(ts(lam[:, 3:4], lam[:, 2:3], LAMBDA_INIT, -1.0, ALU.add, ALU.mult))
        split_up_weights(Index(N_DT + 1))
        e, one_e, ln_e, rest, none = (sp[:, i, :] for i in (1, 2, 3, 4, 5))
        dve.wait_ge(sp_act, 1)
        ts(one_e, e, 1.0, None, ALU.add).then_inc(sp_dve, 1)
        dve.wait_ge(sp_dve, 1)
        step(ts(rest, one_e, -1.0, None, ALU.add))
        step(ts(none, rest, 0.0, None, ALU.is_equal))
        step(tt(rest, rest, none, ALU.add))
        step(nc.vector.reciprocal(rest, rest))
        step(tt(rest, rest, e, ALU.mult))
        dve.wait_ge(sp_act, 3)
        step(tt(ln_e, ln_e, rest, ALU.mult))
        step(tt(none, none, e, ALU.mult))
        step(tt(ln_e, ln_e, none, ALU.add))

        def ch(x):
            return x.rearrange("p (c h) -> p c h", h=HEADS)

        step(stt(par[:, :, DT, :], ch(dn_ps[1][:, 0:P]), 0.0, ch(ln_e), ALU.max, ALU.add))
        stt(par[:, :, DA, :], par[:, :, DT, :], -1.0, a_row[:, :].unsqueeze(1).broadcast_to([P, TT, HEADS]),
            ALU.mult, ALU.mult).then_inc(par_ready, 1)
        dve.wait_ge(dec_mm, 1)
        step(nc.vector.tensor_copy(par[:, :, ACS, :], ch(dn_ps[0][:, 0:P])))
        tt(par[:, :, DECAY, :], ch(dn_ps[0][:, P:2 * P]), par[:, :, ACS, :], ALU.subtract)
        nc.vector.tensor_copy(par[:, :, CHUNKDECAY, :], ch(dn_ps[0][:, P:2 * P])).then_inc(sp_dve, 1)
        dve.wait_ge(sp_act, 5)
        tt(par[:, :, DECAY, :], par[:, :, DECAY, :], par[:, :, DT, :], ALU.mult).then_inc(par_ready, 1)

        def feature_params(tile):
            step(nc.vector.tensor_copy(parf[:, 0:CONV + 1], feat[:, 0:ROW_NW].rearrange("p (k f) -> p k f", f=12)
                                       [:, :, bass.ds(tile, 1)].squeeze(2)))

        def conv(n, x):
            dve.wait_ge(up_free, n.count(2, 2))
            step(ts(x, cin[:, 0:SEQ], parf[:, 0:1], parf[:, CONV:CONV + 1], ALU.mult, ALU.add))
            for k in range(1, CONV):
                ins = stt(x, cin[:, k:k + SEQ], parf[:, k:k + 1], x, ALU.mult, ALU.add)
                step(ins) if k < CONV - 1 else ins.then_inc(conv_done, 1)

        dve.wait_ge(par_ready, 2)
        step(nc.vector.memset(cin[:, 0:CONV - 1], 0.0))
        for g in range(GROUPS):
            n = N_SSD + g * SSD_TILES
            split_up_weights(Index(n + 1))
            feature_params(KT + g)
            conv(Index(n), xsT[:, :])
            split_up_weights(Index(n + 2))
            dve.wait_ge(conv_done, 6 * g + 1)
            feature_params(KT + GROUPS + g)
            conv(Index(n + 1), cT[:, :])
            dve.wait_ge(bt_done, g + 1)
            nc.vector.tensor_copy(cb[:, :], dn_ps[1][:, :]).then_inc(y_read, 1)
            with step.loop(TPG, 11) as j:
                J = Index(g * TPG, j)
                xn = Index(n + 2, j * 2, j)
                split_up_weights(xn + 1)
                nc.vector.tensor_copy(parj[:, :, :, :], par[:, :, :, bass.ds(j * HPT + g * TPG * HPT, HPT)]
                                      ).then_inc(parj_ready, 1)
                step(nc.vector.tensor_copy(parf[:, 5:6], skip[:, bass.ds(j + g * TPG, 1)]))
                feature_params(j + g * TPG)
                conv(xn, xsT[:, :])
                split_up_weights(xn + 2)
                dve.wait_ge(parj_ready, J.count(1))
                for head in range(HPT):
                    dve.wait_ge(cum_done, J.count(head + 1, HPT))
                    if head:
                        dve.wait_ge(y_done, J.count(1, HPT))
                    for c in range(TT):
                        cut = slice(c * P, (c + 1) * P)
                        last = stt(mt[:, cut], dn_ps[1 - head][:, cut], parj[:, c, ACS, head:head + 1], negmask[:, :],
                                   ALU.subtract, ALU.add)
                    last.then_inc(seg_done, 1)
                    if head == 0:
                        dve.wait_ge(xt_done, J.count(1))
                        for x, kind in ((x_dt, DT), (x_dec, DECAY)):
                            last = tt(x[:, :, :].rearrange("p c (h e) -> p c h e", h=HPT),
                                      dn_ps[0][:, :].rearrange("p (c h e) -> p c h e", c=TT, h=HPT),
                                      parj[:, :, kind, :].unsqueeze(3).broadcast_to([P, TT, HPT, 64]), ALU.mult)
                        last.then_inc(xd_ready, 1)
                        dve.wait_ge(st_done, J.count(1))
                        step(nc.vector.tensor_copy(state[:, 1, :], up_ps[1][:, 0:P]))
                        for c in range(2, TT):
                            for hh in range(HPT):
                                hs = slice(hh * 64, (hh + 1) * 64)
                                ins = stt(state[:, c, hs], state[:, c - 1, hs],
                                          parj[:, c - 1, CHUNKDECAY, hh:hh + 1],
                                          up_ps[1][:, (c - 1) * P + hh * 64:(c - 1) * P + (hh + 1) * 64],
                                          ALU.mult, ALU.add)
                            step(ins) if c < TT - 1 else ins.then_inc(scan_done, 1)
                    dve.wait_ge(mexp_done, J.count(head + 1, HPT))
                    tt(mt[:, :], mt[:, :], cb[:, :], ALU.mult)
                    dve.wait_ge(cexp_done, J.count(head + 1, HPT))
                    tt(c_dec[:, :], c_dec[:, :], cT[:, :], ALU.mult).then_inc(mc_ready, 1)
                dve.wait_ge(y_done, J.count(HPT, HPT))
                stt(xsT[:, :], xsT[:, :], parf[:, 5:6], up_ps[0][:, :], ALU.mult, ALU.add).then_inc(y_read, 1)
                dve.wait_ge(y_read, J.count(g + 2))
                dve.wait_ge(up_free, (xn + 1).count(2, 2))
                y = big[:, bass.ds(j + g * TPG, 1), :].squeeze(1)
                tt(y, y, xsT[:, :], ALU.mult).then_inc(yg_ready, 1)
        dve.wait_ge(ysq_used, KT)
        ts(rms[:, :, :].rearrange("p g s -> p (g s)"), dn_ps[0][:, 0:GROUPS * TT], 1.0 / (TPG * P), EPS,
           ALU.mult, ALU.add).then_inc(rms_var, 1)
        dve.wait_ge(rms_std, 1)
        nc.vector.reciprocal(rms[:, :, :], rms[:, :, :]).then_inc(rms_ready, 1)
        dve.wait_ge(rms_ready, 1)
        for m in range(KT // 2):
            for c in range(2):
                j = 2 * m + c
                split_strip(Index(Q_SSD + j))
                dve.wait_ge(hid_rounded, j + 1)
                stt(hid_lo[:, c, :], big[:, j, :], feat[:, ROW_NW + j:ROW_NW + j + 1], hid_hi[:, c, :],
                    ALU.mult, ALU.subtract).then_inc(hid_ready, 1)
            if m == 0:
                dve.wait_ge(acc_ready, TT)
            add_down(Index(D_SSD + m), lambda s: rms[:, m // 2, s:s + 1])

        for p in range(KT):
            split_strip(Index(Q_V + p))
        norm(0, big, vgam, vbet)
        step(nc.vector.memset(wsT[64:P, 0:64], 0.0))
        with dve.Fori(0, SGU_G // 2) as i:
            for u in range(2):
                n = Index(N_SGU + u, i * 2, i)
                g = Index(u, i * 2)
                split_up_weights(n + 1)
                split_strip(Index(Q_SGU + u, i * 2, i))
                dve.wait_ge(ws_t, g.count(1))
                nc.vector.tensor_copy(wsT[0:64, :], dn_ps[0][0:64, 0:P])
                nc.vector.tensor_copy(wsT[64:P, 64:P], dn_ps[0][64:P, 64:P]).then_inc(ws_ready, 1)
                dve.wait_ge(up_free, n.count(2, 2))
                dve.wait_ge(mix_done, g.count(1))
                tt(u_t[:, :], u_t[:, :], dn_ps[1][:, :], ALU.mult).then_inc(uy_ready, 1)
                dve.wait_ge(hid_rounded, Index(KT + u, i * 2).count(1))
                tt(hid_lo[:, u, :], u_t[:, :], hid_hi[:, u, :], ALU.subtract).then_inc(hid_ready, 1)
            add_down(Index(D_SGU, i))
        norm(1, acc, gam, bet)

        def mlp(n0, q0, d0, l):
            dve.wait_ge(acc_ready, TT * (1 + n0_round[n0]))

            def turn(i, last):
                for u in range(2):
                    n = Index(n0 + u, i * 2, i)
                    tile = Index(l * (F_FF // P) + u, i * 2)
                    if not (last and u):
                        split_up_weights(n + 1)
                    split_strip(Index(q0 + u, i * 2, i))
                    for b in range(2):
                        cut = slice(b * HALF, (b + 1) * HALF)
                        dve.wait_ge(up_free, n.count(b + 1, 2))
                        tt(sq_h[:, b, :], relu_h[:, b, :], relu_h[:, b, :], ALU.mult).then_inc(sq_done, 1)
                        dve.wait_ge(sq_done, tile.count(b + 1, 2))
                        dve.wait_ge(sq_rounded, tile.count(b + 1, 2))
                        ins = tt(hid_lo[:, u, cut], sq_h[:, b, :], hid_hi[:, u, cut], ALU.subtract)
                    ins.then_inc(hid_ready, 1)
                add_down(Index(d0, i))

            turns = F_FF // P // 2
            with dve.Fori(0, turns - l) as i:
                turn(i, False)
            if l:
                turn(turns - 1, True)

        n0_round = {N_MLP0: 1, N_MLP1: 3}
        mlp(N_MLP0, Q_MLP0, D_MLP0, 0)
        norm(2, acc, gam, bet)

        dve.wait_ge(tab_iota, 1)
        step(ts(e01[:, 0, 0:SEQ], tab[:, :], -0.5 / SCALE, None, ALU.mult))
        step(stt(tab[:, :], tab[:, :], 0.5 / SCALE, e01[:, 0, 0:SEQ], ALU.mult, ALU.min))
        step(nc.vector.memset(tab[0:64, SEQ - 64:SEQ], NEG))
        pt_ps, o_ps = up_ps[0][:, 0:HALF], up_ps[0][:, HALF:SEQ]
        fill_ps, unit_ps = up_ps[1][:, 0:HALF], up_ps[1][:, HALF:SEQ]

        def half_out(n, H, c, b, parity):
            cut = slice(b * HALF, (b + 1) * HALF)
            if c < 2:
                hi, lo = (qs, ks)[c][parity]
                dve.wait_ge(qkv_rounded, H.count(2 * c + b + 1, 4))
                tt(lo[:, cut], fill_ps, hi[:, cut], ALU.subtract).then_inc(up_free, 1)
            else:
                dve.wait_ge(up_done, (n + c).count(b + 1, 2))
                nc.vector.tensor_copy(vT[:, cut], fill_ps).then_inc(up_free, 1)

        def biased(H, k):
            w = (ORDER[k] + 1) * P
            dve.wait_ge(s_done, H.count(k + 1, TT))
            nc.vector.memset(spare[:, :], 0.0)
            for m in range(2):
                last = nc.vector.tensor_tensor_reduce(e01[:, m, ebuf(ORDER[k])], dn_ps[m][:, 0:w], tab[:, SEQ - w:SEQ],
                                                      1.0, -3e38, ALU.add, ALU.max, cols[:, m:m + 1])
            last.then_inc(s_biased, 1)
            dve.wait_ge(s_biased, H.count(k + 1, TT))
            ts(cols[:, 2:4], cols[:, 0:2], -SCALE, None, ALU.mult).then_inc(negmax, 1)

        def combine(H, k, parity):
            s = ORDER[k]
            dve.wait_ge(e_done, H.count(k + 1, TT))
            nc.vector.reciprocal(inv0[:, parity, s:s + 1], cols[:, 4:5])
            step(nc.vector.reciprocal(cols[:, 6:7], cols[:, 5:6]))
            step(stt(cols[:, 7:8], cols[:, 4:5], lam[:, 3:4], cols[:, 6:7], ALU.mult, ALU.mult))
            stt(e01[:, 0, ebuf(s)], e01[:, 1, ebuf(s)], cols[:, 7:8], e01[:, 0, ebuf(s)], ALU.mult, ALU.add
                ).then_inc(attn_ready, 1)

        def group_lo(H, gr):
            dve.wait_ge(hid_rounded_att, H.count(gr + 1, 2))
            stt(hid_group(hid_lo, gr), group_ps(o_ps, gr), feat[:, ROW_SUB:ROW_SUB + 1], hid_group(hid_hi, gr),
                ALU.mult, ALU.subtract).then_inc(o_read, 1)

        def group_sums(H, gr, parity):
            at = 4 * gr
            dve.wait_ge(osum_done, H.count(gr + 1, 2))
            for lo in range(2):
                g2 = GROUP[gr][2 * lo]
                step(tt(ostat[:, 0, g2:g2 + 2], unit_ps[:, 2 * lo:2 * lo + 2], inv0[:, parity, g2:g2 + 2], ALU.mult))
                last = tt(ostat[:, 0, g2:g2 + 2], ostat[:, 0, g2:g2 + 2], inv0[:, parity, g2:g2 + 2], ALU.mult)
            last.then_inc(os_dve, 1)

        def factors(H, parity):
            dve.wait_ge(os_dve, H.count(2, 2))
            ts(ostat[:, 1, :], ostat[:, 0, :], 1.0 / P, EPS, ALU.mult, ALU.add).then_inc(os_ready, 1)
            dve.wait_ge(os_std, H.count(1))
            step(nc.vector.reciprocal(ostat[:, 1, :], ostat[:, 1, :]))
            step(stt(ostat[:, 2, :], ostat[:, 1, :], 1.0 - LAMBDA_INIT, inv0[:, parity, :], ALU.mult, ALU.mult))

        def units(H, at, to):
            for x in range(at, to):
                s, b = UNITS[x]
                cut = slice(b * HALF, (b + 1) * HALF)
                dve.wait_ge(du_done, H.count(x + 1, 2 * TT))
                if H.at:
                    dve.wait_ge(du_free, (H + -1).count(x + 1, 2 * TT))
                stt(acc[:, s, cut], unit_ps, ostat[:, 2, s:s + 1], acc[:, s, cut], ALU.mult, ALU.add
                    ).then_inc(du_free, 1)

        def split_att_strip(H):
            dve.wait_ge(wd_rounded, Index(Q_ATT + H.at, H.off).count(1))
            tt(wd_lo[:, 0], wd_raw[:, 0], wd_hi[:, 0], ALU.subtract).then_inc(wd_split, 1)

        def head(H, parity, n, down, more, filled):
            prev = H + -1
            for k in range(TT):
                if k == 0 and filled:
                    half_out(n + -3, H, 2, 1, parity)
                combine(H, k, parity)
                if k and more and k - 1 in UP_AT:
                    half_out(n, H + 1, *UP_AT[k - 1], 1 - parity)
                if k == 0:
                    dve.wait_ge(vt_rounded, H.count(1))
                    tt(v_lo[:, :, :], eight(up_ps[1]), v_hi[:, :, :], ALU.subtract).then_inc(v_ready, 1)
                if k < TT - 1:
                    biased(H, k + 1)
                elif more:
                    step(ts(tab[:, :], tab[:, :], 0.5, None, ALU.mult))
                    dve.wait_ge(pt_done, H.count(TT, TT))
                    biased(H + 1, 0)
                if k == 0 and down:
                    group_lo(prev, 1)
                if k == 4:
                    group_lo(H, 0)
                dve.wait_ge(pt_rounded, H.count(k + 1, TT))
                w = min(ORDER[k] + 1, 4)
                tt(pt_lo[:, 0:w, :], four(pt_ps)[:, 0:w, :], pt_hi[:, 0:w, :], ALU.subtract).then_inc(pt_ready, 1)
                if k == 0 and down:
                    group_sums(prev, 1, 1 - parity)
                    factors(prev, 1 - parity)
                    split_att_strip(prev)
                if k == 4:
                    group_sums(H, 0, parity)
                at, to = UNITS_AT[k] if down else (0, 0)
                units(prev, at, min(at + 1, to))
                if ORDER[k] >= 4:
                    dve.wait_ge(ptb_rounded, H.count(k // 2 + 1, 4))
                    w = ORDER[k] + 1
                    tt(pt_lo[:, 4:w, :], four(pt_ps)[:, 0:w - 4, :], pt_hi[:, 4:w, :], ALU.subtract
                       ).then_inc(ptb_ready, 1)
                units(prev, at + 1, to)
                if more and k in UP_AT and UP_AT[k][1] == 0:
                    split_up_weights(n + (UP_AT[k][0] + 1))

        for c in range(3):
            n = Index(N_ATT)
            split_up_weights(n + (c + 1))
            for b in range(2):
                half_out(n, Index(0), c, b, 0)
        biased(Index(0), 0)
        dve.wait_ge(acc_ready, 3 * TT)
        head(Index(0), 0, Index(N_ATT + 3), False, True, False)
        with step.loop(DIFF_H // 2 - 1, 46) as i:
            for u in range(2):
                head(Index(1 + u, i * 2), 1 - u, Index(N_ATT + 6 + 3 * u, i * 6, i * 3), True, True, True)
        last_head = Index(DIFF_H - 1)
        head(last_head, 1, Index(N_MLP1), True, False, True)
        group_lo(last_head, 1)
        group_sums(last_head, 1, 1)
        factors(last_head, 1)
        split_att_strip(last_head)
        units(last_head, 0, 2 * TT)
        norm(3, acc, gam, bet)
        mlp(N_MLP1, Q_MLP1, D_MLP1, 1)
        norm(4, acc, gam, bet)


_INS = ['x', 'even_w_in', 'even_conv_w', 'even_conv_b', 'even_dt_bias', 'even_a_log', 'even_d', 'even_ssd_norm_w',
        'even_sgu_ln_g', 'even_sgu_ln_b', 'even_sgu_w', 'even_sgu_b', 'even_w_out', 'odd_w_qkv', 'odd_lambda_q1',
        'odd_lambda_k1', 'odd_lambda_q2', 'odd_lambda_k2', 'odd_subln_w', 'odd_w_out', 'ln_mix_g', 'ln_mix_b',
        'ln_ffn_g', 'ln_ffn_b', 'mlp_w_up', 'mlp_w_down']


def kernel(**inputs):
    import numpy as np
    import concourse.bacc as bacc
    from concourse.bass_utils import run_bass_kernel_spmd

    nc = bacc.Bacc("TRN2", target_bir_lowering=False, num_devices=1)
    arrays, aps = {}, {}
    for name in _INS:
        a = np.ascontiguousarray(inputs[name])
        arrays[f"in_{name}"] = a
        aps[name] = nc.dram_tensor(f"in_{name}", a.shape, mybir.dt.from_np(a.dtype), kind="ExternalInput").ap()
    out = nc.dram_tensor("out", arrays["in_x"].shape, F32, kind="ExternalOutput").ap()
    build(nc, aps, out)
    result = run_bass_kernel_spmd(nc, [arrays], core_ids=[0])
    return result.results[0]["out"]
```

```python
import math
from contextlib import ExitStack, contextmanager

import concourse.bass as bass
from concourse import mybir

F32 = mybir.dt.float32
F32R = mybir.dt.float32r
ALU = mybir.AluOpType
ACT = mybir.ActivationFunctionType

P = 128
D = 1024
SEQ = 1024
KT = D // P
TT = SEQ // P
HALF = 512
F_FF = 4 * D
HEADS = 16
HPT = 2
GROUPS = 2
TPG = KT // GROUPS
CONV = 4
CHUNK = 64
QK = D
SGU_G = 8
DIFF_H = 8
ALPHA = 4.0 ** 0.25
EPS = 1e-5
LAMBDA_INIT = 0.8 - 0.6 * math.exp(-0.3)
SCALE = 64 ** -0.5
NEG = -1e30
SHARED = 46400 // 4 + TT * D

COL_Z, COL_X = 0, D
COL_B = 2 * D
COL_C = COL_B + GROUPS * P
COL_DT = COL_C + GROUPS * P
COL_U = COL_DT + HEADS
COL_V = COL_U + D

N_DT, N_SSD = 0, 1
SSD_TILES = 2 + 2 * TPG
N_SGU = N_SSD + GROUPS * SSD_TILES
N_MLP0 = N_SGU + SGU_G
N_ATT = N_MLP0 + F_FF // P
N_MLP1 = N_ATT + 3 * DIFF_H
N_END = N_MLP1 + F_FF // P
Q_SSD = 0
Q_V = Q_SSD + KT
Q_SGU = Q_V + KT
Q_MLP0 = Q_SGU + SGU_G
Q_ATT = Q_MLP0 + F_FF // P
Q_MLP1 = Q_ATT + DIFF_H
Q_END = Q_MLP1 + F_FF // P
D_SSD = 0
D_SGU = D_SSD + KT // 2
D_MLP0 = D_SGU + SGU_G // 2
D_MLP1 = D_MLP0 + F_FF // P // 2
D_END = D_MLP1 + F_FF // P // 2

H_SGU = KT
H_MLP0 = H_SGU + SGU_G
H_MLP1 = H_MLP0 + F_FF // P

ROW_CW, ROW_CB, ROW_NW, ROW_SUB = 0, CONV * 12, CONV * 12 + 12, CONV * 12 + 20
ROWS = ROW_SUB + 1
SMALL = 11
DA, ACS, DT, DECAY, CHUNKDECAY = range(5)

ORDER = [7, 0, 6, 1, 5, 2, 4, 3]
BLOCKS = TT + 1
GROUP = ((0, 1, 6, 7), (2, 3, 4, 5))
UP_AT = {0: (0, 0), 1: (0, 1), 2: (1, 0), 3: (1, 1), 5: (2, 0), 7: (2, 1)}
SPLIT_AT = {1: 1, 3: 2, 5: 3}
UNITS = [(s, b) for gr in GROUP for s in gr for b in range(2)]
UNITS_AT = {0: (0, 0), 1: (0, 3), 2: (3, 6), 3: (6, 8), 4: (8, 10), 5: (10, 12), 6: (12, 14), 7: (14, 16)}


class Chain:

    def __init__(self, eng, sem):
        self.eng, self.sem, self.k, self.off = eng, sem, 0, 0

    def __call__(self, ins):
        ins.then_inc(self.sem, 1)
        self.k += 1
        self.eng.wait_ge(self.sem, self.off + self.k)

    @contextmanager
    def loop(self, times, steps):
        with self.eng.Fori(0, times) as i:
            off, k = self.off, self.k
            if steps:
                self.off = self.off + i * steps
            yield i
            assert self.k - k == steps, (self.k - k, steps)
            self.off, self.k = off, k + steps * times


class Index:

    def __init__(self, at, off=0, half=0):
        self.at, self.off, self.half = at, off, half

    def __add__(self, k):
        return Index(self.at + k, self.off, self.half)

    def count(self, k, per=1):
        return self.off * per + (self.at * per + k)

    @property
    def slot(self):
        return self.at % 2

    def filled(self):
        return self.half * 16 + 16 * (self.at // 2 + 1)


def build(nc, t, out):
    with ExitStack() as ctx:
        program(nc, ctx, t, out)


def program(nc, ctx, t, out):
    def sb(name, shape, dt=F32, at=None):
        return (at or ctx).enter_context(nc.sbuf_tensor(name, shape, dt))

    def sem(name):
        return ctx.enter_context(nc.semaphore(name))

    act_hi = sb("act_hi", [P, KT, SEQ], F32R)
    act_lo = sb("act_lo", [P, KT, SEQ], F32R)
    at = ExitStack()
    ysq_sum = sb("ysq_sum", [P, GROUPS, SEQ], at=at)
    ysq_new = sb("ysq_new", [P, SEQ], at=at)
    at.close()
    hid_hi = sb("hid_hi", [P, 2, SEQ], F32R)
    hid_lo = sb("hid_lo", [P, 2, SEQ], F32R)
    wu_raw = sb("wu_raw", [P, 2, KT, P])
    wu_hi = sb("wu_hi", [P, 2, KT, P], F32R)
    wu_lo = sb("wu_lo", [P, 2, KT, P], F32R)
    wd_raw = sb("wd_raw", [P, 2, D])
    wd_hi = sb("wd_hi", [P, 2, D], F32R)
    wd_lo = sb("wd_lo", [P, 2, D], F32R)
    ident = sb("ident", [P, P])
    ones = sb("ones", [P, P])
    feat = sb("feat", [P, ROWS])
    skip = sb("skip", [P, KT])
    stats = sb("stats", [P, TT, 2, 6])
    moments = sb("moments", [P, TT, 4])
    rms = sb("rms", [P, GROUPS, TT])
    lam = sb("lam", [P, 8])
    cols = sb("cols", [P, 8])
    spare = sb("spare", [P, 1])
    inv0 = sb("inv0", [P, 2, TT])
    ostat = sb("ostat", [P, 3, TT])

    def share(*tensors, at=None):
        at = at or ctx
        return [sb(name, shape, dt, at) for name, shape, dt in tensors]

    at = ExitStack()
    big, = share(("big", [P, TT, D], F32), at=at)
    ssd_at = ExitStack()
    upper, negmask, par, parj, parf = share(
        ("upper", [P, P], F32),
        ("negmask", [P, P], F32),
        ("par", [P, TT, 5, HEADS], F32), ("parj", [P, TT, 5, HPT], F32), ("parf", [P, 8], F32), at=ssd_at)
    tmp_at = ExitStack()
    rows, d_rows, d_rep, dtT, dtb, sp, a_row, lrow = share(
        ("rows", [ROWS, P], F32), ("d_rows", [KT, 2], F32), ("d_rep", [KT, P], F32), ("dtT", [HEADS, SEQ], F32),
        ("dtb", [HEADS, 1], F32), ("sp", [P, 6, P], F32), ("a_row", [P, HEADS], F32), ("lrow", [P, 4, 64], F32),
        at=tmp_at)
    tmp_at.close()
    cT, b_tok, cb, cin, xsT, x_dt, x_dec, c_dec, mt, state = share(
        ("cT", [P, SEQ], F32), ("b_tok", [P, TT, P], F32), ("cb", [P, SEQ], F32), ("cin", [P, CONV - 1 + SEQ], F32),
        ("xsT", [P, SEQ], F32), ("x_dt", [P, TT, P], F32), ("x_dec", [P, TT, P], F32), ("c_dec", [P, SEQ], F32),
        ("mt", [P, SEQ], F32), ("state", [P, TT, P], F32), at=tmp_at)
    tmp_at.close()
    ssd_at.close()
    vgam, vbet = share(("vgam", [P, D], F32), ("vbet", [P, D], F32), at=tmp_at)
    tmp_at.close()
    u_t, wsT, _, v_g, ws, bs = share(
        ("u_t", [P, SEQ], F32), ("wsT", [P, P], F32), ("under_vbet", [P, D - P], F32), ("v_g", [P, TT, P], F32),
        ("ws", [P, P], F32), ("bs", [P, P], F32), at=tmp_at)
    tmp_at.close()
    at.close()
    relu_h, sq_h, gam, bet = share(("relu_h", [P, 2, HALF], F32), ("sq_h", [P, 2, HALF], F32),
                                   ("gam", [P, D], F32), ("bet", [P, D], F32), at=at)
    at.close()
    q_hi, q_lo, k_hi, k_lo, v_hi, v_lo, pt_hi, pt_lo = share(
        *[(f"{x}_{y}", [P, SEQ], F32R) for x in "qk" for y in ("hi", "lo")],
        *[(f"{x}_{y}", [P, TT, P], F32R) for x in ("v", "pt") for y in ("hi", "lo")], at=at)
    tab, e01 = share(("tab", [P, SEQ], F32), ("e01", [P, 2, BLOCKS * P], F32), at=at)
    at.close()
    sb("shared", [P, SHARED - TT * D])
    acc = sb("acc", [P, TT, D])
    qs = ((q_hi, q_lo), (hid_hi[:, 1, :], hid_lo[:, 1, :]))
    ks = ((k_hi, k_lo), (wd_hi[:, 1, :], wd_lo[:, 1, :]))
    vT = wd_raw[:, 1, :]
    osq = wd_raw[:, 1, 0:HALF]

    up_ps = [ctx.enter_context(nc.psum_tensor(f"up_ps{i}", [P, SEQ], F32)) for i in range(2)]
    dn_ps = [ctx.enter_context(nc.psum_tensor(f"dn_ps{i}", [P, SEQ], F32)) for i in range(2)]

    x_in = [sem(f"x_in{i}") for i in range(4)]
    small_in = sem("small_in")
    consts = sem("consts")
    acc_in = sem("acc_in")
    wu_in = [sem("wu_in0"), sem("wu_in1")]
    wu_rounded = sem("wu_rounded")
    wu_split = sem("wu_split")
    wd_in = [sem("wd_in0"), sem("wd_in1")]
    wd_rounded = sem("wd_rounded")
    wd_split = sem("wd_split")
    up_done = sem("up_done")
    up_free = sem("up_free")
    dn_done = sem("dn_done")
    dn_free = sem("dn_free")
    hid_rounded = sem("hid_rounded")
    hid_ready = sem("hid_ready")
    tr_done = sem("tr_done")
    tr_rounded = sem("tr_rounded")
    tr_split = sem("tr_split")
    acc_ready = sem("acc_ready")
    ln_in = sem("ln_in")
    stats_done = sem("stats_done")
    ln_var = sem("ln_var")
    ln_std = sem("ln_std")
    ln_scaled = sem("ln_scaled")
    ln_unit = sem("ln_unit")
    ln_done = sem("ln_done")
    dve_step = sem("dve_step")
    act_step = sem("act_step")
    par_t = sem("par_t")
    feat_ready = sem("feat_ready")
    feat_done = sem("feat_done")
    lam_act = sem("lam_act")
    sq_rounded = sem("sq_rounded")
    hid_rounded_att = sem("hid_rounded_att")
    dt_tok = sem("dt_tok")
    sp_dve = sem("sp_dve")
    sp_act = sem("sp_act")
    dec_mm = sem("dec_mm")
    par_ready = sem("par_ready")
    cin_ready = sem("cin_ready")
    conv_done = sem("conv_done")
    silu_done = sem("silu_done")
    bt_done = sem("bt_done")
    bt_evac = sem("bt_evac")
    y_read = sem("y_read")
    sq_done = sem("sq_done")
    parj_ready = sem("parj_ready")
    conv_step = sem("conv_step")
    xt_done = sem("xt_done")
    xd_ready = sem("xd_ready")
    st_done = sem("st_done")
    scan_done = sem("scan_done")
    cum_done = sem("cum_done")
    seg_done = sem("seg_done")
    cexp_done = sem("cexp_done")
    mexp_done = sem("mexp_done")
    mc_ready = sem("mc_ready")
    y_done = sem("y_done")
    yg_ready = sem("yg_ready")
    pool_step = sem("pool_step")
    ysq_used = sem("ysq_used")
    rms_var = sem("rms_var")
    rms_std = sem("rms_std")
    rms_ready = sem("rms_ready")
    v_done = sem("v_done")
    v_evac = sem("v_evac")
    v_piece = sem("v_piece")
    g_in = sem("g_in")
    vg_ready = sem("vg_ready")
    ws_t = sem("ws_t")
    ws_ready = sem("ws_ready")
    mix_done = sem("mix_done")
    uy_ready = sem("uy_ready")
    tab_iota = sem("tab_iota")
    lam_dve = sem("lam_dve")
    qkv_rounded = sem("qkv_rounded")
    vt_done = sem("vt_done")
    vt_rounded = sem("vt_rounded")
    v_ready = sem("v_ready")
    s_done = sem("s_done")
    ptb_done = sem("ptb_done")
    ptb_rounded = sem("ptb_rounded")
    ptb_ready = sem("ptb_ready")
    o_read = sem("o_read")
    du_done = sem("du_done")
    du_free = sem("du_free")
    s_biased = sem("s_biased")
    negmax = sem("negmax")
    e_done = sem("e_done")
    attn_ready = sem("attn_ready")
    pt_done = sem("pt_done")
    pt_rounded = sem("pt_rounded")
    pt_ready = sem("pt_ready")
    o_done = sem("o_done")
    osq_done = sem("osq_done")
    osum_done = sem("osum_done")
    os_dve = sem("os_dve")
    os_ready = sem("os_ready")
    os_std = sem("os_std")
    out_sent = sem("out_sent")

    w_in, w_out0 = t["even_w_in"][0], t["even_w_out"][0]
    w_qkv, w_out1 = t["odd_w_qkv"][0], t["odd_w_out"][0]
    x_tok = t["x"][0].rearrange("(t p) d -> p t d", p=P)
    out_tok = out[0].rearrange("(t p) d -> p t d", p=P)

    def halves(x):
        return x.rearrange("p (b n) -> p b n", b=2)

    def eight(ps):
        return ps[:, :].rearrange("p (k n) -> p k n", k=KT)

    def mlp_load(eng, load, l, n0):
        with eng.Fori(0, F_FF // P // 2) as i:
            for u in range(2):
                load(Index(n0 + u, i * 2, i), t["mlp_w_up"][l], (i * 2 + u) * P)

    def mlp_strips(eng, strip, l, q0):
        with eng.Fori(0, F_FF // P // 2 - 1) as i:
            for u in range(2):
                strip(Index(q0 + 2 + u, i * 2, i), t["mlp_w_down"][l], i * 2 * P + (2 + u) * P)

    def ln_load(eng, number, gname, bname, l):
        eng.wait_ge(ln_done, TT * number)
        eng.dma_start(gam[:, :], t[gname][l].partition_broadcast(P)).then_inc(ln_in, 16)
        eng.dma_start(bet[:, :], t[bname][l].partition_broadcast(P)).then_inc(ln_in, 16)

    def ln_order(number):
        return [s for gr in GROUP for s in gr] if number == 3 else list(range(TT))

    def wait_piece(eng, p):
        if p % 4 == 3:
            eng.wait_ge(v_done, TT * (p // 4 + 1))
        else:
            eng.wait_ge(v_piece, p // 4 * 3 + p % 4 + 1)

    def ebuf(s):
        w = (s + 1) * P
        return slice(0, w) if s >= 4 else slice(BLOCKS * P - w, BLOCKS * P)

    def four(ps):
        return ps.rearrange("p (k n) -> p k n", k=4)

    def hid_group(hid, gr):
        pairs = hid[:, 0, :].rearrange("p (a n) -> p a n", n=2 * P)
        return pairs[:, 0:4:3, :] if gr == 0 else pairs[:, 1:3, :]

    def group_ps(ps, gr):
        return ps.rearrange("p (a n) -> p a n", n=2 * P)

    block = ctx.enter_context(nc.Block())

    @block.sync
    def _(sp_):
        def load(n, w, col):
            if n.at >= 2:
                sp_.wait_ge(wu_split, n.count(-1))
            sp_.dma_start(wu_raw[:, n.slot], w.rearrange("(k p) n -> p k n", p=P)[:, :, bass.ds(col, P)]
                          ).then_inc(wu_in[n.slot], 16)

        for i in range(4):
            sp_.dma_start(big[:, 2 * i:2 * i + 2, :], x_tok[:, 2 * i:2 * i + 2, :]).then_inc(x_in[i], 16)
        load(Index(N_DT), w_in, COL_DT)
        for g in range(GROUPS):
            n = N_SSD + g * SSD_TILES
            load(Index(n), w_in, COL_B + g * P)
            load(Index(n + 1), w_in, COL_C + g * P)
            with sp_.Fori(0, TPG) as j:
                load(Index(n + 2, j * 2, j), w_in, (j + g * TPG) * P + COL_X)
                load(Index(n + 3, j * 2, j), w_in, j * HPT * (P // HPT) + (COL_Z + g * TPG * P))
        with sp_.Fori(0, SGU_G // 2) as i:
            for u in range(2):
                load(Index(N_SGU + u, i * 2, i), w_in, (i * 2 + u) * P + COL_U)
        mlp_load(sp_, load, 0, N_MLP0)
        with sp_.Fori(0, DIFF_H // 2) as i:
            for u in range(2):
                for c in range(3):
                    load(Index(N_ATT + 3 * u + c, i * 6, i * 3), w_qkv, (i * 2 + (u + c * QK // P)) * P)
        mlp_load(sp_, load, 1, N_MLP1)
        for s in range(TT):
            sp_.wait_ge(ln_done, TT * 4 + s + 1)
            sp_.dma_start(out_tok[:, s, :], acc[:, s, :]).then_inc(out_sent, 16)
        sp_.wait_ge(out_sent, 16 * TT)

    @block.gpsimd
    def _(pool):
        def strip(q, w, row):
            if q.at >= 2:
                pool.wait_ge(wd_split, q.count(-1))
            pool.dma_start(wd_raw[:, q.slot], w[bass.ds(row, P), :]).then_inc(wd_in[q.slot], 16)

        small = [
            (rows[ROW_CW:ROW_CB], t["even_conv_w"][0].rearrange("k (t p) -> (k t) p", p=P)),
            (rows[ROW_CB:ROW_NW], t["even_conv_b"][0].rearrange("(t p) -> t p", p=P)),
            (rows[ROW_NW:ROW_SUB], t["even_ssd_norm_w"][0].rearrange("(t p) -> t p", p=P)),
            (rows[ROW_SUB:ROWS], t["odd_subln_w"]),
            (d_rows[:, :], t["even_d"][0].rearrange("(j h) -> j h", h=HPT)),
            (dtb[:, :], t["even_dt_bias"][0].rearrange("(h o) -> h o", o=1)),
            (a_row[:, :], t["even_a_log"][0].partition_broadcast(P)),
        ] + [(lrow[:, i, :], t[name][0].partition_broadcast(P)) for i, name in
             enumerate(("odd_lambda_q1", "odd_lambda_k1", "odd_lambda_q2", "odd_lambda_k2"))]
        assert len(small) == SMALL
        for dst, src in small:
            pool.dma_start(dst, src).then_inc(small_in, 16)
        nc.gpsimd.memset(ident[:, :], 0.0).then_inc(consts, 1)
        nc.gpsimd.memset(upper[:, :], 1.0).then_inc(consts, 1)
        nc.gpsimd.memset(negmask[:, :], 0.0).then_inc(consts, 1)
        nc.gpsimd.memset(ones[:, :], 1.0).then_inc(consts, 1)
        pool.wait_ge(consts, 4)
        nc.gpsimd.affine_select(out=ident[:, :], in_=ident[:, :], compare_op=ALU.not_equal, fill=1.0, base=0,
                                pattern=[[-1, P]], channel_multiplier=1).then_inc(consts, 1)
        for m, fill in ((upper, 0.0), (negmask, NEG)):
            nc.gpsimd.affine_select(out=m[:, :], in_=m[:, :], compare_op=ALU.is_ge, fill=fill, base=0,
                                    pattern=[[1, P]], channel_multiplier=-1).then_inc(consts, 1)

        for j in range(2):
            strip(Index(Q_SSD + j), w_out0, j * P)
        sq_step = Chain(pool, pool_step)
        sq_step(nc.gpsimd.memset(ysq_sum[:, :, :], 0.0))
        for g in range(GROUPS):
            with sq_step.loop(TPG, 2) as j:
                pool.wait_ge(yg_ready, Index(g * TPG, j).count(1))
                y = big[:, bass.ds(j + g * TPG, 1), :].squeeze(1)
                sq_step(nc.gpsimd.tensor_tensor(ysq_new[:, :], y, y, ALU.mult))
                sq_step(nc.gpsimd.tensor_tensor(ysq_sum[:, g, :], ysq_sum[:, g, :], ysq_new[:, :], ALU.add))
        pool.wait_ge(rms_ready, 1)
        pool.dma_start(acc[:, :, :], x_tok).then_inc(acc_in, 16)
        pool.dma_start(vgam[:, :], t["even_sgu_ln_g"][0].partition_broadcast(P)).then_inc(ln_in, 16)
        pool.dma_start(vbet[:, :], t["even_sgu_ln_b"][0].partition_broadcast(P)).then_inc(ln_in, 16)
        for j in range(2, KT):
            strip(Index(Q_SSD + j), w_out0, j * P)
        for b in range(2):
            for kp in range(KT // 2):
                q = Q_V + b * (KT // 2) + kp
                pool.wait_ge(wd_split, q - 1)
                pool.dma_start(halves(wd_raw[:, q % 2]),
                               w_in[2 * kp * P:2 * (kp + 1) * P, COL_V + b * HALF:COL_V + (b + 1) * HALF]
                               .rearrange("(k p) n -> p k n", p=P)).then_inc(wd_in[q % 2], 16)
        with pool.Fori(0, SGU_G // 2) as i:
            for u in range(2):
                g = i * 2 + u
                pool.dma_start(ws[:, :], t["even_sgu_w"][0].rearrange("g t s -> (g t) s")[bass.ds(g * P, P), :]
                               ).then_inc(g_in, 16)
                pool.dma_start(bs[0:1, :], t["even_sgu_b"][0][bass.ds(g, 1), :]).then_inc(g_in, 16)
                strip(Index(Q_SGU + u, i * 2, i), w_out0, i * 2 * P + (D + u * P))
                for b in range(2):
                    pool.wait_ge(ln_done, TT // 2 * (b + 1))
                    nc.gpsimd.tensor_copy(v_g[:, 4 * b:4 * b + 4, :], big[:, 4 * b:4 * b + 4, bass.ds(g * P, P)]
                                          ).then_inc(vg_ready, 1)
                pool.wait_ge(mix_done, g + 1)
        def norm(number):
            for x, s in enumerate(ln_order(number)):
                pool.wait_ge(ln_unit, TT * (number - 1) + x + 1)
                nc.gpsimd.tensor_tensor(acc[:, s, :], acc[:, s, :], bet[:, :], ALU.add).then_inc(ln_done, 1)

        def first_strips(l, q0):
            for u in range(2):
                strip(Index(q0 + u), t["mlp_w_down"][l], u * P)

        ln_load(pool, 1, "ln_mix_g", "ln_mix_b", 0)
        first_strips(0, Q_MLP0)
        norm(1)
        mlp_strips(pool, strip, 0, Q_MLP0)
        nc.gpsimd.iota(tab[:, :], pattern=[[-1, SEQ]], base=SEQ - P, channel_multiplier=1,
                       allow_small_or_imprecise_dtypes=True).then_inc(tab_iota, 1)
        ln_load(pool, 2, "ln_ffn_g", "ln_ffn_b", 0)
        norm(2)

        def att_strip(q, row):
            pool.wait_ge(wd_split, q.count(0))
            pool.dma_start(wd_raw[:, 0], w_out1[bass.ds(row, P), :]).then_inc(wd_in[q.slot], 16)

        with pool.Fori(0, DIFF_H // 2) as i:
            for u in range(2):
                att_strip(Index(Q_ATT + u, i * 2, i), i * 2 * P + u * P)
        pool.wait_ge(du_done, 2 * TT * DIFF_H)
        pool.wait_ge(wd_split, Q_MLP1)
        ln_load(pool, 3, "ln_mix_g", "ln_mix_b", 1)
        first_strips(1, Q_MLP1)
        norm(3)
        mlp_strips(pool, strip, 1, Q_MLP1)
        ln_load(pool, 4, "ln_ffn_g", "ln_ffn_b", 1)
        norm(4)

    @block.tensor
    def _(pe):
        mm = nc.tensor.matmul

        def three(ps, hi, lo, mhi, mlo, start, stop):
            mm(ps, hi, mhi, start=start, stop=False)
            mm(ps, hi, mlo, start=False, stop=False)
            return mm(ps, lo, mhi, start=False, stop=stop)

        def up(n):
            pe.wait_ge(wu_split, n.count(1))
            for b in range(2):
                if n.at >= 2:
                    pe.wait_ge(up_free, n.count(b - 3, 2))
                for k in range(KT):
                    cut = slice(b * HALF, (b + 1) * HALF)
                    last = three(up_ps[n.slot][:, cut], wu_hi[:, n.slot, k, :], wu_lo[:, n.slot, k, :],
                                 act_hi[:, k, cut], act_lo[:, k, cut], k == 0, k == KT - 1)
                last.then_inc(up_done, 1)

        def down(d, width, q, h):
            pe.wait_ge(wd_split, q.count(width))
            for s in range(TT):
                if 8 * d.at + s >= 2:
                    pe.wait_ge(dn_free, d.count(s - 1, TT))
                for c in range(width):
                    if s == 0:
                        pe.wait_ge(hid_ready, h.count(c + 1))
                    w, row, tok = (q + c).slot, (c if width == 2 else q.slot), slice(s * P, (s + 1) * P)
                    for st, mv in ((hid_hi, wd_hi), (hid_hi, wd_lo), (hid_lo, wd_hi)):
                        for b in range(2):
                            cut = slice(b * HALF, (b + 1) * HALF)
                            last = mm(dn_ps[s % 2][:, cut], st[:, row, tok], mv[:, w, cut],
                                      start=(c == 0 and (st, mv) == (hid_hi, wd_hi)),
                                      stop=(c == width - 1 and st is hid_lo))
                last.then_inc(dn_done, 1)

        def transposes(src, number):
            for x, s in enumerate(ln_order(number)):
                if x >= 2:
                    pe.wait_ge(tr_split, TT * number + x - 1)
                if number == 0:
                    pe.wait_ge(x_in[s // 2], 16)
                else:
                    pe.wait_ge(ln_done, TT * number + x + 1)
                for k in range(KT):
                    last = nc.tensor.transpose(up_ps[x % 2][:, k * P:(k + 1) * P], src[:, s, k * P:(k + 1) * P],
                                               ident[:, :])
                last.then_inc(tr_done, 1)
            pe.wait_ge(tr_split, TT * (number + 1))

        pe.wait_ge(consts, 7)
        transposes(big, 0)

        pe.wait_ge(small_in, 16 * SMALL)
        nc.tensor.transpose(dn_ps[0][:, 0:ROWS], rows[:, :], ident[0:ROWS, 0:ROWS])
        pe.wait_ge(feat_ready, 1)
        nc.tensor.transpose(dn_ps[0][:, HALF:HALF + KT], d_rep[:, :], ident[0:KT, 0:KT]).then_inc(par_t, 1)
        up(Index(N_DT))
        pe.wait_ge(up_free, 2)
        for c in range(TT):
            last = nc.tensor.transpose(dn_ps[1][:, c * HEADS:(c + 1) * HEADS], dtT[:, c * P:(c + 1) * P],
                                       ident[0:HEADS, 0:HEADS])
        last.then_inc(dt_tok, 1)
        pe.wait_ge(par_ready, 1)
        pe.wait_ge(feat_done, 1)
        for i, m in enumerate((upper, ones)):
            last = mm(dn_ps[0][:, i * P:(i + 1) * P].rearrange("p (c h) -> p c h", c=TT), m[:, :], par[:, :, DA, :],
                      start=True, stop=True, skip_group_check=True)
        last.then_inc(dec_mm, 1)

        def feature_tile(g, j, more):
            J = Index(g * TPG, j)
            xn = Index(N_SSD + g * SSD_TILES + 2, j * 2, j)

            def running_sums(head, ps):
                for c in range(TT):
                    last = mm(ps[:, c * P:(c + 1) * P], parj[:, c, DA, head:head + 1].broadcast_to([P, P]),
                              upper[:, :], start=True, stop=True, skip_group_check=True)
                last.then_inc(cum_done, 1)

            pe.wait_ge(parj_ready, J.count(1))
            pe.wait_ge(y_read, 5 * g + 1)
            running_sums(0, dn_ps[1])
            pe.wait_ge(y_read, J.count(g + 1))
            up(xn + 1)
            pe.wait_ge(bt_evac, g + 1)
            pe.wait_ge(silu_done, J.count(3 + 2 * g))
            for c in range(TT):
                last = nc.tensor.transpose(dn_ps[0][:, c * P:(c + 1) * P], xsT[:, c * P:(c + 1) * P], ident[:, :])
            last.then_inc(xt_done, 1)
            pe.wait_ge(xd_ready, J.count(1, 2))
            for c in range(TT):
                last = mm(up_ps[1][:, c * P:(c + 1) * P], b_tok[:, c, :], x_dec[:, c, :], start=True, stop=True,
                          skip_group_check=True)
            last.then_inc(st_done, 1)
            pe.wait_ge(xd_ready, J.count(2, 2))
            running_sums(1, dn_ps[0])
            pe.wait_ge(scan_done, J.count(1))
            pe.wait_ge(up_free, (xn + 1).count(2, 2))
            for head in range(HPT):
                if head and more:
                    up(xn + 2)
                pe.wait_ge(mc_ready, J.count(head + 1, HPT))
                hs = slice(head * 64, (head + 1) * 64)
                for c in range(TT):
                    cut = slice(c * P, (c + 1) * P)
                    if c:
                        mm(up_ps[0][hs, cut], state[:, c, hs], c_dec[:, cut], start=True, stop=False,
                           skip_group_check=True)
                    last = mm(up_ps[0][hs, cut], x_dt[:, c, hs], mt[:, cut], start=(c == 0), stop=True,
                              skip_group_check=True)
                last.then_inc(y_done, 1)

        up(Index(N_SSD))
        for g in range(GROUPS):
            n = N_SSD + g * SSD_TILES
            if g:
                pe.wait_ge(y_read, 5 * g)
            up(Index(n + 1))
            pe.wait_ge(silu_done, 6 * g + 1)
            if g == 0:
                pe.wait_ge(par_ready, 2)
            for c in range(TT):
                nc.tensor.transpose(dn_ps[0][:, c * P:(c + 1) * P], xsT[:, c * P:(c + 1) * P], ident[:, :])
            pe.wait_ge(silu_done, 6 * g + 2)
            for c in range(TT):
                cut = slice(c * P, (c + 1) * P)
                last = mm(dn_ps[1][:, cut], xsT[:, cut], cT[:, cut], start=True, stop=True, skip_group_check=True)
            last.then_inc(bt_done, 1)
            up(Index(n + 2))
            turns = TPG - g
            with pe.Fori(0, turns) as j:
                feature_tile(g, j, True)
            if g:
                feature_tile(g, turns, False)
        for g in range(GROUPS):
            pe.wait_ge(pool_step, 1 + 2 * TPG * (g + 1))
            for s in range(TT):
                last = mm(dn_ps[0][:, g * TT + s:g * TT + s + 1], ysq_sum[:, g, s * P:(s + 1) * P], ones[:, 0:1],
                          start=True, stop=True, skip_group_check=True)
        last.then_inc(ysq_used, 1)
        pe.wait_ge(rms_ready, 1)
        for m in range(KT // 2):
            down(Index(D_SSD + m), 2, Index(Q_SSD + 2 * m), Index(2 * m))

        pe.wait_ge(dn_free, TT * D_SGU)
        for b in range(2):
            for kp in range(KT // 2):
                q = Q_V + b * (KT // 2) + kp
                pe.wait_ge(wd_split, q + 1)
                for kk in range(2):
                    k = 2 * kp + kk
                    cut = slice(kk * HALF, (kk + 1) * HALF)
                    for s in range(TT):
                        if b and k == 0:
                            pe.wait_ge(v_evac, s + 1)
                        tok = slice(s * P, (s + 1) * P)
                        ps = (up_ps, dn_ps)[s // 4][s % 4 // 2][:, (s % 2) * HALF:(s % 2 + 1) * HALF]
                        last = three(ps, act_hi[:, k, tok], act_lo[:, k, tok], wd_hi[:, q % 2, cut],
                                     wd_lo[:, q % 2, cut], k == 0, k == KT - 1)
                        if k == KT - 1:
                            last.then_inc(v_done, 1)
                if k < KT - 1:
                    last.then_inc(v_piece, 1)
        pe.wait_ge(v_evac, 2 * TT)
        for u in range(2):
            up(Index(N_SGU + u))

        def sgu(i, more):
            for u in range(2):
                g = Index(u, i * 2)
                pe.wait_ge(g_in, g.count(32, 32))
                if u:
                    pe.wait_ge(uy_ready, g.count(0))
                else:
                    pe.wait_ge(dn_free, Index(D_SGU, i).count(0, TT))
                nc.tensor.transpose(dn_ps[0][:, 0:P], ws[:, :], ident[:, :]).then_inc(ws_t, 1)
                for b in range(2):
                    mm(dn_ps[1][:, b * HALF:(b + 1) * HALF].rearrange("p (c t) -> p c t", t=P), ones[0:1, :],
                       bs[0:1, :].unsqueeze(1).broadcast_to([1, HALF // P, P]), start=True, stop=False,
                       skip_group_check=True)
                pe.wait_ge(ws_ready, g.count(1))
                pe.wait_ge(vg_ready, g.count(2, 2))
                for b in range(TT):
                    last = mm(dn_ps[1][:, b * P:(b + 1) * P], v_g[:, b, :], wsT[:, :], start=False, stop=True,
                              skip_group_check=True)
                last.then_inc(mix_done, 1)
                if more:
                    up(Index(N_SGU + 2 + u, i * 2, i))
            down(Index(D_SGU, i), 2, Index(Q_SGU, i * 2, i), Index(H_SGU, i * 2))

        with pe.Fori(0, SGU_G // 2 - 1) as i:
            sgu(i, True)
        sgu(SGU_G // 2 - 1, False)

        def mlp(n0, q0, d0, h0):
            with pe.Fori(0, F_FF // P // 2) as i:
                for u in range(2):
                    up(Index(n0 + u, i * 2, i))
                down(Index(d0, i), 2, Index(q0, i * 2, i), Index(h0, i * 2))

        transposes(acc, 1)
        mlp(N_MLP0, Q_MLP0, D_MLP0, H_MLP0)
        transposes(acc, 2)

        pt_ps, o_ps = up_ps[0][:, 0:HALF], up_ps[0][:, HALF:SEQ]
        fill_ps, unit_ps = up_ps[1][:, 0:HALF], up_ps[1][:, HALF:SEQ]

        def up_half(n, b, fill_ps=fill_ps, ahead=0):
            if b == 0:
                pe.wait_ge(wu_split, n.count(1))
            pe.wait_ge(up_free, n.count(b - ahead, 2))
            for k in range(KT):
                last = three(fill_ps, wu_hi[:, n.slot, k, :], wu_lo[:, n.slot, k, :],
                             act_hi[:, k, b * HALF:(b + 1) * HALF], act_lo[:, k, b * HALF:(b + 1) * HALF],
                             k == 0, k == KT - 1)
            last.then_inc(up_done, 1)

        def scores(parity, k):
            s = ORDER[k]
            width = (s + 1) * P
            (qh, ql), (kh, kl) = qs[parity], ks[parity]
            for m in range(2):
                d = slice(m * 64, (m + 1) * 64)
                for at in range(0, width, HALF):
                    cut = slice(at, min(at + HALF, width))
                    last = three(dn_ps[m][:, cut], qh[d, s * P:(s + 1) * P], ql[d, s * P:(s + 1) * P],
                                 kh[d, cut], kl[d, cut], True, True)
            last.then_inc(s_done, 1)

        def units(H, at, to):
            for x in range(at, to):
                s, b = UNITS[x]
                pe.wait_ge(du_free, H.count(x, 2 * TT)) if H.at or x else None
                for st, mv in ((hid_hi, wd_hi), (hid_hi, wd_lo), (hid_lo, wd_hi)):
                    last = mm(unit_ps, st[:, 0, s * P:(s + 1) * P], mv[:, 0, b * HALF:(b + 1) * HALF],
                              start=(mv is wd_hi and st is hid_hi), stop=(st is hid_lo))
                last.then_inc(du_done, 1)

        def sums_of_squares(H, gr):
            pe.wait_ge(osq_done, H.count(gr + 1, 2))
            for c in range(4):
                last = mm(unit_ps[:, c:c + 1], osq[:, c * P:(c + 1) * P], ones[:, 0:1], start=True, stop=True,
                          skip_group_check=True)
            last.then_inc(osum_done, 1)

        def head(H, parity, n, down, more):
            prev = H + -1
            for k in range(TT):
                s = ORDER[k]
                K = k
                if k < TT - 1 or more:
                    pe.wait_ge(s_biased, H.count(K + 1, TT))
                    if k == TT - 1:
                        pe.wait_ge(up_free, n.count(4, 2))
                        scores(1 - parity, 0)
                    else:
                        scores(parity, k + 1)
                if k == 0:
                    pe.wait_ge(up_free, n.count(0, 2))
                    pe.wait_ge(attn_ready, H.count(1, TT))
                    for c in range(TT):
                        last = nc.tensor.transpose(up_ps[1][:, c * P:(c + 1) * P], vT[:, c * P:(c + 1) * P],
                                                   ident[:, :])
                        if c % 4 == 3:
                            last.then_inc(vt_done, 1)
                pe.wait_ge(attn_ready, H.count(K + 1, TT))
                e = e01[:, 0, ebuf(s)]
                for c in range(min(s + 1, 4)):
                    last = nc.tensor.transpose(pt_ps[:, c * P:(c + 1) * P], e[:, c * P:(c + 1) * P], ident[:, :])
                last.then_inc(pt_done, 1)
                at, to = UNITS_AT[k] if down else (0, 0)
                if k == 0:
                    pe.wait_ge(v_ready, H.count(1, 2))
                if k == 5:
                    if down:
                        pe.wait_ge(du_free, prev.count(at, 2 * TT))
                    sums_of_squares(H, 0)
                if k not in (0, 1, 5):
                    units(prev, at, min(at + 1, to))
                if more and k in UP_AT:
                    c, b = UP_AT[k]
                    up_half(n + c, b)
                if k == 0:
                    pe.wait_ge(v_ready, H.count(2, 2))
                    if down:
                        sums_of_squares(prev, 1)
                if down and k in (1, 5):
                    if k == 1:
                        pe.wait_ge(os_dve, prev.count(2, 2))
                        pe.wait_ge(o_read, prev.count(2, 2))
                        pe.wait_ge(wd_split, H.count(Q_ATT))
                    else:
                        pe.wait_ge(os_dve, H.count(1, 2))
                    units(prev, at, min(at + 1, to))
                if s >= 4:
                    pe.wait_ge(pt_ready, H.count(K + 1, TT))
                    for c in range(4, s + 1):
                        last = nc.tensor.transpose(pt_ps[:, (c - 4) * P:(c - 3) * P], e[:, c * P:(c + 1) * P],
                                                   ident[:, :])
                    last.then_inc(ptb_done, 1)
                units(prev, at + 1, min(at + 2, to))
                if s < 4:
                    pe.wait_ge(pt_ready, H.count(K + 1, TT))
                if k == 4:
                    pe.wait_ge(o_read, H.count(1, 2))
                if k == 0 and down:
                    pe.wait_ge(o_read, prev.count(2, 2))
                col = GROUP[k // 4].index(s) * P
                for c in range(s + 1):
                    if c == 4:
                        pe.wait_ge(ptb_ready, H.count(k // 2 + 1, 4))
                    last = three(o_ps[:, col:col + P], v_hi[:, c, :], v_lo[:, c, :], pt_hi[:, c, :], pt_lo[:, c, :],
                                 c == 0, c == s)
                if k % 4 == 3:
                    last.then_inc(o_done, 1)
                units(prev, at + 2, to)

        for c in range(3):
            for b in range(2):
                up_half(Index(N_ATT + c), b, (fill_ps, unit_ps)[b], 1)
        pe.wait_ge(up_free, 2 * N_ATT + 4)
        scores(0, 0)
        head(Index(0), 0, Index(N_ATT + 3), False, True)
        with pe.Fori(0, DIFF_H // 2 - 1) as i:
            for u in range(2):
                head(Index(1 + u, i * 2), 1 - u, Index(N_ATT + 6 + 3 * u, i * 6, i * 3), True, True)
        head(Index(DIFF_H - 1), 1, Index(N_MLP1), True, False)
        last_head = Index(DIFF_H - 1)
        pe.wait_ge(du_free, last_head.count(0, 2 * TT))
        sums_of_squares(last_head, 1)
        pe.wait_ge(os_dve, last_head.count(2, 2))
        pe.wait_ge(wd_split, Q_MLP1)
        units(last_head, 0, 2 * TT)
        transposes(acc, 3)
        mlp(N_MLP1, Q_MLP1, D_MLP1, H_MLP1)

    @block.scalar
    def _(act):
        fn = nc.scalar.activation

        def round_up_weights(n):
            act.wait_ge(wu_in[n.slot], n.filled())
            if n.at >= 2:
                act.wait_ge(up_done, n.count(-2, 2))
            fn(wu_hi[:, n.slot], wu_raw[:, n.slot], ACT.Copy).then_inc(wu_rounded, 1)

        def round_strip(q):
            act.wait_ge(wd_in[q.slot], q.filled())
            fn(wd_hi[:, q.slot], wd_raw[:, q.slot], ACT.Copy).then_inc(wd_rounded, 1)

        def round_act(number, x):
            act.wait_ge(tr_done, TT * number + x + 1)
            s = ln_order(number)[x]
            fn(act_hi[:, :, s * P:(s + 1) * P], eight(up_ps[x % 2]), ACT.Copy).then_inc(tr_rounded, 1)

        def deviation(number, x):
            act.wait_ge(ln_var, TT * number + x + 1)
            m = moments[:, ln_order(number)[x], 2:3]
            fn(m, m, ACT.Sqrt).then_inc(ln_std, 1)

        round_up_weights(Index(N_DT))
        for s in range(TT):
            round_act(0, s)
        act.wait_ge(par_t, 1)
        act.wait_ge(lam_dve, 1)
        fn(lam[:, 0:2], lam[:, 0:2], ACT.Exp).then_inc(lam_act, 1)
        fn(feat[:, :], dn_ps[0][:, 0:ROWS], ACT.Copy)
        fn(skip[:, :], dn_ps[0][:, HALF:HALF + KT], ACT.Copy).then_inc(feat_done, 1)
        round_up_weights(Index(N_DT + 1))
        for b in range(2):
            act.wait_ge(up_done, b + 1)
            fn(dtT[:, b * HALF:(b + 1) * HALF], up_ps[0][0:HEADS, b * HALF:(b + 1) * HALF], ACT.Identity,
               bias=dtb[:, 0:1]).then_inc(up_free, 1)
        act.wait_ge(dt_tok, 1)
        fn(sp[:, 0, :], dn_ps[1][:, 0:P], ACT.Abs).then_inc(act_step, 1)
        act.wait_ge(act_step, 1)
        fn(sp[:, 1, :], sp[:, 0, :], ACT.Exp, scale=-1.0).then_inc(sp_act, 1)
        fn(a_row[:, :], a_row[:, :], ACT.Exp).then_inc(sp_act, 1)
        act.wait_ge(sp_dve, 1)
        fn(sp[:, 3, :], sp[:, 2, :], ACT.Ln).then_inc(sp_act, 1)
        act.wait_ge(sp_dve, 2)
        fn(par[:, :, DECAY, :], par[:, :, DECAY, :], ACT.Exp).then_inc(sp_act, 1)
        fn(par[:, :, CHUNKDECAY, :], par[:, :, CHUNKDECAY, :], ACT.Exp).then_inc(sp_act, 1)

        def conv_in(n, conv):
            for b in range(2):
                act.wait_ge(up_done, n.count(b + 1, 2))
                if b == 0 and conv.at >= 1:
                    act.wait_ge(conv_done, conv.count(0))
                fn(cin[:, CONV - 1 + b * HALF:CONV - 1 + (b + 1) * HALF], up_ps[n.slot][:, b * HALF:(b + 1) * HALF],
                   ACT.Copy).then_inc(up_free, 1)

        def silu_conv(conv, x):
            act.wait_ge(conv_done, conv.count(1))
            fn(x, x, ACT.Silu).then_inc(silu_done, 1)

        act.wait_ge(par_ready, 2)
        for g in range(GROUPS):
            n = N_SSD + g * SSD_TILES
            if g == 0:
                round_up_weights(Index(n + 1))
            conv_in(Index(n), Index(6 * g))
            round_up_weights(Index(n + 2))
            silu_conv(Index(6 * g), xsT[:, :])
            conv_in(Index(n + 1), Index(6 * g + 1))
            round_up_weights(Index(n + 3))
            silu_conv(Index(6 * g + 1), cT[:, :])
            act.wait_ge(bt_done, g + 1)
            fn(b_tok[:, :, :], eight(dn_ps[0]), ACT.Copy).then_inc(bt_evac, 1)

            def feature_tile(j, more):
                J = Index(g * TPG, j)
                xn = Index(n + 2, j * 2, j)
                conv = Index(6 * g + 2, j)
                conv_in(xn, conv)
                silu_conv(conv, xsT[:, :])
                round_up_weights(xn + 2)
                for b in range(2):
                    act.wait_ge(up_done, (xn + 1).count(b + 1, 2))
                    fn(big[:, bass.ds(j + g * TPG, 1), b * HALF:(b + 1) * HALF],
                       up_ps[0][:, b * HALF:(b + 1) * HALF].unsqueeze(1), ACT.Silu).then_inc(up_free, 1)
                for head in range(HPT):
                    act.wait_ge(cum_done, J.count(head + 1, HPT))
                    if head:
                        act.wait_ge(y_done, J.count(1, HPT))
                    else:
                        act.wait_ge(y_read, J.count(g + 1))
                    act.wait_ge(seg_done, J.count(head + 1, HPT))
                    fn(mt[:, :], mt[:, :], ACT.Exp).then_inc(mexp_done, 1)
                    fn(c_dec[:, :], dn_ps[1 - head][:, :], ACT.Exp).then_inc(cexp_done, 1)
                if more:
                    round_up_weights(xn + 3)

            turns = TPG - g
            with act.Fori(0, turns) as j:
                feature_tile(j, True)
            if g:
                feature_tile(turns, False)
        act.wait_ge(rms_var, 1)
        fn(rms[:, :, :], rms[:, :, :], ACT.Sqrt).then_inc(rms_std, 1)
        for c in range(2):
            round_strip(Index(Q_SSD + c))
        for m in range(KT // 2):
            if m:
                act.wait_ge(dn_done, TT * (D_SSD + m))
            for c in range(2):
                j = 2 * m + c
                if m:
                    round_strip(Index(Q_SSD + j))
                fn(hid_hi[:, c, :], big[:, j, :], ACT.Copy, scale=feat[:, ROW_NW + j:ROW_NW + j + 1]
                   ).then_inc(hid_rounded, 1)
            if m == 0:
                act.wait_ge(acc_in, 16)
                for s in range(TT):
                    fn(acc[:, s, :], acc[:, s, :], ACT.Copy, scale=ALPHA).then_inc(acc_ready, 1)

        def v_out(b):
            for s in range(TT):
                act.wait_ge(v_done, b * TT + s + 1)
                ps = (up_ps, dn_ps)[s // 4][s % 4 // 2][:, (s % 2) * HALF:(s % 2 + 1) * HALF]
                fn(big[:, s, b * HALF:(b + 1) * HALF], ps, ACT.Gelu).then_inc(v_evac, 1)

        for p in range(KT):
            if p < 2:
                act.wait_ge(dn_done, TT * D_SGU)
            else:
                wait_piece(act, p - 2)
            if p == KT // 2 + 1:
                v_out(0)
            round_strip(Index(Q_V + p))
        round_up_weights(Index(N_SGU + 1))
        v_out(1)
        for s in range(TT):
            deviation(0, s)
        act.wait_ge(ln_done, TT)

        def sgu(i, more):
            for u in range(2):
                n = Index(N_SGU + u, i * 2, i)
                h = Index(KT + u, i * 2)
                if more or u == 0:
                    round_up_weights(n + 2)
                act.wait_ge(dn_done, Index(D_SGU, i).count(0, TT))
                round_strip(Index(Q_SGU + u, i * 2, i))
                act.wait_ge(hid_ready, h.count(0))
                for b in range(2):
                    act.wait_ge(up_done, n.count(b + 1, 2))
                    fn(u_t[:, b * HALF:(b + 1) * HALF], up_ps[n.slot][:, b * HALF:(b + 1) * HALF], ACT.Gelu
                       ).then_inc(up_free, 1)
                act.wait_ge(uy_ready, Index(u, i * 2).count(1))
                fn(hid_hi[:, u, :], u_t[:, :], ACT.Copy).then_inc(hid_rounded, 1)

        with act.Fori(0, SGU_G // 2 - 1) as i:
            sgu(i, True)
        sgu(SGU_G // 2 - 1, False)

        def mlp(n0, q0, d0, h0, l):
            def turn(i, last):
                for u in range(2):
                    n = Index(n0 + u, i * 2, i)
                    h = Index(h0 + u, i * 2)
                    tile = Index(l * (F_FF // P) + u, i * 2)
                    if not (last and u):
                        round_up_weights(n + 1)
                    act.wait_ge(dn_done, Index(d0, i).count(0, TT))
                    round_strip(Index(q0 + u, i * 2, i))
                    act.wait_ge(hid_ready, h.count(0))
                    for b in range(2):
                        cut = slice(b * HALF, (b + 1) * HALF)
                        act.wait_ge(up_done, n.count(b + 1, 2))
                        fn(relu_h[:, b, :], up_ps[n.slot][:, cut], ACT.Relu).then_inc(up_free, 1)
                        act.wait_ge(up_free, n.count(b + 1, 2))
                        fn(hid_hi[:, u, cut], relu_h[:, b, :], ACT.Square).then_inc(sq_rounded, 1)

            turns = F_FF // P // 2
            with act.Fori(0, turns - l) as i:
                turn(i, False)
            if l:
                turn(turns - 1, True)

        def norm(number):
            for x in range(2):
                deviation(number, x)
            order = ln_order(number)
            lag = 2 if number == 3 else 5
            for x, s in enumerate(order):
                if x + 2 < TT:
                    deviation(number, x + 2)
                act.wait_ge(ln_scaled, TT * (number - 1) + x + 1)
                fn(acc[:, s, :], acc[:, s, :], ACT.Copy, scale=moments[:, s, 3:4]).then_inc(ln_unit, 1)
                if x >= lag and number < 4:
                    round_act(number, x - lag)
            if number < 4:
                for x in range(TT - lag, TT):
                    round_act(number, x)
                for s in order:
                    fn(acc[:, s, :], acc[:, s, :], ACT.Copy, scale=ALPHA).then_inc(acc_ready, 1)

        norm(1)
        mlp(N_MLP0, Q_MLP0, D_MLP0, H_MLP0, 0)
        norm(2)

        pt_ps, o_ps = up_ps[0][:, 0:HALF], up_ps[0][:, HALF:SEQ]
        fill_ps = up_ps[1][:, 0:HALF]

        def half_out(n, c, b, parity, fill_ps=fill_ps):
            if c < 2:
                act.wait_ge(up_done, (n + c).count(b + 1, 2))
                fn((qs, ks)[c][parity][0][:, b * HALF:(b + 1) * HALF], fill_ps, ACT.Copy).then_inc(qkv_rounded, 1)

        def weights(H, k, parity):
            act.wait_ge(negmax, H.count(k + 1, TT))
            for m in range(2):
                e = e01[:, m, ebuf(ORDER[k])]
                last = fn(e, e, ACT.Exp, bias=cols[:, 2 + m:3 + m], scale=SCALE, accum_out=cols[:, 4 + m:5 + m])
            last.then_inc(e_done, 1)

        def group_out(H, gr):
            act.wait_ge(o_done, H.count(gr + 1, 2))
            fn(osq, o_ps, ACT.Square).then_inc(osq_done, 1)
            fn(hid_group(hid_hi, gr), group_ps(o_ps, gr), ACT.Copy, scale=feat[:, ROW_SUB:ROW_SUB + 1]
               ).then_inc(hid_rounded_att, 1)

        def deviations(H):
            act.wait_ge(os_ready, H.count(1))
            fn(ostat[:, 1, :], ostat[:, 1, :], ACT.Sqrt).then_inc(os_std, 1)

        def head(H, parity, n, down, more):
            prev = H + -1
            for k in range(TT):
                w = ORDER[k] + 1

                def last_blocks():
                    if w > 4:
                        act.wait_ge(ptb_done, H.count(k // 2 + 1, 4))
                        fn(pt_hi[:, 4:w, :], four(pt_ps)[:, 0:w - 4, :], ACT.Copy).then_inc(ptb_rounded, 1)

                if k and more and k - 1 in UP_AT:
                    half_out(n, *UP_AT[k - 1], 1 - parity)
                if k == 0:
                    for b in range(2):
                        act.wait_ge(vt_done, H.count(b + 1, 2))
                        fn(v_hi[:, 4 * b:4 * b + 4, :], four(up_ps[1][:, b * HALF:(b + 1) * HALF]), ACT.Copy
                           ).then_inc(vt_rounded, 1)
                act.wait_ge(pt_done, H.count(k + 1, TT))
                fn(pt_hi[:, 0:min(w, 4), :], four(pt_ps)[:, 0:min(w, 4), :], ACT.Copy).then_inc(pt_rounded, 1)
                if k == 0 and down:
                    group_out(prev, 1)
                if k == 4:
                    group_out(H, 0)
                if k not in UP_AT:
                    last_blocks()
                if k < TT - 1:
                    weights(H, k + 1, parity)
                elif more:
                    weights(H + 1, 0, 1 - parity)
                if k in UP_AT:
                    last_blocks()
                if k == 0 and down:
                    if prev.at:
                        act.wait_ge(du_done, prev.count(0, 2 * TT))
                    round_att_strip(prev)
                if k == 1 and down:
                    deviations(prev)
                if more and k in SPLIT_AT:
                    round_up_weights(n + SPLIT_AT[k])

        def round_att_strip(H):
            q = Index(Q_ATT + H.at, H.off, H.half)
            act.wait_ge(wd_in[q.slot], q.filled())
            fn(wd_hi[:, 0], wd_raw[:, 0], ACT.Copy).then_inc(wd_rounded, 1)

        for c in range(3):
            n = Index(N_ATT)
            round_up_weights(n + (c + 1))
            for b in range(2):
                half_out(n, c, b, 0, up_ps[1][:, b * HALF:(b + 1) * HALF])
        weights(Index(0), 0, 0)
        head(Index(0), 0, Index(N_ATT + 3), False, True)
        with act.Fori(0, DIFF_H // 2 - 1) as i:
            for u in range(2):
                head(Index(1 + u, i * 2, i), 1 - u, Index(N_ATT + 6 + 3 * u, i * 6, i * 3), True, True)
        last_head = Index(DIFF_H - 1)
        head(last_head, 1, Index(N_MLP1), True, False)
        group_out(last_head, 1)
        deviations(last_head)
        act.wait_ge(du_done, last_head.count(0, 2 * TT))
        round_att_strip(last_head)
        norm(3)
        mlp(N_MLP1, Q_MLP1, D_MLP1, H_MLP1, 1)
        norm(4)

    @block.vector
    def _(dve):
        ts, tt, stt = nc.vector.tensor_scalar, nc.vector.tensor_tensor, nc.vector.scalar_tensor_tensor
        step = Chain(dve, dve_step)

        def split_up_weights(n):
            dve.wait_ge(wu_rounded, n.count(1))
            tt(wu_lo[:, n.slot], wu_raw[:, n.slot], wu_hi[:, n.slot], ALU.subtract).then_inc(wu_split, 1)

        def split_strip(q):
            dve.wait_ge(wd_rounded, q.count(1))
            tt(wd_lo[:, q.slot], wd_raw[:, q.slot], wd_hi[:, q.slot], ALU.subtract).then_inc(wd_split, 1)

        def split_act(number, x):
            dve.wait_ge(tr_rounded, TT * number + x + 1)
            s = ln_order(number)[x]
            cut = slice(s * P, (s + 1) * P)
            tt(act_lo[:, :, cut], eight(up_ps[x % 2]), act_hi[:, :, cut], ALU.subtract).then_inc(tr_split, 1)

        def half_stats(s, b, src):
            nc.vector.bn_stats(stats[:, s, b, :], src[:, s, b * HALF:(b + 1) * HALF]).then_inc(stats_done, 1)

        def variance(number, x, src, first=0):
            s = ln_order(number)[x]
            m = moments[:, s]
            for b in range(first, 2):
                half_stats(s, b, src)
            dve.wait_ge(stats_done, 2 * (TT * number + x + 1) if number else TT + x + 1)
            step(nc.vector.bn_aggr(m[:, 0:2], stats[:, s].rearrange("p b c -> p (b c)")))
            ts(m[:, 2:3], m[:, 1:2], EPS, None, ALU.add).then_inc(ln_var, 1)

        def scaled(number, x, src, gain, bias):
            s = ln_order(number)[x]
            m = moments[:, s]
            if x == 0:
                dve.wait_ge(ln_in, 32 * (number + 1))
            dve.wait_ge(ln_std, TT * number + x + 1)
            nc.vector.reciprocal(m[:, 3:4], m[:, 2:3])
            ins = stt(src[:, s, :], src[:, s, :], m[:, 0:1], gain[:, :], ALU.subtract, ALU.mult)
            if number:
                ins.then_inc(ln_scaled, 1)
            else:
                step(ins)
                stt(src[:, s, :], src[:, s, :], m[:, 3:4], bias[:, :], ALU.mult, ALU.add).then_inc(ln_done, 1)

        def add_down(d, scale=None, norm=None):
            for s in range(TT):
                dve.wait_ge(dn_done, d.count(s + 1, TT))
                if d.at:
                    dve.wait_ge(dn_free, d.count(s - TT + 1, TT))
                if scale is None:
                    ins = tt(acc[:, s, :], dn_ps[s % 2][:, :], acc[:, s, :], ALU.add)
                else:
                    ins = stt(acc[:, s, :], dn_ps[s % 2][:, :], scale(s), acc[:, s, :], ALU.mult, ALU.add)
                ins.then_inc(dn_free, 1)
                if norm and s:
                    dve.wait_ge(dn_free, d.count(s, TT))
                    variance(norm, s - 1, acc)
                    if s >= 3:
                        scaled(norm, s - 3, acc, gam, bet)
            if norm:
                dve.wait_ge(dn_free, d.count(TT, TT))
                variance(norm, TT - 1, acc)

        def norm(number, src, gain, bias, first=0):
            for x in range(first, TT):
                scaled(number, x, src, gain, bias)
                if x > 2 and not first and number:
                    split_act(number, x - 3)
            if 0 < number < 4:
                for x in range(0 if first else TT - 3, TT):
                    split_act(number, x)

        dve.wait_ge(small_in, 16 * SMALL)
        for i in range(2):
            last = nc.vector.tensor_tensor_reduce(lrow[:, 2 * i, :], lrow[:, 2 * i, :], lrow[:, 2 * i + 1, :], 1.0, 0.0,
                                                  ALU.mult, ALU.add, lam[:, i:i + 1])
        last.then_inc(lam_dve, 1)
        nc.vector.tensor_copy(d_rep[:, :].rearrange("j (h p) -> j h p", h=HPT),
                              d_rows[:, :].unsqueeze(2).broadcast_to([KT, HPT, 64])).then_inc(feat_ready, 1)
        split_up_weights(Index(N_DT))
        for s in range(TT):
            split_act(0, s)
        dve.wait_ge(lam_act, 1)
        step(tt(lam[:, 2:3], lam[:, 0:1], lam[:, 1:2], ALU.subtract))
        step(ts(lam[:, 3:4], lam[:, 2:3], LAMBDA_INIT, -1.0, ALU.add, ALU.mult))
        split_up_weights(Index(N_DT + 1))
        e, one_e, ln_e, rest, none = (sp[:, i, :] for i in (1, 2, 3, 4, 5))
        dve.wait_ge(sp_act, 1)
        ts(one_e, e, 1.0, None, ALU.add).then_inc(sp_dve, 1)
        dve.wait_ge(sp_dve, 1)
        step(ts(rest, one_e, -1.0, None, ALU.add))
        step(ts(none, rest, 0.0, None, ALU.is_equal))
        step(tt(rest, rest, none, ALU.add))
        step(nc.vector.reciprocal(rest, rest))
        step(tt(rest, rest, e, ALU.mult))
        dve.wait_ge(sp_act, 3)
        step(tt(ln_e, ln_e, rest, ALU.mult))
        step(tt(none, none, e, ALU.mult))
        step(tt(ln_e, ln_e, none, ALU.add))

        def ch(x):
            return x.rearrange("p (c h) -> p c h", h=HEADS)

        step(stt(par[:, :, DT, :], ch(dn_ps[1][:, 0:P]), 0.0, ch(ln_e), ALU.max, ALU.add))
        stt(par[:, :, DA, :], par[:, :, DT, :], -1.0, a_row[:, :].unsqueeze(1).broadcast_to([P, TT, HEADS]),
            ALU.mult, ALU.mult).then_inc(par_ready, 1)
        dve.wait_ge(dec_mm, 1)
        step(nc.vector.tensor_copy(par[:, :, ACS, :], ch(dn_ps[0][:, 0:P])))
        tt(par[:, :, DECAY, :], ch(dn_ps[0][:, P:2 * P]), par[:, :, ACS, :], ALU.subtract)
        nc.vector.tensor_copy(par[:, :, CHUNKDECAY, :], ch(dn_ps[0][:, P:2 * P])).then_inc(sp_dve, 1)
        dve.wait_ge(sp_act, 5)
        tt(par[:, :, DECAY, :], par[:, :, DECAY, :], par[:, :, DT, :], ALU.mult).then_inc(par_ready, 1)

        def feature_params(tile):
            step(nc.vector.tensor_copy(parf[:, 0:CONV + 1], feat[:, 0:ROW_NW].rearrange("p (k f) -> p k f", f=12)
                                       [:, :, bass.ds(tile, 1)].squeeze(2)))

        def conv(n, x):
            dve.wait_ge(up_free, n.count(2, 2))
            step(ts(x, cin[:, 0:SEQ], parf[:, 0:1], parf[:, CONV:CONV + 1], ALU.mult, ALU.add))
            for k in range(1, CONV):
                ins = stt(x, cin[:, k:k + SEQ], parf[:, k:k + 1], x, ALU.mult, ALU.add)
                step(ins) if k < CONV - 1 else ins.then_inc(conv_done, 1)

        def decay_products(J, head):
            dve.wait_ge(mexp_done, J.count(head + 1, HPT))
            tt(mt[:, :], mt[:, :], cb[:, :], ALU.mult)
            dve.wait_ge(cexp_done, J.count(head + 1, HPT))
            tt(c_dec[:, :], c_dec[:, :], cT[:, :], ALU.mult).then_inc(mc_ready, 1)

        def tile_heads(first):
            nc.vector.tensor_copy(parj[:, :, :, :], par[:, :, :, bass.ds(first, HPT)]).then_inc(parj_ready, 1)

        dve.wait_ge(par_ready, 2)
        tile_heads(0)
        step(nc.vector.memset(cin[:, 0:CONV - 1], 0.0))
        for g in range(GROUPS):
            n = N_SSD + g * SSD_TILES
            if g == 0:
                split_up_weights(Index(n + 1))
            feature_params(KT + g)
            conv(Index(n), xsT[:, :])
            split_up_weights(Index(n + 2))
            dve.wait_ge(conv_done, 6 * g + 1)
            feature_params(KT + GROUPS + g)
            conv(Index(n + 1), cT[:, :])
            split_up_weights(Index(n + 3))
            dve.wait_ge(bt_done, g + 1)
            nc.vector.tensor_copy(cb[:, :], dn_ps[1][:, :]).then_inc(y_read, 1)
            def feature_tile(j, more):
                J = Index(g * TPG, j)
                xn = Index(n + 2, j * 2, j)
                step(nc.vector.tensor_copy(parf[:, 5:6], skip[:, bass.ds(j + g * TPG, 1)]))
                feature_params(j + g * TPG)
                conv(xn, xsT[:, :])
                split_up_weights(xn + 2)
                dve.wait_ge(parj_ready, J.count(1))
                for head in range(HPT):
                    dve.wait_ge(cum_done, J.count(head + 1, HPT))
                    if head:
                        dve.wait_ge(y_done, J.count(1, HPT))
                    for c in range(TT):
                        cut = slice(c * P, (c + 1) * P)
                        last = stt(mt[:, cut], dn_ps[1 - head][:, cut], parj[:, c, ACS, head:head + 1], negmask[:, :],
                                   ALU.subtract, ALU.add)
                    last.then_inc(seg_done, 1)
                    if head == 0:
                        dve.wait_ge(xt_done, J.count(1))
                        for x, kind in ((x_dec, DECAY), (x_dt, DT)):
                            tt(x[:, :, :].rearrange("p c (h e) -> p c h e", h=HPT),
                               dn_ps[0][:, :].rearrange("p (c h e) -> p c h e", c=TT, h=HPT),
                               parj[:, :, kind, :].unsqueeze(3).broadcast_to([P, TT, HPT, 64]), ALU.mult
                               ).then_inc(xd_ready, 1)
                        decay_products(J, 0)
                        dve.wait_ge(st_done, J.count(1))
                        step(nc.vector.tensor_copy(state[:, 1, :], up_ps[1][:, 0:P]))
                        for c in range(2, TT):
                            for hh in range(HPT):
                                hs = slice(hh * 64, (hh + 1) * 64)
                                ins = stt(state[:, c, hs], state[:, c - 1, hs],
                                          parj[:, c - 1, CHUNKDECAY, hh:hh + 1],
                                          up_ps[1][:, (c - 1) * P + hh * 64:(c - 1) * P + (hh + 1) * 64],
                                          ALU.mult, ALU.add)
                            step(ins) if c < TT - 1 else ins.then_inc(scan_done, 1)
                    else:
                        decay_products(J, 1)
                if more:
                    tile_heads(j * HPT + (g * TPG + 1) * HPT)
                    split_up_weights(xn + 3)
                dve.wait_ge(y_done, J.count(HPT, HPT))
                stt(xsT[:, :], xsT[:, :], parf[:, 5:6], up_ps[0][:, :], ALU.mult, ALU.add).then_inc(y_read, 1)
                dve.wait_ge(y_read, J.count(g + 2))
                dve.wait_ge(up_free, (xn + 1).count(2, 2))
                y = big[:, bass.ds(j + g * TPG, 1), :].squeeze(1)
                tt(y, y, xsT[:, :], ALU.mult).then_inc(yg_ready, 1)

            turns = TPG - g
            with step.loop(turns, 11) as j:
                feature_tile(j, True)
            if g:
                feature_tile(turns, False)
        dve.wait_ge(ysq_used, 1)
        ts(rms[:, :, :].rearrange("p g s -> p (g s)"), dn_ps[0][:, 0:GROUPS * TT], 1.0 / (TPG * P), EPS,
           ALU.mult, ALU.add).then_inc(rms_var, 1)
        dve.wait_ge(rms_std, 1)
        nc.vector.reciprocal(rms[:, :, :], rms[:, :, :]).then_inc(rms_ready, 1)
        dve.wait_ge(rms_ready, 1)
        for m in range(KT // 2):
            for c in range(2):
                j = 2 * m + c
                split_strip(Index(Q_SSD + j))
                dve.wait_ge(hid_rounded, j + 1)
                stt(hid_lo[:, c, :], big[:, j, :], feat[:, ROW_NW + j:ROW_NW + j + 1], hid_hi[:, c, :],
                    ALU.mult, ALU.subtract).then_inc(hid_ready, 1)
            if m == 0:
                dve.wait_ge(acc_ready, TT)
            add_down(Index(D_SSD + m), lambda s: rms[:, m // 2, s:s + 1])

        for p in range(KT):
            split_strip(Index(Q_V + p))
            if p > KT // 2:
                for s in range((p - 5) * 3, min((p - 4) * 3, TT)):
                    dve.wait_ge(v_evac, s + 1)
                    half_stats(s, 0, big)
        split_up_weights(Index(N_SGU + 1))
        for s in range(TT):
            dve.wait_ge(v_evac, TT + s + 1)
            variance(0, s, big, 1)
        norm(0, big, vgam, vbet)
        dve.wait_ge(ln_done, TT)
        step(nc.vector.memset(wsT[64:P, 0:64], 0.0))

        def sgu(i, norm):
            for u in range(2):
                n = Index(N_SGU + u, i * 2, i)
                g = Index(u, i * 2)
                if norm is None or u == 0:
                    split_up_weights(n + 2)
                split_strip(Index(Q_SGU + u, i * 2, i))
                dve.wait_ge(ws_t, g.count(1))
                nc.vector.tensor_copy(wsT[0:64, :], dn_ps[0][0:64, 0:P])
                nc.vector.tensor_copy(wsT[64:P, 64:P], dn_ps[0][64:P, 64:P]).then_inc(ws_ready, 1)
                dve.wait_ge(up_free, n.count(2, 2))
                dve.wait_ge(mix_done, g.count(1))
                tt(u_t[:, :], u_t[:, :], dn_ps[1][:, :], ALU.mult).then_inc(uy_ready, 1)
                dve.wait_ge(hid_rounded, Index(KT + u, i * 2).count(1))
                tt(hid_lo[:, u, :], u_t[:, :], hid_hi[:, u, :], ALU.subtract).then_inc(hid_ready, 1)
            add_down(Index(D_SGU, i), norm=norm)

        with dve.Fori(0, SGU_G // 2 - 1) as i:
            sgu(i, None)
        sgu(SGU_G // 2 - 1, 1)
        norm(1, acc, gam, bet, TT - 3)

        def mlp(n0, q0, d0, l):
            dve.wait_ge(acc_ready, TT * (1 + n0_round[n0]))

            def turn(i, last=False):
                for u in range(2):
                    n = Index(n0 + u, i * 2, i)
                    tile = Index(l * (F_FF // P) + u, i * 2)
                    if not (last and u and l):
                        split_up_weights(n + 1)
                    split_strip(Index(q0 + u, i * 2, i))
                    for b in range(2):
                        cut = slice(b * HALF, (b + 1) * HALF)
                        dve.wait_ge(up_free, n.count(b + 1, 2))
                        tt(sq_h[:, b, :], relu_h[:, b, :], relu_h[:, b, :], ALU.mult).then_inc(sq_done, 1)
                        dve.wait_ge(sq_done, tile.count(b + 1, 2))
                        dve.wait_ge(sq_rounded, tile.count(b + 1, 2))
                        ins = tt(hid_lo[:, u, cut], sq_h[:, b, :], hid_hi[:, u, cut], ALU.subtract)
                    ins.then_inc(hid_ready, 1)
                add_down(Index(d0, i), norm=2 + 2 * l if last else None)

            turns = F_FF // P // 2
            with dve.Fori(0, turns - 1) as i:
                turn(i)
            turn(turns - 1, last=True)

        n0_round = {N_MLP0: 1, N_MLP1: 3}
        mlp(N_MLP0, Q_MLP0, D_MLP0, 0)
        norm(2, acc, gam, bet, TT - 3)

        dve.wait_ge(tab_iota, 1)
        step(ts(e01[:, 0, 0:SEQ], tab[:, :], -0.5 / SCALE, None, ALU.mult))
        step(stt(tab[:, :], tab[:, :], 0.5 / SCALE, e01[:, 0, 0:SEQ], ALU.mult, ALU.min))
        step(nc.vector.memset(tab[0:64, SEQ - 64:SEQ], NEG))
        pt_ps, o_ps = up_ps[0][:, 0:HALF], up_ps[0][:, HALF:SEQ]
        fill_ps, unit_ps = up_ps[1][:, 0:HALF], up_ps[1][:, HALF:SEQ]

        def half_out(n, H, c, b, parity, fill_ps=fill_ps):
            cut = slice(b * HALF, (b + 1) * HALF)
            if c < 2:
                hi, lo = (qs, ks)[c][parity]
                dve.wait_ge(qkv_rounded, H.count(2 * c + b + 1, 4))
                tt(lo[:, cut], fill_ps, hi[:, cut], ALU.subtract).then_inc(up_free, 1)
            else:
                dve.wait_ge(up_done, (n + c).count(b + 1, 2))
                nc.vector.tensor_copy(vT[:, cut], fill_ps).then_inc(up_free, 1)

        def biased(H, k):
            w = (ORDER[k] + 1) * P
            dve.wait_ge(s_done, H.count(k + 1, TT))
            nc.vector.memset(spare[:, :], 0.0)
            for m in range(2):
                last = nc.vector.tensor_tensor_reduce(e01[:, m, ebuf(ORDER[k])], dn_ps[m][:, 0:w], tab[:, SEQ - w:SEQ],
                                                      1.0, -3e38, ALU.add, ALU.max, cols[:, m:m + 1])
            last.then_inc(s_biased, 1)
            dve.wait_ge(s_biased, H.count(k + 1, TT))
            ts(cols[:, 2:4], cols[:, 0:2], -SCALE, None, ALU.mult).then_inc(negmax, 1)

        def combine(H, k, parity):
            s = ORDER[k]
            dve.wait_ge(e_done, H.count(k + 1, TT))
            nc.vector.reciprocal(inv0[:, parity, s:s + 1], cols[:, 4:5])
            step(nc.vector.reciprocal(cols[:, 6:7], cols[:, 5:6]))
            step(stt(cols[:, 7:8], cols[:, 4:5], lam[:, 3:4], cols[:, 6:7], ALU.mult, ALU.mult))
            stt(e01[:, 0, ebuf(s)], e01[:, 1, ebuf(s)], cols[:, 7:8], e01[:, 0, ebuf(s)], ALU.mult, ALU.add
                ).then_inc(attn_ready, 1)

        def group_lo(H, gr):
            dve.wait_ge(hid_rounded_att, H.count(gr + 1, 2))
            stt(hid_group(hid_lo, gr), group_ps(o_ps, gr), feat[:, ROW_SUB:ROW_SUB + 1], hid_group(hid_hi, gr),
                ALU.mult, ALU.subtract).then_inc(o_read, 1)

        def group_sums(H, gr, parity):
            at = 4 * gr
            dve.wait_ge(osum_done, H.count(gr + 1, 2))
            for lo in range(2):
                g2 = GROUP[gr][2 * lo]
                step(tt(ostat[:, 0, g2:g2 + 2], unit_ps[:, 2 * lo:2 * lo + 2], inv0[:, parity, g2:g2 + 2], ALU.mult))
                last = tt(ostat[:, 0, g2:g2 + 2], ostat[:, 0, g2:g2 + 2], inv0[:, parity, g2:g2 + 2], ALU.mult)
            last.then_inc(os_dve, 1)

        def factors(H, parity):
            dve.wait_ge(os_dve, H.count(2, 2))
            ts(ostat[:, 1, :], ostat[:, 0, :], 1.0 / P, EPS, ALU.mult, ALU.add).then_inc(os_ready, 1)
            dve.wait_ge(os_std, H.count(1))
            step(nc.vector.reciprocal(ostat[:, 1, :], ostat[:, 1, :]))
            step(stt(ostat[:, 2, :], ostat[:, 1, :], 1.0 - LAMBDA_INIT, inv0[:, parity, :], ALU.mult, ALU.mult))

        def units(H, at, to):
            for x in range(at, to):
                s, b = UNITS[x]
                cut = slice(b * HALF, (b + 1) * HALF)
                dve.wait_ge(du_done, H.count(x + 1, 2 * TT))
                if H.at:
                    dve.wait_ge(du_free, (H + -1).count(x + 1, 2 * TT))
                stt(acc[:, s, cut], unit_ps, ostat[:, 2, s:s + 1], acc[:, s, cut], ALU.mult, ALU.add
                    ).then_inc(du_free, 1)

        def split_att_strip(H):
            dve.wait_ge(wd_rounded, Index(Q_ATT + H.at, H.off).count(1))
            tt(wd_lo[:, 0], wd_raw[:, 0], wd_hi[:, 0], ALU.subtract).then_inc(wd_split, 1)

        def head(H, parity, n, down, more):
            prev = H + -1
            for k in range(TT):
                w = ORDER[k] + 1

                def first_blocks():
                    dve.wait_ge(pt_rounded, H.count(k + 1, TT))
                    tt(pt_lo[:, 0:min(w, 4), :], four(pt_ps)[:, 0:min(w, 4), :], pt_hi[:, 0:min(w, 4), :], ALU.subtract
                       ).then_inc(pt_ready, 1)

                if k and more and k - 1 in UP_AT:
                    half_out(n, H + 1, *UP_AT[k - 1], 1 - parity)
                if k == 0:
                    for b in range(2):
                        dve.wait_ge(vt_rounded, H.count(b + 1, 2))
                        tt(v_lo[:, 4 * b:4 * b + 4, :], four(up_ps[1][:, b * HALF:(b + 1) * HALF]),
                           v_hi[:, 4 * b:4 * b + 4, :], ALU.subtract).then_inc(v_ready, 1)
                at, to = UNITS_AT[k] if down else (0, 0)

                def last_blocks():
                    dve.wait_ge(ptb_rounded, H.count(k // 2 + 1, 4))
                    tt(pt_lo[:, 4:w, :], four(pt_ps)[:, 0:w - 4, :], pt_hi[:, 4:w, :], ALU.subtract
                       ).then_inc(ptb_ready, 1)

                if k % 2 == 0:
                    first_blocks()
                if k not in UP_AT:
                    units(prev, at, min(at + 1, to))
                    last_blocks()
                if k == 4:
                    group_lo(H, 0)
                if k < TT - 1:
                    biased(H, k + 1)
                elif more:
                    step(ts(tab[:, :], tab[:, :], 0.5, None, ALU.mult))
                    dve.wait_ge(pt_done, H.count(TT, TT))
                    biased(H + 1, 0)
                if k % 2:
                    first_blocks()
                if k == 0 and down:
                    group_lo(prev, 1)
                if k == 1 and down:
                    group_sums(prev, 1, 1 - parity)
                    factors(prev, 1 - parity)
                if k == 5:
                    group_sums(H, 0, parity)
                if k in UP_AT:
                    units(prev, at, min(at + 1, to))
                    if k == TT - 1 and more:
                        half_out(n, H + 1, *UP_AT[k], 1 - parity)
                    if w > 4:
                        last_blocks()
                units(prev, at + 1, min(at + 2, to))
                if k < TT - 1:
                    combine(H, k + 1, parity)
                elif more:
                    combine(H + 1, 0, 1 - parity)
                units(prev, at + 2, to)
                if k == 0 and down:
                    split_att_strip(prev)
                if more and k in SPLIT_AT:
                    split_up_weights(n + SPLIT_AT[k])

        for c in range(3):
            n = Index(N_ATT)
            split_up_weights(n + (c + 1))
            for b in range(2):
                half_out(n, Index(0), c, b, 0, (fill_ps, unit_ps)[b])
        biased(Index(0), 0)
        combine(Index(0), 0, 0)
        dve.wait_ge(acc_ready, 3 * TT)
        head(Index(0), 0, Index(N_ATT + 3), False, True)
        with step.loop(DIFF_H // 2 - 1, 46) as i:
            for u in range(2):
                head(Index(1 + u, i * 2), 1 - u, Index(N_ATT + 6 + 3 * u, i * 6, i * 3), True, True)
        last_head = Index(DIFF_H - 1)
        head(last_head, 1, Index(N_MLP1), True, False)
        group_lo(last_head, 1)
        group_sums(last_head, 1, 1)
        factors(last_head, 1)
        split_att_strip(last_head)
        for x in range(TT):
            units(last_head, 2 * x, 2 * x + 2)
            if x:
                dve.wait_ge(du_free, last_head.count(2 * x, 2 * TT))
                variance(3, x - 1, acc)
        dve.wait_ge(du_free, 2 * TT * DIFF_H)
        variance(3, TT - 1, acc)
        norm(3, acc, gam, bet)
        mlp(N_MLP1, Q_MLP1, D_MLP1, 1)
        norm(4, acc, gam, bet, TT - 3)


_INS = ['x', 'even_w_in', 'even_conv_w', 'even_conv_b', 'even_dt_bias', 'even_a_log', 'even_d', 'even_ssd_norm_w',
        'even_sgu_ln_g', 'even_sgu_ln_b', 'even_sgu_w', 'even_sgu_b', 'even_w_out', 'odd_w_qkv', 'odd_lambda_q1',
        'odd_lambda_k1', 'odd_lambda_q2', 'odd_lambda_k2', 'odd_subln_w', 'odd_w_out', 'ln_mix_g', 'ln_mix_b',
        'ln_ffn_g', 'ln_ffn_b', 'mlp_w_up', 'mlp_w_down']


def kernel(**inputs):
    import numpy as np
    import concourse.bacc as bacc
    from concourse.bass_utils import run_bass_kernel_spmd

    nc = bacc.Bacc("TRN2", target_bir_lowering=False, num_devices=1)
    arrays, aps = {}, {}
    for name in _INS:
        a = np.ascontiguousarray(inputs[name])
        arrays[f"in_{name}"] = a
        aps[name] = nc.dram_tensor(f"in_{name}", a.shape, mybir.dt.from_np(a.dtype), kind="ExternalInput").ap()
    out = nc.dram_tensor("out", arrays["in_x"].shape, F32, kind="ExternalOutput").ap()
    build(nc, aps, out)
    result = run_bass_kernel_spmd(nc, [arrays], core_ids=[0])
    return result.results[0]["out"]
```
